# Optimizing a Trainium2 kernel written in Bass

```python
import jax
import jax.numpy as jnp
from jax import lax
import numpy as np

D_MODEL = 1024
BATCH = 1
SEQ = 1024
DEPTH = 1

D_MIX = D_MODEL
ATT_HEADS = 8
ATT_KV_HEADS = 2
ATT_HEAD_DIM = D_MIX // 16
ATT_WIDTH = ATT_HEADS * ATT_HEAD_DIM
ATT_KV_WIDTH = ATT_KV_HEADS * ATT_HEAD_DIM
WINDOW = 128
MLSTM_HEADS = 4
MLSTM_WIDTH = D_MIX - ATT_WIDTH
MLSTM_HEAD_DIM = MLSTM_WIDTH // MLSTM_HEADS
MLSTM_CHUNK = 64
QK_CONV_WIDTH = 4
IN_COLS = ATT_WIDTH + 2 * ATT_KV_WIDTH + 4 * MLSTM_WIDTH + 2 * MLSTM_HEADS
X_HEADS = 4
X_HEAD_DIM = D_MODEL // X_HEADS
MEM_LEN = 256
D_FF = 2816
FFN_CONV_WIDTH = 3
RMS_EPS = 1e-6
NEG_BIG = -1e30


def rmsnorm(x, g):
    xf = x.astype(jnp.float32)
    y = xf * lax.rsqrt(jnp.mean(xf * xf, axis=-1, keepdims=True) + RMS_EPS)
    return (y * g.astype(jnp.float32)).astype(x.dtype)

def causal_depthwise_conv(x, w, b):
    K, C = w.shape
    y = lax.conv_general_dilated(
        x, w.astype(x.dtype)[:, None, :], window_strides=(1,),
        padding=[(K - 1, 0)], dimension_numbers=('NWC', 'WIO', 'NWC'),
        feature_group_count=C)
    return y + b.astype(x.dtype)

def alibi_slopes(n_heads):
    return 2.0 ** (-8.0 * jnp.arange(1, n_heads + 1, dtype=jnp.float32) / n_heads)

def sliding_window_attention(q, k, v, sinks, slopes):
    B, S, _, D = q.shape
    W = WINDOW
    nb = S // W
    G = ATT_HEADS // ATT_KV_HEADS
    qb = q.reshape(B, nb, W, ATT_KV_HEADS, G, D)
    kb = k.reshape(B, nb, W, ATT_KV_HEADS, D)
    vb = v.reshape(B, nb, W, ATT_KV_HEADS, D)
    pad = ((0, 0), (1, 0), (0, 0), (0, 0), (0, 0))
    kk = jnp.concatenate([jnp.pad(kb, pad)[:, :-1], kb], axis=2)
    vv = jnp.concatenate([jnp.pad(vb, pad)[:, :-1], vb], axis=2)
    s = jnp.einsum('bnqhgd,bnkhd->bnhgqk', qb, kk,
                   preferred_element_type=jnp.float32) * (D ** -0.5)
    qi = jnp.arange(W)[:, None]
    kj = jnp.arange(2 * W)[None, :]
    dist = qi + W - kj
    in_band = (dist >= 0) & (dist < W)
    valid = in_band[None] & ((jnp.arange(nb)[:, None, None] > 0) | (kj >= W)[None])
    bias = -slopes.reshape(ATT_KV_HEADS, G)[:, :, None, None] * dist.astype(jnp.float32)
    s = jnp.where(valid[None, :, None, None], s + bias[None, None], NEG_BIG)
    sink = sinks.astype(jnp.float32).reshape(ATT_KV_HEADS, G)[None, None, :, :, None, None]
    m = jnp.maximum(jnp.max(s, axis=-1, keepdims=True), sink)
    p = jnp.exp(s - m)
    p = p / (jnp.sum(p, axis=-1, keepdims=True) + jnp.exp(sink - m))
    o = jnp.einsum('bnhgqk,bnkhd->bnqhgd', p.astype(vv.dtype), vv)
    return o.reshape(B, S, ATT_HEADS * D)

def mlstm_chunkwise(q, k, v, i_pre, f_pre):
    B, S, H, D = q.shape
    L = MLSTM_CHUNK
    nc = S // L
    q = q * (D ** -0.5)

    def to_chunks(a):
        return a.reshape(B, nc, L, H, D).transpose(1, 0, 3, 2, 4)

    def gate_chunks(a):
        return a.reshape(B, nc, L, H).transpose(1, 0, 3, 2)

    causal = jnp.tril(jnp.ones((L, L), dtype=bool))

    def step(carry, inp):
        C, n, m = carry
        qc, kc, vc, igc, lfc = inp
        b = jnp.cumsum(lfc, axis=-1)
        dmat = jnp.where(causal, b[..., :, None] - b[..., None, :] + igc[..., None, :], NEG_BIG)
        inter = b + m[..., None]
        m_t = jnp.maximum(inter, jnp.max(dmat, axis=-1))
        w_inter = jnp.exp(inter - m_t)
        sc = jnp.einsum('bhtd,bhsd->bhts', qc, kc) * jnp.exp(dmat - m_t[..., None])
        num = (w_inter[..., None] * jnp.einsum('bhtd,bhde->bhte', qc, C)
               + jnp.einsum('bhts,bhse->bhte', sc, vc))
        den = w_inter * jnp.einsum('bhtd,bhd->bht', qc, n) + jnp.sum(sc, axis=-1)
        h = num / jnp.maximum(jnp.abs(den), jnp.exp(-m_t))[..., None]
        b_end = b[..., -1]
        g = b_end[..., None] - b + igc
        m_new = jnp.maximum(b_end + m, jnp.max(g, axis=-1))
        decay = jnp.exp(b_end + m - m_new)
        ws = jnp.exp(g - m_new[..., None])
        C_new = decay[..., None, None] * C + jnp.einsum('bhs,bhsd,bhse->bhde', ws, kc, vc)
        n_new = decay[..., None] * n + jnp.einsum('bhs,bhsd->bhd', ws, kc)
        return (C_new, n_new, m_new), h

    init = (jnp.zeros((B, H, D, D), jnp.float32),
            jnp.zeros((B, H, D), jnp.float32),
            jnp.zeros((B, H), jnp.float32))
    xs = (to_chunks(q), to_chunks(k), to_chunks(v),
          gate_chunks(i_pre), gate_chunks(jax.nn.log_sigmoid(f_pre)))
    _, h = lax.scan(step, init, xs)
    return h.transpose(1, 0, 3, 2, 4).reshape(B, S, H * D)

def cross_attention(hq, hm, wq, wkv, wo):
    B, S, _ = hq.shape
    M = hm.shape[1]
    q = (hq @ wq).reshape(B, S, X_HEADS, X_HEAD_DIM)
    kv = hm @ wkv
    k = kv[..., :D_MODEL].reshape(B, M, X_HEADS, X_HEAD_DIM)
    v = kv[..., D_MODEL:].reshape(B, M, X_HEADS, X_HEAD_DIM)
    s = jnp.einsum('bshd,bmhd->bhsm', q, k,
                   preferred_element_type=jnp.float32) * (X_HEAD_DIM ** -0.5)
    a = jax.nn.softmax(s, axis=-1).astype(v.dtype)
    o = jnp.einsum('bhsm,bmhd->bshd', a, v).reshape(B, S, X_HEADS * X_HEAD_DIM)
    return o @ wo

def first_inputs(seed: int = 0) -> dict:
    key = jax.random.key(seed)
    ks = jax.random.split(key, 22)
    f32 = jnp.float32

    def nrm(k, shape, scale):
        return jax.random.normal(k, shape, f32) * scale

    def gain(k, shape):
        return 1.0 + 0.02 * jax.random.normal(k, shape, f32)

    L = DEPTH
    f_bias = jnp.linspace(3.0, 6.0, MLSTM_HEADS, dtype=f32)
    return {
        'x': nrm(ks[0], (BATCH, SEQ, D_MODEL), 1.0),
        'mem': nrm(ks[1], (BATCH, MEM_LEN, D_MODEL), 1.0),
        'norm_mix_g': gain(ks[2], (L, D_MODEL)),
        'w_in': nrm(ks[3], (L, D_MODEL, IN_COLS), D_MODEL ** -0.5),
        'b_gate_if': jnp.concatenate(
            [nrm(ks[4], (L, MLSTM_HEADS), 0.1),
             f_bias[None] + nrm(ks[5], (L, MLSTM_HEADS), 0.1)], axis=-1),
        'conv_qk_w': nrm(ks[6], (L, QK_CONV_WIDTH, 2 * MLSTM_WIDTH), QK_CONV_WIDTH ** -0.5),
        'conv_qk_b': nrm(ks[7], (L, 2 * MLSTM_WIDTH), 0.02),
        'attn_sinks': nrm(ks[8], (L, ATT_HEADS), 0.5),
        'w_out': nrm(ks[9], (L, D_MIX, D_MODEL), D_MIX ** -0.5),
        'norm_xattn_g': gain(ks[10], (L, D_MODEL)),
        'norm_mem_g': gain(ks[11], (L, D_MODEL)),
        'wq_x': nrm(ks[12], (L, D_MODEL, X_HEADS * X_HEAD_DIM), D_MODEL ** -0.5),
        'wkv_x': nrm(ks[13], (L, D_MODEL, 2 * X_HEADS * X_HEAD_DIM), D_MODEL ** -0.5),
        'wo_x': nrm(ks[14], (L, X_HEADS * X_HEAD_DIM, D_MODEL), D_MODEL ** -0.5),
        'norm_ffn_g': gain(ks[15], (L, D_MODEL)),
        'w_up': nrm(ks[16], (L, D_MODEL, 2 * D_FF), D_MODEL ** -0.5),
        'conv_ffn_w': nrm(ks[17], (L, FFN_CONV_WIDTH, D_FF), FFN_CONV_WIDTH ** -0.5),
        'conv_ffn_b': nrm(ks[18], (L, D_FF), 0.02),
        'w_down': nrm(ks[19], (L, D_FF, D_MODEL), D_FF ** -0.5),
        'norm_final_g': gain(ks[20], (D_MODEL,)),
    }

def first_block(x, mem, norm_mix_g, w_in, b_gate_if, conv_qk_w, conv_qk_b, attn_sinks,
              w_out, norm_xattn_g, norm_mem_g, wq_x, wkv_x, wo_x, norm_ffn_g, w_up,
              conv_ffn_w, conv_ffn_b, w_down, norm_final_g):
    B, S, _ = x.shape
    H = MLSTM_HEADS
    slopes = alibi_slopes(ATT_HEADS)
    o0 = ATT_WIDTH
    o1 = o0 + ATT_KV_WIDTH
    o2 = o1 + ATT_KV_WIDTH
    o3 = o2 + 2 * MLSTM_WIDTH
    o4 = o3 + MLSTM_WIDTH
    o5 = o4 + MLSTM_WIDTH
    for l in range(DEPTH):
        h = rmsnorm(x, norm_mix_g[l])
        p = h @ w_in[l]
        aq = p[..., :o0].reshape(B, S, ATT_HEADS, ATT_HEAD_DIM)
        ak = p[..., o0:o1].reshape(B, S, ATT_KV_HEADS, ATT_HEAD_DIM)
        av = p[..., o1:o2].reshape(B, S, ATT_KV_HEADS, ATT_HEAD_DIM)
        attn_out = sliding_window_attention(aq, ak, av, attn_sinks[l], slopes)

        mqk = jax.nn.silu(causal_depthwise_conv(p[..., o2:o3], conv_qk_w[l], conv_qk_b[l]))
        mq = mqk[..., :MLSTM_WIDTH].reshape(B, S, H, MLSTM_HEAD_DIM).astype(jnp.float32)
        mk = mqk[..., MLSTM_WIDTH:].reshape(B, S, H, MLSTM_HEAD_DIM).astype(jnp.float32)
        mv = p[..., o3:o4].reshape(B, S, H, MLSTM_HEAD_DIM).astype(jnp.float32)
        mo = p[..., o4:o5].astype(jnp.float32)
        gif = p[..., o5:].astype(jnp.float32) + b_gate_if[l].astype(jnp.float32)
        m_h = mlstm_chunkwise(mq, mk, mv, gif[..., :H], gif[..., H:])
        mlstm_out = (jax.nn.sigmoid(mo) * m_h).astype(x.dtype)

        x = x + jnp.concatenate([attn_out, mlstm_out], axis=-1) @ w_out[l]

        x = x + cross_attention(rmsnorm(x, norm_xattn_g[l]), rmsnorm(mem, norm_mem_g[l]),
                                wq_x[l], wkv_x[l], wo_x[l])

        hf = rmsnorm(x, norm_ffn_g[l])
        u = hf @ w_up[l]
        g = causal_depthwise_conv(u[..., :D_FF], conv_ffn_w[l], conv_ffn_b[l])
        x = x + (jax.nn.silu(g) * u[..., D_FF:]) @ w_down[l]
    return rmsnorm(x, norm_final_g)


CHUNK = 64
HEAD_DIM = 64
D_RWKV = 512
D_ATT = 512
D_MIX_2 = D_RWKV + D_ATT
N_RWKV_HEADS = D_RWKV // HEAD_DIM
N_ATT_HEADS = D_ATT // HEAD_DIM
LORA_W = 64
LORA_A = 64
N_LEFT_CHUNKS = 8
BAND = (N_LEFT_CHUNKS + 1) * CHUNK
REL_CLIP = 128
N_REL = CHUNK + REL_CLIP
GN_EPS = 64e-5
D_SHIFT = 4 * D_RWKV + LORA_W + LORA_A
D_IN = D_SHIFT + 4 * D_ATT


def rms_norm(x, g):
    x32 = x.astype(jnp.float32)
    y = x32 * lax.rsqrt(jnp.mean(x32 * x32, axis=-1, keepdims=True) + RMS_EPS)
    return y.astype(x.dtype) * g

def token_shift(p, mu):
    prev = jnp.pad(p, ((0, 0), (1, 0), (0, 0)))[:, :-1]
    return p + mu * (prev - p)

def rwkv7_step(state, inp):
    r_t, w_t, k_t, v_t, a_t, b_t = inp
    sa = jnp.einsum('bhij,bhj->bhi', state, a_t)
    state = state * w_t[:, :, None, :] + sa[..., None] * b_t[:, :, None, :] + v_t[..., None] * k_t[:, :, None, :]
    y = jnp.einsum('bhij,bhj->bhi', state, r_t)
    return state, y

def rwkv7_mix(ps, w0, w2, a0, a2, k_k, k_a, r_k, lnx_g, lnx_b):
    b_, s_, _ = ps.shape
    f32 = jnp.float32
    r, k, v, g, wd, ad = jnp.split(ps, [D_RWKV, 2 * D_RWKV, 3 * D_RWKV, 4 * D_RWKV, 4 * D_RWKV + LORA_W], axis=-1)
    w_log = -jax.nn.softplus(-(w0 + jnp.tanh(wd) @ w2).astype(f32)) - 0.5
    decay = jnp.exp(-jnp.exp(w_log))
    a = jax.nn.sigmoid((a0 + ad @ a2).astype(f32))
    heads = lambda t: t.astype(f32).reshape(b_, s_, N_RWKV_HEADS, HEAD_DIM)
    r, k, v, decay, a = heads(r), heads(k), heads(v), heads(decay), heads(a)
    kk = k * k_k.astype(f32).reshape(N_RWKV_HEADS, HEAD_DIM)
    kk = kk / jnp.maximum(jnp.sqrt(jnp.sum(kk * kk, axis=-1, keepdims=True)), 1e-12)
    k = k * (1.0 + (a - 1.0) * k_a.astype(f32).reshape(N_RWKV_HEADS, HEAD_DIM))
    seq_first = lambda t: jnp.moveaxis(t, 1, 0)
    state0 = jnp.zeros((b_, N_RWKV_HEADS, HEAD_DIM, HEAD_DIM), f32)
    _, y = lax.scan(rwkv7_step, state0, (seq_first(r), seq_first(decay), seq_first(k), seq_first(v), seq_first(-kk), seq_first(kk * a)))
    y = jnp.moveaxis(y, 0, 1)
    mean = jnp.mean(y, axis=-1, keepdims=True)
    yc = y - mean
    y = yc * lax.rsqrt(jnp.mean(yc * yc, axis=-1, keepdims=True) + GN_EPS)
    y = y.reshape(b_, s_, D_RWKV) * lnx_g.astype(f32) + lnx_b.astype(f32)
    bonus = jnp.sum(r * k * r_k.astype(f32), axis=-1, keepdims=True) * v
    y = y + bonus.reshape(b_, s_, D_RWKV)
    return y.astype(ps.dtype), g

def chunk_band_attention(q, k, v, q_g, k_g, rel_bias):
    b_, s_, _ = q.shape
    nc = s_ // CHUNK
    pad = N_LEFT_CHUNKS * CHUNK
    def heads(t):
        return t.reshape(b_, s_, N_ATT_HEADS, HEAD_DIM).transpose(0, 2, 1, 3)
    q = heads(rms_norm(q.reshape(b_, s_, N_ATT_HEADS, HEAD_DIM), q_g).reshape(b_, s_, D_ATT))
    k = heads(rms_norm(k.reshape(b_, s_, N_ATT_HEADS, HEAD_DIM), k_g).reshape(b_, s_, D_ATT))
    v = heads(v)
    qc = q.reshape(b_, N_ATT_HEADS, nc, CHUNK, HEAD_DIM)
    def band(t):
        tp = jnp.pad(t, ((0, 0), (0, 0), (pad, 0), (0, 0))).reshape(b_, N_ATT_HEADS, nc + N_LEFT_CHUNKS, CHUNK, HEAD_DIM)
        return jnp.concatenate([tp[:, :, i:i + nc] for i in range(N_LEFT_CHUNKS + 1)], axis=3)
    kb, vb = band(k), band(v)
    s = jnp.einsum('bhnqd,bhnkd->bhnqk', qc, kb).astype(jnp.float32) * (HEAD_DIM ** -0.5)
    dist = jnp.arange(CHUNK)[:, None] + pad - jnp.arange(BAND)[None, :]
    rel_idx = jnp.clip(dist, -(CHUNK - 1), REL_CLIP) + (CHUNK - 1)
    bias = rel_bias[:, rel_idx].astype(jnp.float32)
    valid = (jnp.arange(nc)[:, None] * CHUNK + jnp.arange(BAND)[None, :] - pad) >= 0
    s = s + bias[None, :, None]
    s = jnp.where(valid[None, None, :, None, :], s, -1e30)
    p = jax.nn.softmax(s, axis=-1).astype(v.dtype)
    o = jnp.einsum('bhnqk,bhnkd->bhnqd', p, vb)
    return o.reshape(b_, N_ATT_HEADS, s_, HEAD_DIM).transpose(0, 2, 1, 3).reshape(b_, s_, D_ATT)

def second_inputs(seed: int = 0) -> dict:
    key = jax.random.key(seed)
    ks = jax.random.split(key, 22)
    n = lambda i, shape: jax.random.normal(ks[i], shape, jnp.float32)
    L = DEPTH
    return {
        'x': n(0, (BATCH, SEQ, D_MODEL)),
        'c': n(1, (BATCH, D_MODEL)),
        'norm_g': 1.0 + 0.1 * n(2, (L, D_MODEL)),
        'w_ada': n(3, (L, D_MODEL, 3 * D_MODEL)) * (0.5 * D_MODEL ** -0.5),
        'b_ada': 0.02 * n(4, (L, 3 * D_MODEL)),
        'w_in': n(5, (L, D_MODEL, D_IN)) * (D_MODEL ** -0.5),
        'mu_shift': jax.random.uniform(ks[6], (L, D_SHIFT), jnp.float32),
        'w0': -1.0 + 0.5 * n(7, (L, D_RWKV)),
        'w2': n(8, (L, LORA_W, D_RWKV)) * (0.5 * LORA_W ** -0.5),
        'a0': 0.5 * n(9, (L, D_RWKV)),
        'a2': n(10, (L, LORA_A, D_RWKV)) * (0.5 * LORA_A ** -0.5),
        'k_k': 0.85 + 0.05 * n(11, (L, D_RWKV)),
        'k_a': 1.0 + 0.05 * n(12, (L, D_RWKV)),
        'r_k': 0.1 * n(13, (L, N_RWKV_HEADS, HEAD_DIM)),
        'lnx_g': 1.0 + 0.1 * n(14, (L, D_RWKV)),
        'lnx_b': 0.02 * n(15, (L, D_RWKV)),
        'q_norm_g': 1.0 + 0.1 * n(16, (L, HEAD_DIM)),
        'k_norm_g': 1.0 + 0.1 * n(17, (L, HEAD_DIM)),
        'rel_bias': 0.5 * n(18, (L, N_ATT_HEADS, N_REL)),
        'w_out': n(19, (L, D_MIX_2, D_MODEL)) * (D_MIX_2 ** -0.5),
    }

def second_block(x, c, norm_g, w_ada, b_ada, w_in, mu_shift, w0, w2, a0, a2, k_k, k_a, r_k, lnx_g, lnx_b, q_norm_g, k_norm_g, rel_bias, w_out):
    c_act = jax.nn.silu(c)
    for l in range(DEPTH):
        mod = c_act @ w_ada[l] + b_ada[l]
        shift, scale, gate = jnp.split(mod, 3, axis=-1)
        h = rms_norm(x, norm_g[l]) * (1.0 + scale[:, None, :]) + shift[:, None, :]
        proj = h @ w_in[l]
        ps = token_shift(proj[..., :D_SHIFT], mu_shift[l])
        pa = proj[..., D_SHIFT:]
        y_r, g_r = rwkv7_mix(ps, w0[l], w2[l], a0[l], a2[l], k_k[l], k_a[l], r_k[l], lnx_g[l], lnx_b[l])
        q, ka, va, g_a = jnp.split(pa, 4, axis=-1)
        y_a = chunk_band_attention(q, ka, va, q_norm_g[l], k_norm_g[l], rel_bias[l])
        y = jnp.concatenate([y_r * jax.nn.silu(g_r), y_a * jax.nn.silu(g_a)], axis=-1)
        x = x + gate[:, None, :] * (y @ w_out[l])
    return x


def setup_inputs(seed=0):
    out = dict(first_inputs(seed))
    for name, value in second_inputs(seed + 1).items():
        if name != "x":
            out[name + "_2"] = value
    return out


def reference(
    x, mem, norm_mix_g, w_in, b_gate_if, conv_qk_w, conv_qk_b, attn_sinks, w_out, norm_xattn_g,
    norm_mem_g, wq_x, wkv_x, wo_x, norm_ffn_g, w_up, conv_ffn_w, conv_ffn_b, w_down,
    norm_final_g, c_2, norm_g_2, w_ada_2, b_ada_2, w_in_2, mu_shift_2, w0_2, w2_2, a0_2, a2_2,
    k_k_2, k_a_2, r_k_2, lnx_g_2, lnx_b_2, q_norm_g_2, k_norm_g_2, rel_bias_2, w_out_2,
):
    x = first_block(
        x, mem, norm_mix_g, w_in, b_gate_if, conv_qk_w, conv_qk_b, attn_sinks, w_out,
        norm_xattn_g, norm_mem_g, wq_x, wkv_x, wo_x, norm_ffn_g, w_up, conv_ffn_w, conv_ffn_b,
        w_down, norm_final_g,
    )
    return second_block(
        x, c_2, norm_g_2, w_ada_2, b_ada_2, w_in_2, mu_shift_2, w0_2, w2_2, a0_2, a2_2, k_k_2,
        k_a_2, r_k_2, lnx_g_2, lnx_b_2, q_norm_g_2, k_norm_g_2, rel_bias_2, w_out_2,
    )


_drawn_inputs = setup_inputs


def setup_inputs(seed=0):
    import zlib

    import numpy as np

    out = dict(_drawn_inputs(seed))
    spreads = {}
    factors = {'norm_mix_g': 6.933,
     'conv_qk_b': 41.621,
     'attn_sinks': 38.528,
     'norm_xattn_g': 8.0,
     'norm_mem_g': 8.0,
     'norm_ffn_g': 3.826,
     'conv_ffn_b': 5.488,
     'norm_final_g': 2.873,
     'b_ada_2': 4.604,
     'w2_2': 5.276,
     'k_k_2': 200.0,
     'k_a_2': 17.404,
     'lnx_g_2': 12.647,
     'lnx_b_2': 64.0,
     'q_norm_g_2': 22.724,
     'k_norm_g_2': 22.964,
     'rel_bias_2': 30.922}
    for name, (base, spread) in spreads.items():
        noise = np.random.default_rng([zlib.crc32(name.encode()), seed]).standard_normal(out[name].shape)
        drawn = base * np.exp(spread * noise) if base else spread * noise
        out[name] = jnp.asarray(drawn.astype(out[name].dtype))
    for name, factor in factors.items():
        out[name] = (out[name] * factor).astype(out[name].dtype)
    return out
```

```python
import concourse.bass as bass
from concourse import mybir
from contextlib import ExitStack

F32 = mybir.dt.float32
ALU = mybir.AluOpType
ACT = mybir.ActivationFunctionType
AX = mybir.AxisListType
MUL, ADD, SUB, MAX, MIN = ALU.mult, ALU.add, ALU.subtract, ALU.max, ALU.min
EH = 0.6065306597126334
NSLOT = 4
NSEM = 64

COLS = {}
ROWS = {}
CST = {}


def _lay(table, names):
    at = 0
    for n, w in names:
        table[n] = (at, w)
        at += w
    return at


NCOLS = _lay(COLS, [("g_mix", 8), ("g_x", 8), ("g_mem", 8), ("g_ffn", 8), ("g_fin", 8), ("g_n2", 8), ("c", 8),
                    ("b_ada", 24), ("convw", 32), ("convb", 8), ("fw", 66), ("fb", 22), ("mu", 17), ("w0", 4),
                    ("a0", 4), ("kk", 4), ("ka", 4), ("rk", 4), ("qng", 1), ("kng", 1)])
NROWS = _lay(ROWS, [("bg", 8), ("sinks", 8), ("lng", 512), ("lnb", 512)])
NCST = _lay(CST, [("I", 128), ("ones", 128), ("bo", 2), ("mst", 128), ("selh", 512), ("selp", 512)])
NM2 = 128 * 10


class Queue:

    def __init__(self, sem, eng):
        self.sem, self.n, self.eng, self.seen = sem, 0, eng, {}

    def issue(self, fn, sem, by, waits):
        if self.eng is None:
            return
        for s, v in flat(waits):
            if self.seen.get(id(s), 0) < v:
                self.seen[id(s)] = v
                self.eng.wait_ge(s, v)
        ins = fn(self.eng)
        if sem is not None:
            ins.then_inc(sem, by)

    def __call__(self, fn, *waits, inc=True):
        self.issue(fn, self.sem if inc else None, 1, waits)
        if inc:
            self.n += 1
        return (self.sem, self.n)

    def dma(self, fn, sem, value, *waits):
        self.issue(fn, sem, 16, waits)
        return (sem, value)


def flat(x):
    if x is None:
        return []
    if isinstance(x, tuple) and len(x) == 2 and isinstance(x[1], int):
        return [x]
    return [t for y in x for t in flat(y)]


class Places:

    def __init__(self, items):
        self.free = [(i, []) for i in items]

    def take(self):
        return self.free.pop(0)

    def give(self, item, *toks):
        self.free.append((item, flat(toks)))


def staggered(units, depth):
    units, live = list(units), []
    while units or live:
        if units and len(live) < depth:
            live.append(units.pop(0))
        for u in list(live):
            try:
                next(u)
            except StopIteration:
                live.remove(u)
        yield


def run(gen):
    for _ in gen:
        pass


def build(nc, d):
    with ExitStack() as ctx:
        SB = ctx.enter_context(nc.sbuf_tensor("SB", [128, 52700], F32))
        PS = ctx.enter_context(nc.psum_tensor("PS", [128, 4096], F32))
        sems = [ctx.enter_context(nc.semaphore(f"s{i}")) for i in range(NSEM)]
        spill = nc.dram_tensor("spill", (1024, 1024), F32, kind="Internal").ap()
        block = ctx.enter_context(nc.Block())

        @block.tensor
        def _(eng):
            walk(SB, PS, sems, spill, d, 0, eng)

        @block.vector
        def _(eng):
            walk(SB, PS, sems, spill, d, 1, eng)

        @block.scalar
        def _(eng):
            walk(SB, PS, sems, spill, d, 2, eng)

        @block.gpsimd
        def _(eng):
            walk(SB, PS, sems, spill, d, 3, eng)

        @block.sync
        def _(eng):
            walk(SB, PS, sems, spill, d, 4, eng)


def walk(SB, PS, sems, spill, d, me, engine):
    nsem = [0]

    def sem():
        nsem[0] += 1
        return sems[nsem[0] - 1]

    pe, dve, act, pool, sp = (Queue(sem(), engine if i == me else None) for i in range(5))
    at = [0]

    def region(n):
        a = at[0]
        at[0] += n
        assert at[0] <= 52700
        return SB[:, a:a + n]

    def v3(ap, k):
        return ap.rearrange("p (k n) -> p k n", k=k)

    def once(q, out, in_, *waits):
        return q.dma(lambda e: e.dma_start(out, in_), sem(), 16, *waits)

    cols, rows, cst = region(NCOLS), region(NROWS), region(NCST)
    t_cst = once(act, cst, d["cst"])
    t_col = once(act, cols, d["cols"])
    t_row = once(act, rows, d["rows"])

    def col(name, i=0):
        return cols[:, COLS[name][0] + i:COLS[name][0] + i + 1]

    def row(name, a=0, b=None):
        o, w = ROWS[name]
        return rows[:, o + a:o + (w if b is None else b)]

    def cs(name, a=0, b=None):
        o, w = CST[name]
        return cst[:, o + a:o + (w if b is None else b)]

    I = cs("I")
    mod = region(24)
    gs2 = region(8)
    small = region(704)
    at[0] += -at[0] % 4
    XTr = region(8192)
    RING = region(NSLOT * 2048)
    Hr = region(8192)
    W0 = at[0]
    WN = 52700 - W0
    XT, H = v3(XTr, 8), v3(Hr, 8)

    def work(a, n):
        assert a + n <= WN, (a, n, WN)
        return SB[:, W0 + a:W0 + a + n]

    banks2 = Places([0, 1, 2])
    banks1 = Places([6, 7])

    def pair(b):
        return PS[:, 1024 * b:1024 * b + 1024]

    def bank(b):
        return PS[:, 512 * b:512 * b + 512]

    slots = Places(list(range(NSLOT)))
    slot_sem = [sem() for _ in range(NSLOT)]
    slot_n = [0] * NSLOT

    def slot(i):
        return RING[:, 2048 * i:2048 * i + 2048]

    def slab(w, k0, kn, c0, cn, *waits):
        i, free = slots.take()
        slot_n[i] += 16
        view = slot(i)[:, 0:kn * cn].rearrange("p (k n) -> p k n", k=kn)
        src = w[k0 * 128:(k0 + kn) * 128, c0:c0 + cn].rearrange("(k p) n -> p k n", p=128)
        t = sp.dma(lambda e: e.dma_start(view, src), slot_sem[i], slot_n[i], free, *waits)
        return i, view, t

    def gemmT(w, c0, ntile, src, stok, evac, N=1024):
        K = len(src)
        nk = (K + 7) // 8
        for m0 in range(0, ntile, 2):
            mn = min(2, ntile - m0)
            sl = [slab(w, 8 * a, min(8, K - 8 * a), c0 + m0 * 128, mn * 128) for a in range(nk)]
            for m in range(mn):
                b, free = banks2.take()
                for n0 in range(0, N, 512):
                    nn = min(512, N - n0)
                    for k in range(K):
                        _, view, t = sl[k // 8]
                        out = pair(b)[:, n0:n0 + nn]
                        lhs = view[:, k % 8, m * 128:(m + 1) * 128]
                        rhs = src[k][:, n0:n0 + nn]
                        last = k == K - 1
                        tk = pe(lambda e, out=out, lhs=lhs, rhs=rhs, k=k, last=last:
                                e.matmul(out, lhs, rhs, start=(k == 0), stop=last),
                                t, stok[k], free, inc=last)
                if m == mn - 1:
                    for i, _, _ in sl:
                        slots.give(i, tk)
                banks2.give(b, evac(m0 + m, pair(b)[:, 0:N], tk))
                yield

    def gemmN(w, c0, cn, src, stok, evac, T=8):
        i, view, t = slab(w, 0, 8, c0, cn)
        for tt in range(T):
            b, free = banks1.take()
            out = bank(b)[:, 0:cn]
            for k in range(8):
                lhs = src[k][:, tt * 128:(tt + 1) * 128]
                tk = pe(lambda e, out=out, lhs=lhs, k=k:
                        e.matmul(out, lhs, view[:, k, 0:cn], start=(k == 0), stop=(k == 7)),
                        t, stok[k], free, inc=(k == 7))
            if tt == T - 1:
                slots.give(i, tk)
            banks1.give(b, evac(tt, out, tk))
            yield

    def transpose(out, in_, *waits, inc=True):
        p = in_.shape[0]
        idn = I[0:p, 0:p]
        return pe(lambda e: e.transpose(out, in_, idn), *waits, inc=inc)

    def rms(src, stok, T, gcol, dst, dfree, scale1=None, bias=None):
        nt = T // 128
        sq = [act(lambda e, k=k: e.activation(dst[:, k, :], src[:, k, :], ACT.Square), stok[k], dfree)
              for k in range(8)]
        b, free = banks1.take()
        for tt in range(nt):
            for k in range(8):
                tk = pe(lambda e, tt=tt, k=k: e.matmul(bank(b)[:, tt:tt + 1],
                        dst[:, k, tt * 128:(tt + 1) * 128], cs("ones", 0, 1), start=(k == 0), stop=(k == 7)),
                        sq[k], free, t_cst, inc=(k == 7))
        st = small[:, 0:nt]
        t = dve(lambda e: e.tensor_scalar(st, bank(b)[:, 0:nt], 1.0 / 1024, 1e-6, MUL, ADD), tk)
        banks1.give(b, t)
        t = act(lambda e: e.activation(st, st, ACT.Sqrt), t)
        t = dve(lambda e: e.reciprocal(st, st), t)
        i, sfree = slots.take()
        dg = slot(i)[:, 0:T]
        for tt in range(nt):
            t1 = dve(lambda e, tt=tt: e.tensor_scalar(dg[:, tt * 128:(tt + 1) * 128], I, st[:, tt:tt + 1], None,
                                                     MUL), t, sfree)
        p, free = banks2.take()
        for n0 in range(0, T, 512):
            nn = min(512, T - n0)
            tb = pe(lambda e, n0=n0, nn=nn: e.matmul(pair(p)[:, n0:n0 + nn], cs("ones"), dg[:, n0:n0 + nn],
                                                    start=True, stop=True), t1, free)
        slots.give(i, tb)
        out = []
        for k in range(8):
            t = dve(lambda e, k=k: e.scalar_tensor_tensor(out=dst[:, k, :], in0=src[:, k, :], scalar=gcol(k),
                                                          in1=pair(p)[:, 0:T], op0=MUL, op1=MUL),
                    tb, tk, t_col, scale1)
            last = t
            if bias is not None:
                t = act(lambda e, k=k: e.activation(dst[:, k, :], dst[:, k, :], ACT.Identity, bias=bias(k)),
                        t, scale1)
            out.append(t)
        banks2.give(p, last)
        return out

    def tiles(v):
        return [v[:, k, :] for k in range(v.shape[1])]

    def add_x(src_toks, new):
        def evac(m, ps, tk):
            new[m] = dve(lambda e: e.tensor_tensor(XT[:, m, :], ps, XT[:, m, :], ADD), tk, src_toks[m])
            return new[m]
        return evac

    finals = []
    prior = []

    def ada():
        cact = small[:, 16:24]
        tc = act(lambda e: e.activation(cact, cols[:, COLS["c"][0]:COLS["c"][0] + 8], ACT.Silu), t_col)
        b, free = banks1.take()
        for m0 in range(0, 24, 2):
            i, view, t = slab(d["w_ada"], 0, 8, m0 * 128, 256)
            for m in range(2):
                for k in range(8):
                    tk = pe(lambda e, m=m, k=k, view=view, m0=m0: e.matmul(
                        bank(b)[:, m0 + m:m0 + m + 1], view[:, k, m * 128:(m + 1) * 128],
                        cact[:, k:k + 1], start=(k == 0), stop=(k == 7)),
                        t, tc, free, inc=(k == 7))
            slots.give(i, tk)
        ba = cols[:, COLS["b_ada"][0]:COLS["b_ada"][0] + 24]
        t = dve(lambda e: e.tensor_tensor(mod, bank(b)[:, 0:24], ba, ADD), tk, t_col)
        banks1.give(b, t)
        g2 = cols[:, COLS["g_n2"][0]:COLS["g_n2"][0] + 8]
        t2 = dve(lambda e: e.tensor_scalar(gs2, mod[:, 8:16], 1.0, None, ADD), t)
        t2 = dve(lambda e: e.tensor_tensor(gs2, gs2, g2, MUL), t2)
        return [t, t2]

    def softmax(S, tS, P, W, G, scale, bias, sinks, st, pfree, extra=None):
        mx, nm, sm, es = (st[:, k * G:(k + 1) * G] for k in range(4))
        if bias is not None:
            t = dve(lambda e: e.scalar_tensor_tensor(out=P, in0=S, scalar=scale, in1=bias, op0=MUL, op1=ADD),
                    tS, pfree, extra)
            tr = t
            src, sc, neg = P, 1.0, -1.0
        else:
            src, sc, neg, t, tr = S, scale, -scale, tS, None
        t = dve(lambda e: e.tensor_reduce(mx, src, AX.X, MAX), t, pfree)
        if sinks is not None:
            t = dve(lambda e: e.tensor_tensor(mx, mx, sinks, MAX), t, t_row)
        t = dve(lambda e: e.tensor_scalar(nm, mx, neg, None, MUL), t)
        if sinks is not None:
            te = dve(lambda e: e.tensor_tensor(es, nm, sinks, ADD), t)
            te = act(lambda e: e.activation(es, es, ACT.Exp), te)
        for g in range(G):
            tx = act(lambda e, g=g: e.activation(P[:, g, :], src[:, g, :], ACT.Exp, bias=nm[:, g:g + 1], scale=sc,
                                                 accum_out=sm[:, g:g + 1]), t)
        ts = tx
        if sinks is not None:
            tx = dve(lambda e: e.tensor_tensor(sm, sm, es, ADD), tx, te)
        tx = dve(lambda e: e.reciprocal(sm, sm), tx)
        for g in range(G):
            tp = dve(lambda e, g=g: e.tensor_scalar(P[:, g, :], P[:, g, :], sm[:, g:g + 1], None, MUL), tx)
        return tp, (tr if bias is not None else ts)

    tX = [once(sp, XT[:, k, :], d["xT"][k * 128:(k + 1) * 128, :]) for k in range(8)]
    t_mod = ada()
    tH = rms(XT, tX, 1024, lambda k: col("g_mix", k), H, None)
    Hs = tiles(H)

    aqT, akT = v3(work(0, 4096), 4), work(4096, 1024)
    avt = v3(work(5120, 1024), 8)
    mqk = v3(work(6144, 8192), 8)
    mva = work(14336, 4128).rearrange("p (t h e) -> p t h e", t=8, h=4)
    mo = v3(work(18464, 4096), 4)
    pads = [work(22560, 1028), work(23588, 1028)]
    gt = v3(small[:, 32:96], 8)
    pad_free = [[], []]
    T = {}

    t_ones = pool(lambda e: e.memset(mva[:, :, :, 128:129], 1.0))

    def ev_gate(tt, ps, tk):
        T["gt", tt] = dve(lambda e: e.tensor_tensor(gt[:, tt, :], ps, row("bg"), ADD), tk, t_row)
        return T["gt", tt]

    def ev_av(tt, ps, tk):
        T["av", tt] = act(lambda e: e.activation(avt[:, tt, :], ps, ACT.Copy), tk)
        return T["av", tt]

    def ev_mv(c):
        def f(tt, ps, tk):
            o = mva[:, tt, 2 * c:2 * c + 2, 0:128]
            T["mv", tt, c] = act(lambda e: e.activation(o, ps.rearrange("p (h e) -> p h e", h=2), ACT.Copy), tk)
            return T["mv", tt, c]
        return f

    def ev_q(m, ps, tk):
        T["aq", m] = act(lambda e: e.activation(aqT[:, m, :], ps, ACT.Copy), tk)
        return T["aq", m]

    def ev_k(m, ps, tk):
        T["ak"] = act(lambda e: e.activation(akT, ps, ACT.Copy), tk)
        return T["ak"]

    def ev_mo(m, ps, tk):
        T["mo", m] = act(lambda e: e.activation(mo[:, m, :], ps, ACT.Sigmoid), tk)
        return T["mo", m]

    def conv(pad, taps, w, b, dst, K, t, dfree=None):
        t = dve(lambda e: e.tensor_scalar(dst, pad[:, 0:1024], w(0), b, MUL, ADD), t, t_col, dfree)
        for j in range(1, K):
            t = dve(lambda e, j=j: e.scalar_tensor_tensor(out=dst, in0=pad[:, j:j + 1024], scalar=w(j), in1=dst,
                                                          op0=MUL, op1=ADD), t)
        return t

    tz = [dve(lambda e, i=i: e.memset(pads[i][:, 0:3], 0.0)) for i in range(2)]

    def ev_mqk(m, ps, tk):
        i = m % 2
        pad = pads[i]
        te = act(lambda e: e.activation(pad[:, 3:1027], ps, ACT.Copy), tk, pad_free[i])
        t = conv(pad, 4, lambda j: col("convw", m * 4 + j), col("convb", m), mqk[:, m, :], 4, [te, tz[i]])
        pad_free[i] = t
        T["mqk", m] = act(lambda e: e.activation(mqk[:, m, :], mqk[:, m, :], ACT.Silu), t)
        return te

    w_in = d["w_in"]
    run(gemmN(d["w_in"], 2816, 8, Hs, tH, ev_gate))
    run(gemmT(w_in, 768, 8, Hs, tH, ev_mqk))
    run(gemmN(w_in, 640, 128, Hs, tH, ev_av))
    for c in range(2):
        run(gemmN(w_in, 1792 + 256 * c, 256, Hs, tH, ev_mv(c)))
    run(gemmT(w_in, 2304, 4, Hs, tH, ev_mo))
    run(gemmT(w_in, 0, 4, Hs, tH, ev_q))
    run(gemmT(w_in, 512, 1, Hs, tH, ev_k))
    h_free = (pe.sem, pe.n)

    ids, sfree = zip(*[slots.take() for _ in range(4)])
    rowreg = [slot(ids[0])[:, 0:1024], slot(ids[0])[:, 1024:2048], slot(ids[1])[:, 0:1024],
              slot(ids[1])[:, 1024:2048], pads[0][:, 0:1024], pads[1][:, 0:1024]]
    rowfree = [sfree[0], sfree[0], sfree[1], sfree[1], pad_free[0], pad_free[1]]
    Pb = Places([0, 1])
    PTb = Places([0, 1])
    Pv = [slot(ids[2])[:, 0:1024], slot(ids[2])[:, 1024:2048]]
    PTv = [slot(ids[3])[:, 0:1024], slot(ids[3])[:, 1024:2048]]
    Pb.free = [(0, sfree[2]), (1, sfree[2])]
    PTb.free = [(0, sfree[3]), (1, sfree[3])]
    alibi = small
    alib = Hr[:, 0:2048]
    t_alib = once(sp, alib, d["alibi"], h_free)
    mixA = v3(work(0, 4096), 4)
    mixM = v3(Hr[:, 4096:8192], 4)
    mix_tok = {}

    stn = [0]

    def stat():
        stn[0] = (stn[0] + 1) % 4
        return small[:, 128 + 32 * stn[0]:160 + 32 * stn[0]]

    def window(n, jp):
        W = 128 if n == 0 else 256
        k0 = 0 if n == 0 else (n - 1) * 128
        nk = W // 128
        b, free = banks2.take()
        S = pair(b).rearrange("p (g w) -> p g w", g=4)
        for a in range(2):
            for jj in range(2):
                j = 2 * jp + jj
                tS = pe(lambda e, a=a, jj=jj, j=j: e.matmul(
                    S[:, 2 * a + jj, 0:W], aqT[64 * a:64 * a + 64, j, n * 128:(n + 1) * 128],
                    akT[64 * a:64 * a + 64, k0:k0 + W], start=True, stop=True),
                    T["aq", j], T["ak"], free, inc=(a == 1 and jj == 1))
        p, pfree = Pb.take()
        P = Pv[p].rearrange("p (g w) -> p g w", g=4)
        bias = alib[:, 1024 * jp:1024 * jp + 1024].rearrange("p (g w) -> p g w", g=4)[:, :, 256 - W:256]
        tP, tr = softmax(S[:, :, 0:W], tS, P[:, :, 0:W], W, 4, 0.125, bias, row("sinks", 4 * jp, 4 * jp + 4),
                         stat(), pfree, t_alib)
        banks2.give(b, tr)
        yield
        b, free = banks2.take()
        for g in range(4):
            for kt in range(nk):
                tt = transpose(pair(b)[:, (g * nk + kt) * 128:(g * nk + kt + 1) * 128],
                               P[:, g, kt * 128:(kt + 1) * 128], tP, free, t_cst,
                               inc=(g == 3 and kt == nk - 1))
        Pb.give(p, tt)
        q, qfree = PTb.take()
        PT = PTv[q]
        hw = 256 * nk
        if nk == 1:
            t1 = t2 = act(lambda e: e.activation(PT[:, 0:512], pair(b)[:, 0:512], ACT.Copy), tt, qfree)
        else:
            t1 = act(lambda e: e.activation(PT[:, 0:hw], pair(b)[:, 0:hw], ACT.Copy), tt, qfree)
            t2 = dve(lambda e: e.tensor_copy(PT[:, hw:2 * hw], pair(b)[:, hw:2 * hw]), tt, qfree)
        banks2.give(b, t1, t2)
        yield
        b, free = banks1.take()
        for a in range(2):
            for jj in range(2):
                for kt in range(nk):
                    g = 2 * a + jj
                    tile = k0 // 128 + kt
                    to = pe(lambda e, a=a, jj=jj, kt=kt, g=g, tile=tile: e.matmul(
                        bank(b)[64 * a:64 * a + 64, jj * 128:(jj + 1) * 128],
                        avt[:, tile, 64 * a:64 * a + 64],
                        PT[:, (g * nk + kt) * 128:(g * nk + kt + 1) * 128],
                        start=(kt == 0), stop=(kt == nk - 1)),
                        t1, t2, T["av", tile], free, inc=(g == 3 and kt == nk - 1))
        PTb.give(q, to)
        o = aqT[:, 2 * jp:2 * jp + 2, n * 128:(n + 1) * 128]
        t = act(lambda e: e.activation(o, bank(b)[:, 0:256].rearrange("p (j q) -> p j q", j=2), ACT.Copy), to)
        banks1.give(b, t)
        mix_tok["a", n, jp] = t

    run(staggered([window(n, jp) for jp in range(2) for n in range(8)], 3))

    R = [r[0:4, :] for r in rowreg]
    iR, fR, bR, mR, c1, wi = R
    tg = []
    for q, dst in ((0, iR), (1, fR)):
        b, free = banks2.take()
        for tt in range(8):
            t = transpose(pair(b)[0:4, tt * 128:(tt + 1) * 128], gt[:, tt, 4 * q:4 * q + 4], T["gt", tt], free,
                          t_cst, inc=(tt == 7))
        t = dve(lambda e, dst=dst, b=b: e.tensor_copy(dst, pair(b)[0:4, :]), t, rowfree)
        banks2.give(b, t)
        tg.append(t)
    em = wi
    t = act(lambda e: e.activation(c1, fR, ACT.Abs), tg)
    t = act(lambda e: e.activation(c1, c1, ACT.Exp, scale=-1.0), t)
    t = act(lambda e: e.activation(c1, c1, ACT.Ln, bias=1.0), t)
    t = dve(lambda e: e.scalar_tensor_tensor(out=fR, in0=fR, scalar=0.0, in1=c1, op0=MIN, op1=SUB), t)
    t_rs = once(sp, wi, d["reset128"], rowfree)
    tb = dve(lambda e: e.tensor_tensor_scan(bR, wi, fR, 0.0, MUL, ADD), t, t_rs)
    tm = dve(lambda e: e.tensor_tensor_scan(mR, fR, iR, 0.0, ADD, MAX), tb)
    M9 = small[0:4, 256:265]
    c8 = lambda v: v.rearrange("p (c t) -> p c t", c=8)
    t0 = dve(lambda e: e.memset(M9[:, 0:1], 0.0))
    t1 = dve(lambda e: e.tensor_copy(M9[:, 1:9], c8(mR)[:, :, 127]), tm, t0)
    tc1 = dve(lambda e: e.tensor_tensor(c1, iR, bR, SUB), tb, tm)
    tR1 = dve(lambda e: e.tensor_tensor(bR, bR, mR, SUB), tc1)
    R1 = bR
    t_em = act(lambda e: e.activation(fR, mR, ACT.Exp, scale=-1.0), tm)
    twi = dve(lambda e: e.tensor_tensor(c8(wi), c8(R1), M9[:, 0:8].unsqueeze(2).to_broadcast([4, 8, 128]), ADD),
              tR1, t1)
    twi = act(lambda e: e.activation(wi, wi, ACT.Exp), twi)
    tws = dve(lambda e: e.tensor_tensor(c8(iR), c8(c1), c8(R1)[:, :, 127:128].to_broadcast([4, 8, 128]), ADD), tR1)
    tws = act(lambda e: e.activation(iR, iR, ACT.Exp), tws)
    mc = small[:, 288:384].rearrange("p (q t h) -> p q t h", q=3, t=8)
    b, free = banks1.take()
    for q, (src, tk) in enumerate(((c1, tc1), (iR, tws), (fR, t_em))):
        for tt in range(8):
            o = bank(b)[:, q * 32 + tt * 4:q * 32 + tt * 4 + 4]
            t = transpose(o, src[:, tt * 128:(tt + 1) * 128], tk, free, inc=(q == 2 and tt == 7))
    tmc = dve(lambda e: e.tensor_copy(small[:, 288:384], bank(b)[:, 0:96]), t)
    banks1.give(b, tmc)
    dec = small[:, 384:416]

    tmpA = Places([0, 1])
    XA = [work(4096, 1024), work(5120, 1024)]
    att_done = [mix_tok["a", n, jp] for jp in range(2) for n in range(8)]
    XB = [Pv[0], Pv[1]]
    XC = [PTv[0], PTv[1]]
    Cb = [Hr[:, 0:516].rearrange("p (s e) -> p s e", s=4), Hr[:, 516:1032].rearrange("p (s e) -> p s e", s=4)]
    hbuf = [Hr[:, 2048:3072], Hr[:, 3072:4096]]
    hfree = [[], []]
    SC = 128.0 ** -0.5
    pe_att = (pe.sem, pe.n)
    xfree = [[pe_att], [pe_att]]

    def mlstm(h):
        u = h % 2
        E, kt, qt = XA[u], XB[u], XC[u]
        qT, kT = mqk[:, h, :], mqk[:, 4 + h, :]
        hn = hbuf[u]
        wfree = [xfree[u], att_done]
        sel = cs("selh", 128 * h, 128 * h + 128)[0:4, :]
        b, free = banks2.take()
        for n in range(2):
            tk = pe(lambda e, n=n: e.matmul(pair(b)[:, 512 * n:512 * n + 512], sel, R1[:, 512 * n:512 * n + 512],
                                            start=True, stop=True), tR1, free, inc=(n == 1))
        for c in range(8):
            t = dve(lambda e, c=c: e.scalar_tensor_tensor(
                out=E[:, c * 128:(c + 1) * 128], in0=pair(b)[:, c * 128:(c + 1) * 128],
                scalar=mc[:, 0, c, h:h + 1], in1=cs("mst"), op0=ADD, op1=ADD), tk, tmc, wfree)
        banks2.give(b, t)
        tE = act(lambda e: e.activation(E, E, ACT.Exp), t)
        b, free = banks2.take()
        for n in range(2):
            tk = pe(lambda e, n=n, b=b: e.matmul(pair(b)[:, 512 * n:512 * n + 512], sel,
                                                 wi[:, 512 * n:512 * n + 512], start=True, stop=True),
                    twi, free, inc=(n == 1))
        tq = dve(lambda e, b=b: e.scalar_tensor_tensor(out=qt, in0=qT, scalar=SC, in1=pair(b), op0=MUL, op1=MUL),
                 tk, T["mqk", h], wfree)
        td = dve(lambda e, b=b: e.tensor_copy(dec[:, 8 * h:8 * h + 8], c8(pair(b))[:, :, 127]), tk)
        banks2.give(b, tq, td)
        yield
        b, free = banks2.take()
        for c in range(8):
            sl = slice(c * 128, (c + 1) * 128)
            tk = pe(lambda e, sl=sl, b=b: e.matmul(pair(b)[:, sl], kT[:, sl], qT[:, sl], start=True, stop=True),
                    T["mqk", h], T["mqk", 4 + h], free, inc=(c == 7))
        tsc = dve(lambda e, b=b: e.scalar_tensor_tensor(out=E, in0=pair(b), scalar=SC, in1=E, op0=MUL, op1=MUL),
                  tk, tE)
        banks2.give(b, tsc)
        b, free = banks2.take()
        for c in range(8):
            sl = slice(c * 128, (c + 1) * 128)
            tk = transpose(pair(b)[:, sl], kT[:, sl], free, inc=(c == 7))
        for c in range(8):
            sl = slice(c * 128, (c + 1) * 128)
            tkt = act(lambda e, sl=sl, c=c, b=b: e.activation(kt[:, sl], pair(b)[:, sl], ACT.Copy,
                                                              scale=mc[:, 1, c, h:h + 1]), tk, tmc, wfree)
        banks2.give(b, tkt)
        yield
        tC = None
        vt = [T["mv", tt, c] for tt in range(8) for c in range(2)]
        th = []
        for c in range(8):
            sl = slice(c * 128, (c + 1) * 128)
            va = mva[:, c, h, :]
            Cold, Cnew = Cb[u][:, (c + 3) % 4, :], Cb[u][:, c % 4, :]
            b, free = banks1.take()
            num = bank(b)[:, 0:129]
            tn = pe(lambda e, num=num, sl=sl, va=va, c=c: e.matmul(num, E[:, sl], va, start=True, stop=(c == 0)),
                    tsc, vt, t_ones, free, inc=(c == 0))
            if c:
                tn = pe(lambda e, num=num, sl=sl, Cold=Cold: e.matmul(num, qt[:, sl], Cold, start=False,
                                                                      stop=True), tq, tC)
            if c < 7:
                b2, free = banks1.take()
                kv = bank(b2)[:, 0:129]
                tk = pe(lambda e, kv=kv, sl=sl, va=va: e.matmul(kv, kt[:, sl], va, start=True, stop=True),
                        tkt, free)
                if c == 0:
                    tC2 = dve(lambda e, kv=kv, Cnew=Cnew: e.tensor_copy(Cnew, kv), tk, h_free, xfree[u], t_alib)
                else:
                    tC2 = dve(lambda e, kv=kv, Cnew=Cnew, Cold=Cold, c=c: e.scalar_tensor_tensor(
                        out=Cnew, in0=Cold, scalar=dec[:, 8 * h + c:8 * h + c + 1], in1=kv, op0=MUL, op1=ADD),
                        tk, tC, td, tn)
                banks1.give(b2, tC2)
                tC = tC2
            dn = small[:, 416 + 8 * h + c:417 + 8 * h + c]
            t = act(lambda e: e.activation(dn, num[:, 128:129], ACT.Abs), tn)
            t = dve(lambda e: e.tensor_tensor(dn, dn, mc[:, 2, c, h:h + 1], MAX), t)
            t = dve(lambda e, dn=dn: e.reciprocal(dn, dn), t)
            t = dve(lambda e, num=num, dn=dn, sl=sl: e.tensor_scalar(hn[:, sl], num[:, 0:128], dn, None, MUL),
                    t, h_free, hfree[u])
            banks1.give(b, t)
            th.append(t)
            if c % 2:
                yield
        b, free = banks2.take()
        for c in range(8):
            sl = slice(c * 128, (c + 1) * 128)
            tk = transpose(pair(b)[:, sl], hn[:, sl], th[c], free, inc=(c == 7))
        hfree[u] = [tk]
        xfree[u] = [tk, pe_att]
        t = dve(lambda e, b=b: e.tensor_tensor(mixM[:, h, :], pair(b), mo[:, h, :], MUL), tk, T["mo", h], h_free)
        banks2.give(b, t)
        mix_tok["m", h] = t

    run(staggered([mlstm(h) for h in range(4)], 1))
    ml_done = [mix_tok["m", h] for h in range(4)] + [(pe.sem, pe.n), (dve.sem, dve.n), (act.sem, act.n)]
    for i in ids:
        slots.give(i, ml_done)

    mixs = tiles(aqT) + tiles(mixM)
    mtok = [[mix_tok["a", n, k // 2] for n in range(8)] for k in range(4)] + \
           [mix_tok["m", h] for h in range(4)]
    tX2 = {}
    run(gemmT(d["w_out"], 0, 8, mixs, mtok, add_x(tX, tX2)))
    done1 = (pe.sem, pe.n)
    qx = v3(work(0, 8192), 8)
    memT = v3(work(8192, 2048), 8)
    hm = v3(work(10240, 2048), 8)
    kx = v3(work(12288, 2048), 8)
    vx = v3(work(14336, 2048), 2)
    Pv2 = [work(16384, 1024), work(17408, 1024)]
    PTv2 = [work(18432, 1024), work(19456, 1024)]
    wfree = [ml_done, done1]
    t_mem = once(sp, memT, d["memT"].rearrange("(k p) n -> p k n", p=128), wfree)
    tm = rms(memT, [t_mem] * 8, 256, lambda k: col("g_mem", k), hm, wfree)
    hms = tiles(hm)
    T2 = {}

    def ev_kx(m, ps, tk):
        T2["k", m] = act(lambda e: e.activation(kx[:, m, :], ps, ACT.Copy), tk, wfree)
        return T2["k", m]

    def ev_vx(c):
        def f(tt, ps, tk):
            T2["v", tt, c] = act(lambda e: e.activation(vx[:, tt, 256 * c:256 * c + 256], ps, ACT.Copy), tk,
                                 wfree)
            return T2["v", tt, c]
        return f
    run(gemmT(d["wkv"], 0, 8, hms, tm, ev_kx, N=256))
    for c in range(4):
        run(gemmN(d["wkv"], 1024 + 256 * c, 256, hms, tm, ev_vx(c), T=2))
    xt = [tX2[m] for m in range(8)]
    tH = rms(XT, xt, 1024, lambda k: col("g_x", k), H, done1)

    def ev_qx(m, ps, tk):
        T2["q", m] = act(lambda e: e.activation(qx[:, m, :], ps, ACT.Copy), tk, wfree)
        return T2["q", m]
    run(gemmT(d["wq"], 0, 8, Hs, tH, ev_qx))
    qdone = (pe.sem, pe.n)
    Pb = Places([0, 1, ])
    PTb = Places([0, 1])
    Pb.free = [(0, wfree), (1, wfree)]
    PTb.free = [(0, wfree), (1, wfree)]
    tO = {}

    def cross(n):
        b, free = banks2.take()
        S = pair(b).rearrange("p (g w) -> p g w", g=4)
        for h in range(4):
            for dd in range(2):
                tS = pe(lambda e, h=h, dd=dd: e.matmul(
                    S[:, h, :], qx[:, 2 * h + dd, n * 128:(n + 1) * 128], kx[:, 2 * h + dd, :],
                    start=(dd == 0), stop=(dd == 1)), T2["q", 2 * h + dd], T2["k", 2 * h + dd], free,
                    inc=(dd == 1))
        p, pfree = Pb.take()
        P = Pv2[p].rearrange("p (g w) -> p g w", g=4)
        tP, tr = softmax(S, tS, P, 256, 4, 1.0 / 16, None, None, stat(), pfree)
        banks2.give(b, tr)
        yield
        b, free = banks2.take()
        for g in range(4):
            for kt in range(2):
                tt = transpose(pair(b)[:, (2 * g + kt) * 128:(2 * g + kt + 1) * 128],
                               P[:, g, kt * 128:(kt + 1) * 128], tP, free, inc=(g == 3 and kt == 1))
        Pb.give(p, tt)
        q, qfree = PTb.take()
        PT = PTv2[q]
        t1 = act(lambda e: e.activation(PT[:, 0:512], pair(b)[:, 0:512], ACT.Copy), tt, qfree)
        t2 = dve(lambda e: e.tensor_copy(PT[:, 512:1024], pair(b)[:, 512:1024]), tt, qfree)
        banks2.give(b, t1, t2)
        yield
        b, free = banks2.take()
        for h in range(4):
            for dd in range(2):
                for kt in range(2):
                    m = 2 * h + dd
                    to = pe(lambda e, h=h, kt=kt, m=m, b=b: e.matmul(
                        pair(b)[:, m * 128:(m + 1) * 128], vx[:, kt, m * 128:(m + 1) * 128],
                        PT[:, (2 * h + kt) * 128:(2 * h + kt + 1) * 128], start=(kt == 0), stop=(kt == 1)),
                        t1, t2, T2["v", kt, m // 2], free, inc=(kt == 1))
        PTb.give(q, to)
        t = dve(lambda e: e.tensor_copy(H[:, :, n * 128:(n + 1) * 128],
                                        pair(b).rearrange("p (m q) -> p m q", m=8)), to, qdone)
        banks2.give(b, t)
        tO[n] = t
    run(staggered([cross(n) for n in range(8)], 3))
    ot = [[tO[n] for n in range(8)]] * 8
    tX3 = {}
    run(gemmT(d["wo"], 0, 8, Hs, ot, add_x(xt, tX3)))
    done2 = (pe.sem, pe.n)
    acts = v3(work(0, 22528), 22)
    pads = [work(22528, 1026), work(23554, 1026)]
    wfree = [done2, (act.sem, act.n), (dve.sem, dve.n)]
    xt = [tX3[m] for m in range(8)]
    tH = rms(XT, xt, 1024, lambda k: col("g_ffn", k), H, done2)
    tz = [dve(lambda e, i=i: e.memset(pads[i][:, 0:2], 0.0), wfree) for i in range(2)]
    pf = [wfree, wfree]
    tA = {}

    def ev_g(m, ps, tk):
        i = m % 2
        te = act(lambda e: e.activation(pads[i][:, 2:1026], ps, ACT.Copy), tk, pf[i])
        t = conv(pads[i], 3, lambda j: col("fw", m * 3 + j), col("fb", m), acts[:, m, :], 3, [te, tz[i]],
                 wfree)
        pf[i] = t
        tA[m] = act(lambda e: e.activation(acts[:, m, :], acts[:, m, :], ACT.Silu), t)
        return te

    def ev_u(m, ps, tk):
        tA[m] = dve(lambda e: e.tensor_tensor(acts[:, m, :], ps, acts[:, m, :], MUL), tk, tA[m])
        return tA[m]
    for m in range(0, 22, 2):
        run(gemmT(d["w_up"], m * 128, 2, Hs, tH, lambda i, ps, tk, m=m: ev_g(m + i, ps, tk)))
        if m:
            run(gemmT(d["w_up"], 2816 + (m - 2) * 128, 2, Hs, tH,
                      lambda i, ps, tk, m=m: ev_u(m - 2 + i, ps, tk)))
    run(gemmT(d["w_up"], 2816 + 20 * 128, 2, Hs, tH, lambda i, ps, tk: ev_u(20 + i, ps, tk)))
    tX4 = {}
    run(gemmT(d["w_down"], 0, 8, tiles(acts), [tA[m] for m in range(22)], add_x(xt, tX4)))
    xt = [tX4[m] for m in range(8)]
    done3 = (pe.sem, pe.n)
    tY0 = rms(XT, xt, 1024, lambda k: col("g_fin", k), H, done3)
    tY = [act(lambda e, k=k: e.activation(XT[:, k, :], H[:, k, :], ACT.Copy), tY0[k]) for k in range(8)]
    tH = rms(XT, tY, 1024, lambda k: gs2[:, k:k + 1], H, [tY, tY0], scale1=t_mod,
             bias=lambda k: mod[:, k:k + 1])
    spilled = spill.rearrange("(k p) n -> p k n", p=128)
    t_spill = once(sp, spilled, XT, tY)
    wfree = [(pe.sem, pe.n), (act.sem, act.n), (dve.sem, dve.n)]
    W2 = d["w_in2"]
    aq, ak = v3(work(0, 4096), 4), v3(work(4096, 4096), 4)
    av = v3(work(8192, 4096), 8)
    ag = v3(work(12288, 4096), 4)
    BT = v3(work(16384, 5120), 8)
    t_bt = once(sp, BT, d["band"].rearrange("p (h k) -> p h k", h=8), wfree)
    t_b2 = once(sp, work(21504, 640), d["bmask"], wfree)
    bmask = work(21504, 640)
    tBT = None
    for h in range(8):
        tBT = dve(lambda e, h=h: e.tensor_tensor(BT[:, h, :], BT[:, h, :], bmask, ADD), t_bt, t_b2)
    T3 = {}

    def ev_copy(name, dst):
        def f(m, ps, tk):
            T3[name, m] = act(lambda e: e.activation(dst[:, m, :], ps, ACT.Copy), tk, wfree)
            return T3[name, m]
        return f

    def ev_ag(m, ps, tk):
        T3["ag", m] = act(lambda e: e.activation(ag[:, m, :], ps, ACT.Silu), tk, wfree)
        return T3["ag", m]

    def ev_av2(c):
        def f(tt, ps, tk):
            T3["av", tt, c] = act(lambda e: e.activation(av[:, tt, 256 * c:256 * c + 256], ps, ACT.Copy), tk,
                                  wfree)
            return T3["av", tt, c]
        return f
    run(gemmT(W2, 2176, 4, Hs, tH, ev_copy("aq", aq)))
    run(gemmT(W2, 2688, 4, Hs, tH, ev_copy("ak", ak)))
    for c in range(2):
        run(gemmN(W2, 3200 + 256 * c, 256, Hs, tH, ev_av2(c)))
    run(gemmT(W2, 3712, 4, Hs, tH, ev_ag))

    def head_scale(tl, toks, fin, tmp, tfree):
        b, free = banks1.take()
        sqf = [tfree, tfree]
        for j in range(4):
            sq = tmp[:, 1024 * (j % 2):1024 * (j % 2) + 1024]
            ts = act(lambda e, j=j, sq=sq: e.activation(sq, tl[j], ACT.Square), toks[j], sqf[j % 2])
            for tt in range(8):
                o = bank(b)[:, tt * 8 + 2 * j:tt * 8 + 2 * j + 2]
                tk = pe(lambda e, sq=sq, tt=tt, o=o: e.matmul(o, sq[:, tt * 128:(tt + 1) * 128], cs("bo"),
                                                              start=True, stop=True), ts, free)
            sqf[j % 2] = tk
        st = small[:, 448:512]
        t = fin(st, bank(b)[:, 0:64], tk)
        banks1.give(b, t[0])
        t = t[1]
        p, free = banks2.take()
        for tt in range(8):
            tk2 = transpose(pair(p)[0:8, tt * 128:(tt + 1) * 128], st[:, tt * 8:tt * 8 + 8], t, free,
                            inc=(tt == 7))
        rr = tmp[0:8, 0:1024]
        t = dve(lambda e: e.tensor_copy(rr, pair(p)[0:8, :]), tk2, tk)
        banks2.give(p, t)
        return rr, t

    def head_mult(tl, toks, rr, tr, scal, out):
        for j in range(4):
            p, free = banks2.take()
            for n in range(2):
                tk = pe(lambda e, j=j, n=n, p=p: e.matmul(
                    pair(p)[:, 512 * n:512 * n + 512], cs("selp", 128 * j, 128 * j + 128)[0:8, :],
                    rr[:, 512 * n:512 * n + 512], start=True, stop=True), tr, free, inc=(n == 1))
            out[j] = dve(lambda e, j=j, p=p: e.scalar_tensor_tensor(
                out=tl[j], in0=tl[j], scalar=scal(j), in1=pair(p), op0=MUL, op1=MUL), tk, toks[j], t_col)
            banks2.give(p, out[j])
        return tk

    def fin_rms(st, ps, tk):
        a = dve(lambda e: e.tensor_scalar(st, ps, 1.0 / 64, 1e-6, MUL, ADD), tk)
        t = act(lambda e: e.activation(st, st, ACT.Sqrt), a)
        return a, dve(lambda e: e.reciprocal(st, st), t)

    for name, tl, g in (("aq", aq, "qng"), ("ak", ak, "kng")):
        i, sfree = slots.take()
        toks = [T3[name, m] for m in range(4)]
        rr, tr = head_scale(tiles(tl), toks, fin_rms, slot(i), sfree)
        out = {}
        tk = head_mult(tiles(tl), toks, rr, tr, lambda j, g=g: col(g), out)
        slots.give(i, tk)
        for m in range(4):
            T3[name, m] = out[m]
    Pi, pf0 = slots.take()
    Qi, qf0 = slots.take()
    Pb, PTb = Places([]), Places([])
    Pb.free = [(0, pf0), (1, pf0), (2, pf0)]
    PTb.free = [(0, qf0), (1, qf0), (2, qf0)]
    Pv3 = [slot(Pi)[:, 640 * i:640 * i + 640] for i in range(3)]
    PTv3 = [slot(Qi)[:, 640 * i:640 * i + 640] for i in range(3)]
    ob = {}
    tya = {}

    def band(j, n, a):
        nk = min(5, n + 1)
        W = 128 * nk
        k0 = (n + 1 - nk) * 128
        h = 2 * j + a
        b, free = banks2.take()
        for c0 in range(0, W, 512):
            cn = min(512, W - c0)
            tS = pe(lambda e, c0=c0, cn=cn, b=b: e.matmul(
                pair(b)[:, c0:c0 + cn], aq[64 * a:64 * a + 64, j, n * 128:(n + 1) * 128],
                ak[64 * a:64 * a + 64, j, k0 + c0:k0 + c0 + cn], start=True, stop=True),
                T3["aq", j], T3["ak", j], free)
        p, pfree = Pb.take()
        P = Pv3[p][:, 0:W].rearrange("p (g w) -> p g w", g=1)
        S = pair(b)[:, 0:W].rearrange("p (g w) -> p g w", g=1)
        bias = BT[:, h:h + 1, 640 - W:640]
        tP, tr = softmax(S, tS, P, W, 1, 0.125, bias, None, stat(), pfree, tBT)
        banks2.give(b, tr)
        yield
        b, free = banks2.take()
        for kt in range(nk):
            tt = transpose(pair(b)[:, kt * 128:(kt + 1) * 128], P[:, 0, kt * 128:(kt + 1) * 128], tP, free,
                           inc=(kt == nk - 1))
        Pb.give(p, tt)
        q, qfree = PTb.take()
        PT = PTv3[q]
        t1 = act(lambda e, b=b: e.activation(PT[:, 0:W], pair(b)[:, 0:W], ACT.Copy), tt, qfree)
        banks2.give(b, t1)
        yield
        if a == 0:
            ob[j, n] = banks1.take()
        b, free = ob[j, n]
        for kt in range(nk):
            tile = k0 // 128 + kt
            to = pe(lambda e, kt=kt, tile=tile, b=b: e.matmul(
                bank(b)[64 * a:64 * a + 64, 0:128], av[:, tile, 64 * h:64 * h + 64],
                PT[:, kt * 128:(kt + 1) * 128], start=(kt == 0), stop=(kt == nk - 1)),
                t1, T3["av", tile, h // 4], free, inc=(kt == nk - 1))
        PTb.give(q, to)
        if a == 1:
            sl = slice(n * 128, (n + 1) * 128)
            t = dve(lambda e, b=b: e.tensor_tensor(aq[:, j, sl], bank(b)[:, 0:128], ag[:, j, sl], MUL), to,
                    T3["ag", j])
            banks1.give(b, t)
            tya[j, n] = t
    run(staggered([band(j, n, a) for j in range(4) for n in range(8) for a in range(2)], 3))
    slots.give(Pi, (pe.sem, pe.n), (act.sem, act.n), (dve.sem, dve.n))
    slots.give(Qi, (pe.sem, pe.n), (act.sem, act.n), (dve.sem, dve.n))
    rr_, kk_, vv_, gg_ = (v3(work(4096 * (1 + i), 4096), 4) for i in range(4))
    lo = work(20480, 1024)
    pads = [work(21504, 1025), work(22529, 1025)]
    lw = work(23554, 1024)
    wfree = [(pe.sem, pe.n), (act.sem, act.n), (dve.sem, dve.n)]
    t_lw = once(sp, lw[:, 0:512], d["lora"], wfree)
    tz = [dve(lambda e, i=i: e.memset(pads[i][:, 0:1], 0.0), wfree) for i in range(2)]
    pf = [wfree, wfree]
    T4 = {}
    mun = small[:, 512:529]
    tmu = dve(lambda e: e.tensor_scalar(mun, cols[:, COLS["mu"][0]:COLS["mu"][0] + 17], -1.0, 1.0, MUL, ADD),
              t_col)
    cnt = [0]

    def ev_shift(base, name, dst):
        def f(m, ps, tk):
            i = cnt[0] % 2
            cnt[0] += 1
            pad = pads[i]
            te = act(lambda e: e.activation(pad[:, 1:1025], ps, ACT.Copy), tk, pf[i])
            q = base + m
            t = dve(lambda e: e.tensor_scalar(dst[m], pad[:, 1:1025], mun[:, q:q + 1], None, MUL), te, tmu,
                    wfree)
            t = dve(lambda e: e.scalar_tensor_tensor(out=dst[m], in0=pad[:, 0:1024], scalar=col("mu", q),
                                                     in1=dst[m], op0=MUL, op1=ADD), t, tz[i])
            pf[i] = t
            if name == "g":
                t = act(lambda e: e.activation(dst[m], dst[m], ACT.Silu), t)
            T4[name, m] = t
            return te
        return f
    run(gemmT(W2, 2048, 1, Hs, tH, ev_shift(16, "lo", [lo])))
    for q, (nm, dst) in enumerate((("r", rr_), ("k", kk_), ("v", vv_), ("g", gg_))):
        run(gemmT(W2, 512 * q, 4, Hs, tH, ev_shift(4 * q, nm, tiles(dst))))
    hfree5 = [(pe.sem, pe.n)]
    ttanh = act(lambda e: e.activation(lo[0:64, :], lo[0:64, :], ACT.Tanh), T4["lo", 0])
    sg, aa = v3(Hr[:, 0:4096], 4), v3(Hr[:, 4096:8192], 4)
    for q, (dst, bias) in enumerate(((sg, "w0"), (aa, "a0"))):
        for j in range(4):
            b, free = banks2.take()
            for n in range(2):
                tk = pe(lambda e, q=q, j=j, n=n, b=b: e.matmul(
                    pair(b)[:, 512 * n:512 * n + 512], lw[64 * q:64 * q + 64, 128 * j:128 * j + 128],
                    lo[64 * q:64 * q + 64, 512 * n:512 * n + 512], start=True, stop=True),
                    t_lw, ttanh, T4["lo", 0], free, inc=(n == 1))
            T4[bias, j] = act(lambda e, b=b, j=j, dst=dst, bias=bias: e.activation(
                dst[:, j, :], pair(b), ACT.Sigmoid, bias=col(bias, j)), tk, hfree5)
            banks2.give(b, T4[bias, j])
    lora_done = [(pe.sem, pe.n)]
    allf = [(pe.sem, pe.n), (act.sem, act.n), (dve.sem, dve.n)]
    sl_ids = [slots.take() for _ in range(4)]
    sf = [x[1] for x in sl_ids]
    i0 = [x[0] for x in sl_ids]
    rs64 = slot(i0[0])[:, 0:1024]
    t_rs64 = once(sp, rs64, d["reset64"], sf[0])
    XS = [XT[:, k, :] for k in range(8)]
    kn = v3(XTr[:, 0:4096], 4)
    PLc = v3(small[:, 544:608], 4)
    tkk = {}
    for j in range(4):
        tkk[j] = act(lambda e, j=j: e.activation(kn[:, j, :], kk_[:, j, :], ACT.Copy, scale=col("kk", j)),
                     T4["k", j], t_spill)

    def fin_l2(st, ps, tk):
        t = act(lambda e: e.activation(st, ps, ACT.Sqrt), tk)
        t2 = dve(lambda e: e.tensor_scalar(st, st, 1e-12, None, MAX), t)
        return t, dve(lambda e: e.reciprocal(st, st), t2)
    rr, tr = head_scale(tiles(kn), tkk, fin_l2, slot(i0[1]), sf[1])
    out = {}
    head_mult(tiles(kn), tkk, rr, tr, lambda j: 1.0, out)
    bon = v3(small[:, 608:672], 8)
    b, freeb = banks1.take()
    tr_ = {}
    for j in range(4):
        A, B, C, D = (XTr[:, 4096 + 1024 * i:5120 + 1024 * i] for i in range(4))
        A2 = slot(i0[0])[:, 1024:2048]
        pt = T4.get(("prep", j - 1))
        t1 = dve(lambda e, j=j: e.tensor_scalar(A, aa[:, j, :], 1.0, col("ka", j), SUB, MUL), T4["a0", j],
                 t_spill, pt)
        t1 = dve(lambda e, j=j: e.scalar_tensor_tensor(out=kk_[:, j, :], in0=A, scalar=1.0, in1=kk_[:, j, :],
                                                       op0=ADD, op1=MUL), t1, tkk[j])
        t2 = dve(lambda e, j=j: e.tensor_tensor(aa[:, j, :], aa[:, j, :], kn[:, j, :], MUL), out[j], t1)
        t3 = dve(lambda e, j=j: e.scalar_tensor_tensor(out=D, in0=rr_[:, j, :], scalar=col("rk", j),
                                                       in1=kk_[:, j, :], op0=MUL, op1=MUL), t1, T4["r", j],
                 pt, t_col)
        for tt in range(8):
            o = bank(b)[:, tt * 8 + 2 * j:tt * 8 + 2 * j + 2]
            tbo = pe(lambda e, tt=tt, o=o: e.matmul(o, D[:, tt * 128:(tt + 1) * 128], cs("bo"), start=True,
                                                    stop=True), t3, freeb)
        t4 = dve(lambda e, j=j: e.tensor_tensor_scan(B, rs64, sg[:, j, :], 0.0, MUL, ADD), T4["w0", j],
                 t_rs64, pt)
        t5 = dve(lambda e, j=j: e.tensor_tensor(A, B, sg[:, j, :], SUB), t4, t1)
        t6 = act(lambda e: e.activation(C, B, ACT.Exp, scale=EH), t4, pt)
        t7 = act(lambda e: e.activation(B, B, ACT.Exp, scale=-EH), t4, t5)
        t8 = act(lambda e: e.activation(A, A, ACT.Exp, scale=-EH), t5)
        t9 = dve(lambda e, j=j: e.scalar_tensor_tensor(out=sg[:, j, :], in0=kn[:, j, :], scalar=-1.0, in1=A,
                                                       op0=MUL, op1=MUL), t8, t5)
        ta = dve(lambda e, j=j: e.tensor_tensor(aa[:, j, :], aa[:, j, :], C, MUL), t6, t2)
        tb_ = dve(lambda e, j=j: e.tensor_tensor(kk_[:, j, :], kk_[:, j, :], C, MUL), t6, t3)
        tc = dve(lambda e, j=j: e.tensor_tensor(rr_[:, j, :], rr_[:, j, :], B, MUL), t7, t3)
        td = dve(lambda e, j=j: e.tensor_copy(PLc[:, j, :], B.rearrange("p (c t) -> p c t", c=16)[:, :, 63]),
                 t7)
        T4["prep", j] = [t9, ta, tb_, tc, td, tbo]
    prep = [T4["prep", j] for j in range(4)]
    tbon = dve(lambda e: e.tensor_copy(small[:, 608:672], bank(b)[:, 0:64]), tbo)
    banks1.give(b, tbon)
    At, Bh, Kh, Rt = sg, aa, kk_, rr_

    allf = [prep, tbon, lora_done]
    m2 = XTr[:, 0:1280]
    t_m2 = once(sp, m2, d["m2"], allf)
    mAR = m2[:, 0:256].rearrange("p (q t) -> p q t", q=2)
    mL, m0, m0T = m2[:, 256:384], m2[:, 384:512], m2[:, 512:640]
    lv = [m2[:, 640 + 128 * l:768 + 128 * l] for l in range(5)]
    spare = [XTr[:, 1280:8192], RING, work(20480, WN - 20480)]
    used = [0, 0, 0]

    def place(n):
        for i, r in enumerate(spare):
            if used[i] + n <= r.shape[1]:
                used[i] += n
                return r[:, used[i] - n:used[i]]
        assert False
    per = [dict(TT=place(1024), RB=place(1024), NV=place(512), RKV=place(512), vt=place(512), kt=place(512),
                bt=place(512)) for _ in range(2)]
    gMT, gM, gT, gX, gN = place(1024), place(1024), place(1024), place(1024), place(1024)
    gRK = gX
    Zb = v3(place(512), 4)
    Xs, Us = place(512), place(512)
    Zt = place(512)
    ych = [place(512), place(512)]
    t_z = dve(lambda e: e.memset(Zb, 0.0), allf)
    state = {"Z": t_z, "gfree": allf, "xs": allf, "us": allf}
    pfree_ = [allf, allf]
    yfree = [allf, allf]
    h8 = lambda v: v.rearrange("p (h t) -> p h t", h=8)
    yr = Rt
    tyr = {}

    def bc(m, n=8):
        return m.unsqueeze(1).to_broadcast([128, n, 128])

    def pre(cp):
        r = per[cp % 2]
        sl = slice(128 * cp, 128 * cp + 128)
        fr = [pfree_[cp % 2]]
        gf = state["gfree"]
        TT, RB = h8(r["TT"]), h8(r["RB"])
        MT, M, Tm, X, N = h8(gMT), h8(gM), h8(gT), h8(gX), h8(gN)
        RK = h8(gRK)
        tks = []
        for src, dst in ((vv_, "vt"), (Kh, "kt"), (Bh, "bt")):
            b, free = banks1.take()
            for j in range(4):
                tk = transpose(bank(b)[:, 128 * j:128 * j + 128], src[:, j, sl], free, prep,
                               T4["v", j], inc=(j == 3))
            t = act(lambda e, b=b, dst=dst: e.activation(r[dst], bank(b), ACT.Copy), tk, fr)
            banks1.give(b, t)
            tks.append(t)
        for lhs, outs in ((Bh, ((MT, At, 0), (RB, Rt, 1))), (Kh, ((N, At, 0), (RK, Rt, 1)))):
            for dst, rhs, q in outs:
                b, free = banks2.take()
                for a in range(2):
                    for j in range(4):
                        o = pair(b)[:, 512 * a + 128 * j:512 * a + 128 * j + 128]
                        tk = pe(lambda e, a=a, j=j, o=o, lhs=lhs, rhs=rhs: e.matmul(
                            o, lhs[64 * a:64 * a + 64, j, sl], rhs[64 * a:64 * a + 64, j, sl], start=True,
                            stop=True), free, prep, inc=(a == 1 and j == 3))
                t = dve(lambda e, b=b, dst=dst, q=q: e.tensor_tensor(dst, h8(pair(b)), bc(mAR[:, q, :]), MUL),
                        tk, t_m2, fr, gf)
                banks2.give(b, t)
                r["t", id(dst)] = t
                if dst is MT:
                    tMT = t
                elif dst is RB:
                    tRB = t
                elif dst is N:
                    tN = t
                else:
                    tRK = t
        b, free = banks2.take()
        for a in range(2):
            for j in range(4):
                o = pair(b)[:, 512 * a + 128 * j:512 * a + 128 * j + 128]
                tk = pe(lambda e, a=a, j=j, o=o, b=b: e.matmul(
                    o, At[64 * a:64 * a + 64, j, sl], Bh[64 * a:64 * a + 64, j, sl], start=True, stop=True),
                    free, inc=(a == 1 and j == 3))
        tM = dve(lambda e, b=b: e.tensor_tensor(M, h8(pair(b)), bc(m0), MUL), tk, t_m2, gf)
        banks2.give(b, tM)
        yield
        for src, tsrc, dst in ((N, tN, "NV"), (RK, tRK, "RKV")):
            b, free = banks1.take()
            for g in range(8):
                hh = 2 * (g % 4) + g // 4
                tk = pe(lambda e, g=g, hh=hh, b=b, src=src: e.matmul(
                    bank(b)[:, 64 * g:64 * g + 64], src[:, g, :], r["vt"][:, 64 * hh:64 * hh + 64],
                    start=True, stop=True), tsrc, tks[0], free, inc=(g == 7))
            t = act(lambda e, b=b, dst=dst: e.activation(r[dst], bank(b), ACT.Copy), tk, fr)
            banks1.give(b, t)
            r["t" + dst] = t
        tT = dve(lambda e: e.tensor_tensor(Tm, M, bc(I), ADD), tM, gf)
        tTT = dve(lambda e: e.tensor_tensor(TT, MT, bc(m0T), MUL), tMT, fr)
        tTT = dve(lambda e: e.tensor_tensor(TT, TT, bc(I), ADD), tTT)
        tX_ = [t]
        for l in range(5):
            b, free = banks2.take()
            for g in range(8):
                tk = pe(lambda e, g=g, b=b: e.matmul(pair(b)[:, 128 * g:128 * g + 128], MT[:, g, :],
                                                     Tm[:, g, :], start=True, stop=True), tMT, tT, free,
                        inc=(g == 7))
            tXX = dve(lambda e, b=b, l=l: e.tensor_tensor(X, h8(pair(b)), bc(lv[l]), MUL), tk, tX_)
            banks2.give(b, tXX)
            yield
            b, free = banks2.take()
            for g in range(8):
                tk = pe(lambda e, g=g, b=b: e.matmul(pair(b)[:, 128 * g:128 * g + 128], X[:, g, :],
                                                     TT[:, g, :], start=True, stop=True), tXX, tTT, free,
                        inc=(g == 7))
            tk1 = tk
            if l < 4:
                b2, free = banks2.take()
                for g in range(8):
                    tk = pe(lambda e, g=g, b2=b2: e.matmul(pair(b2)[:, 128 * g:128 * g + 128], TT[:, g, :],
                                                           X[:, g, :], start=True, stop=True), free,
                            inc=(g == 7))
                tT = dve(lambda e, b2=b2: e.tensor_tensor(Tm, h8(pair(b2)), Tm, ADD), tk, tT)
                banks2.give(b2, tT)
            tTT = dve(lambda e, b=b: e.tensor_tensor(TT, h8(pair(b)), TT, ADD), tk1, tk, tTT)
            banks2.give(b, tTT)
            tX_ = [tk]
            yield
        r["tTT"], r["tRB"], r["tks"] = tTT, tRB, tks
        state["gfree"] = [tk, tTT]

    def seq(cp):
        r = per[cp % 2]
        sl = slice(128 * cp, 128 * cp + 128)
        TT, RB = h8(r["TT"]), h8(r["RB"])
        y = ych[cp % 2]
        yb, yfr = banks1.take()
        for par in range(2):
            c = 2 * cp + par
            cols_ = slice(64 * c, 64 * c + 64)
            ps_ = slice(64 * par, 64 * par + 64)
            b, free = banks1.take()
            for j in range(4):
                o = bank(b)[ps_, :].rearrange("p (a j i) -> p a j i", a=2, j=4)[:, :, j, :]
                tk = pe(lambda e, j=j, o=o, cols_=cols_: e.matmul(o, At[:, j, cols_], Zb[:, j, :], start=True,
                                                                  stop=True), state["Z"], free, prep,
                        inc=(j == 3))
            tx = dve(lambda e, b=b, ps_=ps_: e.tensor_tensor(Xs[ps_, :], bank(b)[ps_, :], r["NV"][ps_, :],
                                                             ADD), tk, r["tNV"], state["xs"])
            banks1.give(b, tx)
            b, free = banks1.take()
            for g in range(8):
                tk = pe(lambda e, g=g, b=b, ps_=ps_: e.matmul(
                    bank(b)[ps_, 64 * g:64 * g + 64], TT[ps_, g, ps_], Xs[ps_, 64 * g:64 * g + 64],
                    start=True, stop=True), tx, r["tTT"], free, inc=(g == 7))
            state["xs"] = tk
            tu = dve(lambda e, b=b, ps_=ps_: e.tensor_copy(Us[ps_, :], bank(b)[ps_, :]), tk, state["us"])
            banks1.give(b, tu)
            b, free = banks2.take()
            for g in range(8):
                a, j = g // 4, g % 4
                hh = 2 * j + a
                o = pair(b)[64 * a:64 * a + 64, 64 * j:64 * j + 64]
                pe(lambda e, o=o, hh=hh, g=g, ps_=ps_: e.matmul(
                    o, r["bt"][ps_, 64 * hh:64 * hh + 64], Us[ps_, 64 * g:64 * g + 64], start=True,
                    stop=False), tu, r["tks"], free, inc=False)
                tk = pe(lambda e, o=o, hh=hh, ps_=ps_: e.matmul(
                    o, r["kt"][ps_, 64 * hh:64 * hh + 64], r["vt"][ps_, 64 * hh:64 * hh + 64],
                    start=False, stop=True), inc=(g == 7))
            ty = None
            for j in range(4):
                o = bank(yb)[ps_, :].rearrange("p (a j i) -> p a j i", a=2, j=4)[:, :, j, :]
                pe(lambda e, j=j, o=o, cols_=cols_: e.matmul(o, Rt[:, j, cols_], Zb[:, j, :], start=True,
                                                             stop=False, skip_group_check=True),
                   yfr, inc=False)
                for a in range(2):
                    g = 4 * a + j
                    ty = pe(lambda e, g=g, ps_=ps_: e.matmul(
                        bank(yb)[ps_, 64 * g:64 * g + 64], RB[ps_, g, ps_], Us[ps_, 64 * g:64 * g + 64],
                        start=False, stop=True, skip_group_check=True), r["tRB"], inc=(j == 3 and a == 1))
            state["us"] = ty
            tz_ = None
            for a in range(2):
                as_ = slice(64 * a, 64 * a + 64)
                zv = Zb[as_, :, 64 * a:64 * a + 64]
                pv = pair(b)[as_, 0:256].rearrange("p (j i) -> p j i", j=4)
                t1 = dve(lambda e, zv=zv, pv=pv: e.tensor_tensor(zv, pv, zv, ADD), tk, ty, state["Z"])
                tz_ = dve(lambda e, zv=zv, as_=as_, c=c: e.tensor_tensor(
                    zv, zv, PLc[as_, :, c:c + 1].to_broadcast([64, 4, 64]), MUL), t1)
            banks2.give(b, tz_)
            state["Z"] = tz_
            yield
        yf = yfree[cp % 2]
        nat = lambda v: v.rearrange("p (j a i) -> p a j i", j=4, a=2)
        byp = lambda v: v.rearrange("p (a j i) -> p a j i", j=4, a=2)
        ty2 = dve(lambda e: e.tensor_tensor(nat(y), byp(bank(yb)), byp(r["RKV"]), ADD), ty, r["tRKV"], yf)
        banks1.give(yb, ty2)
        yv = y.rearrange("p (g i) -> p g i", g=8)
        st = small[:, 672 + 16 * (cp % 2):688 + 16 * (cp % 2)]
        q2 = Zt
        b8 = lambda v: v.unsqueeze(2).to_broadcast([128, 8, 64])
        t = dve(lambda e: e.tensor_reduce(st[:, 0:8], yv, AX.X, ADD), ty2)
        t = dve(lambda e: e.tensor_scalar(st[:, 0:8], st[:, 0:8], 1.0 / 64, None, MUL), t)
        t = dve(lambda e: e.tensor_tensor(yv, yv, b8(st[:, 0:8]), SUB), t)
        ta = act(lambda e: e.activation(q2, y, ACT.Square), t, state.get("q2"))
        t = dve(lambda e: e.tensor_reduce(st[:, 8:16], q2.rearrange("p (g i) -> p g i", g=8), AX.X, ADD), ta)
        state["q2"] = t
        t = dve(lambda e: e.tensor_scalar(st[:, 8:16], st[:, 8:16], 1.0 / 64, 64e-5, MUL, ADD), t)
        t = act(lambda e: e.activation(st[:, 8:16], st[:, 8:16], ACT.Sqrt), t)
        t = dve(lambda e: e.reciprocal(st[:, 8:16], st[:, 8:16]), t)
        t = dve(lambda e: e.tensor_tensor(yv, yv, b8(st[:, 8:16]), MUL), t)
        t = dve(lambda e: e.tensor_tensor(y, y, row("lng"), MUL), t)
        t = dve(lambda e: e.tensor_tensor(y, y, row("lnb"), ADD), t)
        t = dve(lambda e: e.tensor_tensor(q2.rearrange("p (g i) -> p g i", g=8),
                                          r["vt"].rearrange("p (g i) -> p g i", g=8), b8(bon[:, cp, :]), MUL),
                t, tbon)
        t = dve(lambda e: e.tensor_tensor(y, y, q2, ADD), t)
        state["q2"] = t
        b, free = banks1.take()
        for j in range(4):
            tk = transpose(bank(b)[:, 128 * j:128 * j + 128], y[:, 128 * j:128 * j + 128], t, free,
                           inc=(j == 3))
        yfree[cp % 2] = tk
        t = dve(lambda e, b=b: e.tensor_tensor(yr[:, :, sl], bank(b).rearrange("p (j t) -> p j t", j=4),
                                               gg_[:, :, sl], MUL), tk, [T4["g", m] for m in range(4)], ty)
        banks1.give(b, t)
        tyr[cp] = t
        pfree_[cp % 2] = [t, tk, ty]
        yield

    run(pre(0))
    for cp in range(8):
        if cp < 7:
            run(pre(cp + 1))
        run(seq(cp))
    fin = [(pe.sem, pe.n), (act.sem, act.n), (dve.sem, dve.n)]
    for i in i0:
        slots.give(i, fin)
    tXr = [once(sp, XT[:, k, :], spilled[:, k, :], fin, t_spill) for k in range(8)]
    src = tiles(yr) + tiles(aq)
    stok = [list(tyr.values())] * 4 + [[tya[j, n] for n in range(8)] for j in range(4)]

    def ev_out(m, ps, tk):
        t = dve(lambda e: e.scalar_tensor_tensor(out=XT[:, m, :], in0=ps, scalar=mod[:, 16 + m:17 + m],
                                                 in1=XT[:, m, :], op0=MUL, op1=ADD), tk, tXr[m], t_mod)
        finals.append(once(act, d["out"][m * 128:(m + 1) * 128, :], XT[:, m, :], t))
        return t
    run(gemmT(d["w_out2"], 0, 8, src, stok, ev_out))
    sp(lambda e: e.nop(), finals, inc=False)


def host_layout(inputs):
    import numpy as np
    f = {k: np.asarray(v) for k, v in inputs.items()}

    def colv(v, k):
        return v.reshape(k, 128).T
    s = np.zeros((128, NCOLS), np.float32)

    def put(name, m):
        o, w = COLS[name]
        s[:, o:o + w] = m
    for name, key in (("g_mix", "norm_mix_g"), ("g_x", "norm_xattn_g"), ("g_mem", "norm_mem_g"),
                      ("g_ffn", "norm_ffn_g"), ("g_fin", "norm_final_g"), ("g_n2", "norm_g_2"), ("c", "c_2")):
        put(name, colv(f[key], 8))
    put("b_ada", colv(f["b_ada_2"], 24))
    put("convw", f["conv_qk_w"][0].reshape(4, 8, 128).transpose(2, 1, 0).reshape(128, 32))
    put("convb", colv(f["conv_qk_b"], 8))
    put("fw", f["conv_ffn_w"][0].reshape(3, 22, 128).transpose(2, 1, 0).reshape(128, 66))
    put("fb", colv(f["conv_ffn_b"], 22))
    put("mu", colv(f["mu_shift_2"], 17))
    for name, key in (("w0", "w0_2"), ("a0", "a0_2"), ("kk", "k_k_2"), ("ka", "k_a_2"), ("rk", "r_k_2")):
        put(name, colv(f[key], 4))
    for name, key in (("qng", "q_norm_g_2"), ("kng", "k_norm_g_2")):
        put(name, np.concatenate([f[key][0], f[key][0]])[:, None])
    order = [4 * a + j for j in range(4) for a in range(2)]
    sk = f["attn_sinks"][0]
    sinks = np.concatenate([sk[[2 * jp, 2 * jp + 1, 4 + 2 * jp, 5 + 2 * jp]] for jp in range(2)])
    lng = f["lnx_g_2"][0]
    lnb = f["lnx_b_2"][0]
    rows = np.concatenate([f["b_gate_if"][0], sinks, lng, lnb])
    rows = np.ascontiguousarray(np.broadcast_to(rows, (128, NROWS)))
    cst = np.zeros((128, NCST), np.float32)

    def putc(name, m):
        o, w = CST[name]
        cst[:m.shape[0], o:o + w] = m
    p = np.arange(128)
    putc("I", np.eye(128))
    putc("ones", np.ones((128, 128)))
    putc("bo", (p[:, None] // 64 == np.arange(2)[None]) * 1.0)
    putc("mst", np.where(p[:, None] <= p[None], 0.0, -1e30))
    putc("selh", (np.arange(4)[:, None] == (np.arange(512) // 128)[None]) * 1.0)
    q = np.arange(512)
    putc("selp", (np.arange(8)[:, None] == (2 * (q // 128) + (q % 128) // 64)[None]) * 1.0)
    slopes = 2.0 ** (-np.arange(1, 9, dtype=np.float32))
    dist = p[:, None] + 128 - np.arange(256)[None]
    ok = (dist >= 0) & (dist < 128)
    alibi = np.concatenate([np.where(ok, -slopes[h] * dist, -1e30) for jp in range(2)
                            for h in (2 * jp, 2 * jp + 1, 4 + 2 * jp, 5 + 2 * jp)], axis=1).astype(np.float32)
    r128 = np.ones((4, 1024), np.float32)
    r128[:, ::128] = 0
    r64 = np.ones((128, 1024), np.float32)
    r64[:, ::64] = 0
    same = p[:, None] // 64 == p[None] // 64
    strict = same & (p[:, None] < p[None])
    incl = same & (p[:, None] <= p[None])
    low = same & (p[:, None] > p[None])
    ms = [strict, incl, low]

    def level(l):
        n = 1 << l
        t, u = p[:, None], p[None]
        return (t // (2 * n) == u // (2 * n)) & (t // n % 2 == 1) & (u // n % 2 == 0)
    ms += [level(0), level(0).T] + [level(l) for l in range(1, 6)]
    m2 = np.concatenate([m.astype(np.float32) for m in ms], axis=1)
    rb = f["rel_bias_2"][0]
    kq = np.arange(640)
    dd = p[:, None] + 512 - kq[None]
    idx = np.clip(np.clip(dd, -63, 128) + 63, 0, 191)
    band = np.ascontiguousarray(rb[:, idx].transpose(1, 0, 2).reshape(128, 8 * 640))
    hi = (p[:, None] >= 64)
    bad = (hi & (kq[None] < 64)) | (~hi & (kq[None] >= 576))
    bmask = np.where(bad, -1e30, 0.0).astype(np.float32)
    perm = np.concatenate([np.arange(64) + 64 * h for h in [4 * a + j for j in range(4) for a in range(2)]])
    w_in = f["w_in"][0].copy()
    w_in[:, :512] = f["w_in"][0][:, perm]
    w_out = f["w_out"][0].copy()
    w_out[:512] = f["w_out"][0][perm]
    return {
        "xT": f["x"][0].T, "memT": f["mem"][0].T, "cols": s, "rows": rows, "cst": cst, "alibi": alibi,
        "reset128": r128, "reset64": r64, "m2": m2, "band": band, "bmask": bmask,
        "w_in": w_in, "w_out": w_out, "wq": f["wq_x"][0], "wkv": f["wkv_x"][0], "wo": f["wo_x"][0],
        "w_up": f["w_up"][0], "w_down": f["w_down"][0], "w_ada": f["w_ada_2"][0], "w_in2": f["w_in_2"][0],
        "w_out2": f["w_out_2"][0], "lora": np.concatenate([f["w2_2"][0], f["a2_2"][0]], axis=0),
    }


def kernel(**inputs):
    import numpy as _np
    import concourse.bacc as _bacc
    from concourse import mybir as _mybir
    from concourse.bass_utils import run_bass_kernel_spmd as _run

    nc = _bacc.Bacc("TRN2", target_bir_lowering=False, num_devices=1)
    arrays, d = {}, {}
    for name, a in host_layout(inputs).items():
        a = _np.ascontiguousarray(a)
        arrays[f"in_{name}"] = a
        d[name] = nc.dram_tensor(f"in_{name}", a.shape, _mybir.dt.from_np(a.dtype), kind="ExternalInput").ap()
    d["out"] = nc.dram_tensor("out", (1024, 1024), F32, kind="ExternalOutput").ap()
    build(nc, d)
    r = _run(nc, [arrays], core_ids=[0])
    return _np.ascontiguousarray(r.results[0]["out"].T)[None]
```

```python
import concourse.bass as bass
from concourse import mybir
from contextlib import ExitStack

F32 = mybir.dt.float32
F32R = mybir.dt.float32r
TOTAL = 52700
ALU = mybir.AluOpType
ACT = mybir.ActivationFunctionType
AX = mybir.AxisListType
MUL, ADD, SUB, MAX, MIN = ALU.mult, ALU.add, ALU.subtract, ALU.max, ALU.min
EH = 0.6065306597126334
NSLOT = 4
NSEM = 110
CUT = 2
DW = 3
NW = 0.4
DM = 2
NM = 1
NB = 0.7
NQ = 1
NR = 0.7
DB = 3

COLS = {}
ROWS = {}
CST = {}


def _lay(table, names):
    at = 0
    for n, w in names:
        table[n] = (at, w)
        at += w
    return at


NCOLS = _lay(COLS, [("g_mix", 8), ("g_x", 8), ("g_mem", 8), ("g_ffn", 8), ("g_fin", 8), ("g_n2", 8), ("c", 8),
                    ("b_ada", 24), ("convw", 32), ("convb", 8), ("fw", 66), ("fb", 22), ("mu", 17), ("w0", 4),
                    ("a0", 4), ("kk", 4), ("ka", 4), ("rk", 4), ("qng", 1), ("kng", 1)])
NROWS = _lay(ROWS, [("bg", 8), ("sinks", 8), ("lng", 512), ("lnb", 512)])
NCST = _lay(CST, [("I", 128), ("ones", 128), ("bo", 2), ("mst", 128), ("selh", 512), ("selp", 512)])
NSMALL = 800 + -(NCOLS + NROWS + NCST) % 16
X0 = NCOLS + NROWS + NCST + 32 + NSMALL
PIECES = [X0, 8192, 2048 * NSLOT, 16384, (TOTAL - X0 - 32768) // 16 * 16]


class Queue:

    def __init__(self, sem, eng):
        self.sem, self.n, self.eng, self.seen = sem, 0, eng, {}

    def issue(self, fn, sem, by, waits):
        if self.eng is None:
            return
        for s, v in flat(waits):
            if self.seen.get(id(s), 0) < v:
                self.seen[id(s)] = v
                self.eng.wait_ge(s, v)
        ins = fn(self.eng)
        if sem is not None:
            ins.then_inc(sem, by)

    def __call__(self, fn, *waits, inc=True):
        self.issue(fn, self.sem if inc else None, 1, waits)
        if inc:
            self.n += 1
        return (self.sem, self.n)

    def dma(self, fn, sem, value, *waits):
        self.issue(fn, sem, 16, waits)
        return (sem, value)


def flat(x):
    if x is None:
        return []
    if isinstance(x, dict):
        x = list(x.values())
    if isinstance(x, tuple) and len(x) == 2 and isinstance(x[1], int):
        return [x]
    return [t for y in x for t in flat(y)]


class Places:

    def __init__(self, items):
        self.free = [(i, []) for i in items]

    def take(self):
        return self.free.pop(0)

    def give(self, item, *toks):
        self.free.append((item, flat(toks)))


def staggered(units, depth):
    units, live = list(units), []
    while units or live:
        if units and len(live) < depth:
            live.append(units.pop(0))
        for u in list(live):
            try:
                next(u)
            except StopIteration:
                live.remove(u)
        yield


def run(gen):
    for _ in gen:
        pass


def build(nc, d):
    with ExitStack() as ctx:
        SB, SR = [], []
        for i, n in enumerate(PIECES):
            with nc.sbuf_tensor(f"SB{i}", [128, n], F32) as t:
                SB.append(t)
            SR.append(ctx.enter_context(nc.sbuf_tensor(f"SR{i}", [128, n], F32R)))
        PS = ctx.enter_context(nc.psum_tensor("PS", [128, 4096], F32))
        sems = [ctx.enter_context(nc.semaphore(f"s{i}")) for i in range(NSEM)]
        spill = nc.dram_tensor("spill", (1024, 1024), F32, kind="Internal").ap()
        block = ctx.enter_context(nc.Block())

        plan = []
        walk(SB, SR, PS, sems, spill, d, None, None, plan, True)

        @block.tensor
        def _(eng):
            walk(SB, SR, PS, sems, spill, d, 0, eng, plan, False)

        @block.vector
        def _(eng):
            walk(SB, SR, PS, sems, spill, d, 1, eng, plan, False)

        @block.scalar
        def _(eng):
            walk(SB, SR, PS, sems, spill, d, 2, eng, plan, False)

        @block.gpsimd
        def _(eng):
            walk(SB, SR, PS, sems, spill, d, 3, eng, plan, False)

        @block.sync
        def _(eng):
            walk(SB, SR, PS, sems, spill, d, 4, eng, plan, False)


def walk(SB, SR, PS, sems, spill, d, me, engine, plan, recording):
    nsem = [0]

    def sem():
        nsem[0] += 1
        return sems[nsem[0] - 1]

    pe, dve, act, pool, sp = (Queue(sem(), engine if i == me else None) for i in range(5))
    at = [0]

    def region(n):
        a = at[0]
        at[0] += n
        return SB[0][:, a:a + n]

    def v3(ap, k):
        return ap.rearrange("p (k n) -> p k n", k=k)

    def once(q, out, in_, *waits):
        return q.dma(lambda e: e.dma_start(out, in_), sem(), 16, *waits)

    cols, rows, cst = region(NCOLS), region(NROWS), region(NCST)
    t_cst = once(act, cst, d["cst"])
    t_col = once(act, cols, d["cols"])
    t_row = once(act, rows, d["rows"])

    def col(name, i=0):
        return cols[:, COLS[name][0] + i:COLS[name][0] + i + 1]

    def row(name, a=0, b=None):
        o, w = ROWS[name]
        return rows[:, o + a:o + (w if b is None else b)]

    def cs(name, a=0, b=None):
        o, w = CST[name]
        return cst[:, o + a:o + (w if b is None else b)]

    I = cs("I")
    mod = region(24)
    gs2 = region(8)
    small = region(NSMALL)
    assert at[0] == X0
    G0 = X0 + 8192
    W0 = G0 + NSLOT * 2048
    WN = sum(PIECES[3:])
    XTr = SB[1][:, :]
    XT = v3(XTr, 8)

    def seen(views, a, n):
        i, o = 0, a
        while o >= PIECES[i]:
            o -= PIECES[i]
            i += 1
        assert o + n <= PIECES[i]
        return views[i][:, o:o + n]

    def f32(a, n):
        return seen(SB, a, n)

    def f32r(a, n):
        return seen(SR, a, n)

    def work(a, n):
        return f32(W0 + a, n)

    class Parts:

        def __init__(self, a, b, K=8, N=512, step=None):
            step = step or N
            self.hi = [f32r(a + k * step, N) for k in range(K)]
            self.lo = [f32r(b + k * step, N) for k in range(K)]
            self.fhi = [f32(a + k * step, N) for k in range(K)]
            self.flo = [f32(b + k * step, N) for k in range(K)]

    banks2 = Places([0, 1])
    banks1 = Places([4, 5, 6, 7])

    def pair(b):
        return PS[:, 1024 * b:1024 * b + 1024]

    def bank(b):
        return PS[:, 512 * b:512 * b + 512]

    slots = Places(list(range(NSLOT)))
    slot_sem = [sem() for _ in range(NSLOT)]
    slot_n = [0] * NSLOT

    def slot(i):
        return f32(G0 + 2048 * i, 2048)

    def split(src, hi, lo, tok, *free):
        th = act(lambda e: e.activation(hi, src, ACT.Copy), tok, free)
        tl = dve(lambda e: e.tensor_tensor(lo, src, hi.bitcast(F32), SUB), th, tok, free)
        return [th, tl]

    asked = [0]
    fetched, divided = [], []

    def fetch(w, k0, kn, c0, cn, parts):
        i, free = slots.take()
        slot_n[i] += 16
        view = f32(G0 + 2048 * i, kn * cn).rearrange("p (k n) -> p k n", k=kn)
        src = w[k0 * 128:(k0 + kn) * 128, c0:c0 + cn].rearrange("(k p) n -> p k n", p=128)
        return i, view, sp.dma(lambda e: e.dma_start(view, src), slot_sem[i], slot_n[i], free)

    def divide(i, view, t, kn, cn, parts):
        if not parts:
            return i, view, None, t
        a, n = G0 + 2048 * i, kn * cn
        t = split(f32(a, n), f32r(a + 1024, n), f32r(a, n), t)
        shape = lambda v: v.rearrange("p (k n) -> p k n", k=kn)
        return i, shape(f32r(a + 1024, n)), shape(f32r(a, n)), t

    def lend_ring():
        if recording:
            plan.append(None)
        fetched.append(None)
        divided.append(None)
        asked[0] += 1
        return [slots.take() for _ in range(NSLOT)]

    def slab(w, k0, kn, c0, cn, parts=True):
        if recording:
            plan.append((w, k0, kn, c0, cn, parts))
        at_ = asked[0]
        asked[0] += 1

        def ahead(done, by, f):
            while len(done) < min(at_ + by + 1, len(plan)) and plan[len(done)] is not None:
                done.append(f(len(done)))
        ahead(fetched, 3, lambda q: fetch(*plan[q]))
        ahead(divided, 2, lambda q: divide(*fetched[q], plan[q][2], plan[q][4], plan[q][5]))
        return divided[at_]

    def gemmT(w, c0, ntile, src, stok, evac, N=512, K=8, cut=8):
        for m in range(ntile):
            b, free = banks1.take()
            out = bank(b)[:, 0:N]
            for k0 in range(0, K, 8):
                kn = min(8, K - k0)
                i, whi, wlo, t = slab(w, k0, kn, c0 + m * 128, 128)
                for k in range(k0, k0 + kn):
                    hi, lo = src.hi[k], src.lo[k]
                    pe(lambda e: e.matmul(out, whi[:, k - k0, :], hi, start=(k == 0), stop=False),
                       t, stok[k], free, inc=False)
                    pe(lambda e: e.matmul(out, whi[:, k - k0, :], lo, start=False, stop=False), inc=False)
                    tk = pe(lambda e: e.matmul(out, wlo[:, k - k0, :], hi, start=False, stop=(k == K - 1)),
                            inc=(k == k0 + kn - 1))
                    if (k + 1) % cut == 0 and k < K - 1 and k < k0 + kn - 1:
                        yield
                slots.give(i, tk)
            banks1.give(b, evac(m, out, tk))
            yield

    def gemmN(w, c0, cn, src, stok, evac, T=4):
        kn = min(8, 1024 // cn)
        bs = [banks1.take() for _ in range(T)]
        for k0 in range(0, 8, kn):
            i, whi, wlo, t = slab(w, k0, kn, c0, cn)
            for tt in range(T):
                b, free = bs[tt]
                out = bank(b)[:, 0:cn]
                sl = slice(tt * 128, (tt + 1) * 128)
                for k in range(k0, k0 + kn):
                    hi, lo = src.hi[k][:, sl], src.lo[k][:, sl]
                    pe(lambda e: e.matmul(out, hi, whi[:, k - k0, :], start=(k == 0), stop=False),
                       t, stok[k], free, inc=False)
                    pe(lambda e: e.matmul(out, hi, wlo[:, k - k0, :], start=False, stop=False), inc=False)
                    tk = pe(lambda e: e.matmul(out, lo, whi[:, k - k0, :], start=False, stop=(k == 7)),
                            inc=(k == k0 + kn - 1))
                bs[tt] = (b, free) if k0 + kn < 8 else (b, tk)
            slots.give(i, tk)
        for tt in range(T):
            b, tk = bs[tt]
            banks1.give(b, evac(tt, bank(b)[:, 0:cn], tk))
        yield

    def transpose(out, in_, *waits, inc=True):
        p = in_.shape[0]
        idn = I[0:p, 0:p]
        return pe(lambda e: e.transpose(out, in_, idn), *waits, inc=inc)

    rms_st = [0]

    def rms(src, stok, T, gcol, out, toks, sq, free, extra=None, bias=None, f32out=None):
        nt = T // 128
        ts = [act(lambda e: e.activation(sq[k], src[k], ACT.Square), stok[k], free) for k in range(8)]
        yield
        b, bfree = banks1.take()
        for tt in range(nt):
            for k in range(8):
                tk = pe(lambda e: e.matmul(bank(b)[:, tt:tt + 1], sq[k][:, tt * 128:(tt + 1) * 128],
                                           cs("ones", 0, 1), start=(k == 0), stop=(k == 7)),
                        ts[k], bfree, t_cst, inc=(k == 7))
        rms_st[0] = (rms_st[0] + 1) % 2
        st = small[:, 8 * rms_st[0]:8 * rms_st[0] + nt]
        t = dve(lambda e: e.tensor_scalar(st, bank(b)[:, 0:nt], 1.0 / 1024, 1e-6, MUL, ADD), tk)
        banks1.give(b, t)
        t = act(lambda e: e.activation(st, st, ACT.Sqrt), t)
        t = dve(lambda e: e.reciprocal(st, st), t)
        for tt in range(nt):
            t1 = dve(lambda e: e.tensor_scalar(sq[0][:, tt * 128:(tt + 1) * 128], I, st[:, tt:tt + 1], None, MUL),
                     t, tk)
        yield
        b, bfree = banks1.take()
        tb = pe(lambda e: e.matmul(bank(b)[:, 0:T], cs("ones"), sq[0], start=True, stop=True), t1, bfree)
        for k in range(8):
            o = f32out[k] if f32out else out.flo[k]
            t = dve(lambda e: e.scalar_tensor_tensor(out=o, in0=src[k], scalar=gcol(k), in1=bank(b)[:, 0:T],
                                                     op0=MUL, op1=MUL), tb, t_col, extra, free)
            last = t
            if bias is not None:
                t = act(lambda e: e.activation(o, o, ACT.Identity, bias=bias(k)), t)
            toks[k] = t if f32out else split(o, out.hi[k], out.lo[k], t, tb)
        banks1.give(b, last)

    def together(main, side, n=1):
        run(weave(main, side, n))

    def weave(main, side, n=1):
        live, due = True, 0
        for _ in main:
            due += n
            while due >= 1:
                due -= 1
                if live:
                    live = next(side, "end") != "end"
            yield
        if live:
            yield from side

    def chain(*gens):
        for g in gens:
            yield from g

    def tiles(v):
        return [v[:, k, :] for k in range(v.shape[1])]

    def add_x(half, src_toks, new):
        def evac(m, ps, tk):
            o = XT[:, m, 512 * half:512 * half + 512]
            new[m] = dve(lambda e: e.tensor_tensor(o, ps, o, ADD), tk, src_toks[m])
            return new[m]
        return evac

    finals = []
    prior = []

    t_mod = []

    def ada():
        cact = small[:, 16:24]
        tc = act(lambda e: e.activation(cact, cols[:, COLS["c"][0]:COLS["c"][0] + 8], ACT.Silu), t_col)
        b, free = banks1.take()
        for m in range(24):
            i, view, _, t = slab(d["w_ada"], 0, 8, m * 128, 128, parts=False)
            for k in range(8):
                tk = pe(lambda e: e.matmul(bank(b)[:, m:m + 1], view[:, k, :], cact[:, k:k + 1], start=(k == 0),
                                           stop=(k == 7)), t, tc, free, inc=(k == 7))
            slots.give(i, tk)
            if m % 2:
                yield
        ba = cols[:, COLS["b_ada"][0]:COLS["b_ada"][0] + 24]
        t = dve(lambda e: e.tensor_tensor(mod, bank(b)[:, 0:24], ba, ADD), tk, t_col)
        banks1.give(b, t)
        g2 = cols[:, COLS["g_n2"][0]:COLS["g_n2"][0] + 8]
        t2 = dve(lambda e: e.tensor_scalar(gs2, mod[:, 8:16], 1.0, None, ADD), t)
        t2 = dve(lambda e: e.tensor_tensor(gs2, gs2, g2, MUL), t2)
        t_mod.extend([t, t2])

    def softmax(S, tS, P, W, G, scale, bias, sinks, st, pfree, extra=None):
        mx, nm, sm, es = (st[:, k * G:(k + 1) * G] for k in range(4))
        if bias is not None:
            t = dve(lambda e: e.scalar_tensor_tensor(out=P, in0=S, scalar=scale, in1=bias, op0=MUL, op1=ADD),
                    tS, pfree, extra)
            tr = t
            src, sc, neg = P, 1.0, -1.0
        else:
            src, sc, neg, t, tr = S, scale, -scale, tS, None
        t = dve(lambda e: e.tensor_reduce(mx, src, AX.X, MAX), t, pfree)
        if sinks is not None:
            t = dve(lambda e: e.tensor_tensor(mx, mx, sinks, MAX), t, t_row)
        t = dve(lambda e: e.tensor_scalar(nm, mx, neg, None, MUL), t)
        if sinks is not None:
            te = dve(lambda e: e.tensor_tensor(es, nm, sinks, ADD), t)
            te = act(lambda e: e.activation(es, es, ACT.Exp), te)
        for g in range(G):
            tx = act(lambda e, g=g: e.activation(P[:, g, :], src[:, g, :], ACT.Exp, bias=nm[:, g:g + 1], scale=sc,
                                                 accum_out=sm[:, g:g + 1]), t)
        ts = tx
        if sinks is not None:
            tx = dve(lambda e: e.tensor_tensor(sm, sm, es, ADD), tx, te)
        tx = dve(lambda e: e.reciprocal(sm, sm), tx)
        for g in range(G):
            tp = dve(lambda e, g=g: e.tensor_scalar(P[:, g, :], P[:, g, :], sm[:, g:g + 1], None, MUL), tx)
        return tp, (tr if bias is not None else ts)

    xh = [[f32(X0 + 4096 * h + 512 * k, 512) for k in range(8)] for h in range(2)]
    tXh = [once(sp, v3(f32(X0 + 4096 * h, 4096), 8),
                d["xT"][:, 512 * h:512 * h + 512].rearrange("(k p) n -> p k n", p=128)) for h in range(2)]
    HA = Parts(W0 + 4096, W0)
    HX = Parts(X0, X0 + 4096)
    tH0, tH1 = {}, {}
    g_mix = lambda k: col("g_mix", k)
    run(rms(xh[0], [tXh[0]] * 8, 512, g_mix, HA, tH0, HA.fhi, None))
    free0 = [(dve.sem, dve.n)]

    aqT, akT = v3(work(8192, 4096), 4), work(12288, 1024)
    avt = v3(work(13312, 1024), 8)
    mqk = [work(14336 + 1024 * m, 1024) for m in range(8)]
    mva = work(22528, 4128).rearrange("p (t h e) -> p t h e", t=8, h=4)
    mo = v3(work(26656, 4096), 4)
    pads = [work(30752, 516), work(31268, 516)]
    gt = v3(small[:, 32:96], 8)
    tail = small[:, 704:776]
    pad_free = [[], []]
    T = {}

    t_ones = pool(lambda e: e.memset(mva[:, :, :, 128:129], 1.0))

    def ev_gate(half):
        def f(tt, ps, tk):
            q = 4 * half + tt
            T["gt", q] = dve(lambda e: e.tensor_tensor(gt[:, q, :], ps, row("bg"), ADD), tk, t_row)
            return T["gt", q]
        return f

    def ev_av(half):
        def f(tt, ps, tk):
            q = 4 * half + tt
            T["av", q] = act(lambda e: e.activation(avt[:, q, :], ps, ACT.Copy), tk)
            return T["av", q]
        return f

    def ev_mv(half):
        def f(tt, ps, tk):
            q = 4 * half + tt
            T["mv", q] = act(lambda e: e.activation(mva[:, q, :, 0:128], ps.rearrange("p (h e) -> p h e", h=4),
                                                    ACT.Copy), tk)
            return T["mv", q]
        return f

    def ev_to(name, dst, half, func=ACT.Copy, wait=None, scale=1.0):
        def f(m, ps, tk):
            T[name, m, half] = act(lambda e: e.activation(dst[m][:, 512 * half:512 * half + 512], ps, func,
                                                          scale=scale), tk, wait)
            return T[name, m, half]
        return f

    def ev_swish(name, dst, half, wait):
        def f(m, ps, tk):
            o = dst[m][:, 512 * half:512 * half + 512]
            t = act(lambda e: e.activation(o, ps, ACT.Tanh, scale=0.5), tk, wait)
            T[name, m, half] = dve(lambda e: e.scalar_tensor_tensor(out=o, in0=o, scalar=1.0, in1=ps, op0=ADD,
                                                                    op1=MUL), t)
            return T[name, m, half]
        return f

    cnt = [0]

    def conv_evac(half, name, K, w, b, dst, tl, pf, finish, wait=None, base=0):
        K1 = K - 1

        def f(m, ps, tk):
            q = base + m
            i = cnt[0] % 2
            cnt[0] += 1
            pad, o, tq = pads[i], dst(m), tl[:, K1 * q:K1 * q + K1]
            if half:
                tz = dve(lambda e: e.tensor_copy(pad[:, 0:K1], tq), T[name + "tail", q], pf[i])
            else:
                tz = dve(lambda e: e.memset(pad[:, 0:K1], 0.0), pf[i])
            te = act(lambda e: e.activation(pad[:, K1:K1 + 512], ps, ACT.Copy), tk, pf[i])
            t = te
            if not half:
                T[name + "tail", q] = t2 = dve(lambda e: e.tensor_copy(tq, pad[:, 512:512 + K1]), te)
            t = dve(lambda e: e.tensor_scalar(o, pad[:, 0:512], w(q, 0), b(q), MUL, ADD), te, tz, t_col, wait)
            for j in range(1, K):
                t = dve(lambda e: e.scalar_tensor_tensor(out=o, in0=pad[:, j:j + 512], scalar=w(q, j), in1=o,
                                                         op0=MUL, op1=ADD), t)
            pf[i] = [t] if half else [t, t2]
            finish(m, o, t)
            return te
        return f

    def ev_mqk(half):
        def finish(m, o, t):
            tmp = work(31784, 512)
            t = act(lambda e: e.activation(tmp, o, ACT.Tanh, scale=0.5), t, T.get("tmp"))
            T["mqk", m, half] = dve(lambda e: e.scalar_tensor_tensor(out=o, in0=tmp, scalar=1.0, in1=o, op0=ADD,
                                                                     op1=MUL), t)
            T["tmp"] = T["mqk", m, half]
        return conv_evac(half, "mqk", 4, lambda q, j: col("convw", q * 4 + j), lambda q: col("convb", q),
                         lambda m: mqk[m][:, 512 * half:512 * half + 512], tail, pad_free, finish)

    w_in = d["w_in"]

    def proj_a(half, src, tok):
        yield from gemmT(w_in, 0, 4, src, tok, ev_to("aq", tiles(aqT), half))
        yield from gemmT(w_in, 512, 1, src, tok, ev_to("ak", [akT], half))
        yield from gemmN(w_in, 640, 128, src, tok, ev_av(half))

    def proj_m(half, src, tok):
        yield from gemmN(w_in, 2816, 8, src, tok, ev_gate(half))
        yield from gemmT(w_in, 768, 8, src, tok, ev_mqk(half), cut=CUT)
        yield from gemmN(w_in, 1792, 512, src, tok, ev_mv(half))
        yield from gemmT(w_in, 2304, 4, src, tok, ev_to("mo", tiles(mo), half, ACT.Tanh, scale=0.5),
                         cut=CUT)

    together(chain(proj_a(0, HA, tH0), proj_m(0, HA, tH0)),
             rms(xh[1], [tXh[1]] * 8, 512, g_mix, HX, tH1, HX.fhi, free0), 0.5)
    ha_free = [(pe.sem, pe.n)]
    run(proj_a(1, HX, tH1))

    alib = work(0, 2048)
    t_alib = once(sp, alib, d["alibi"], ha_free)
    Pb, PTb = Places([]), Places([])
    Pb.free = [(0, ha_free), (1, ha_free)]
    PTb.free = [(0, ha_free), (1, ha_free)]
    Pv = [work(2048, 1024), work(3072, 1024)]
    PTv = [work(4096, 1024), work(5120, 1024)]
    mixM = mqk[0:4]
    mix_tok = {}
    stn = [0]

    def stat():
        stn[0] = (stn[0] + 1) % 4
        return small[:, 128 + 32 * stn[0]:160 + 32 * stn[0]]

    def window(n, jp):
        W = 128 if n == 0 else 256
        k0 = 0 if n == 0 else (n - 1) * 128
        nk = W // 128
        b, free = banks2.take()
        S = pair(b).rearrange("p (g w) -> p g w", g=4)
        for a in range(2):
            for jj in range(2):
                j = 2 * jp + jj
                tS = pe(lambda e, a=a, jj=jj, j=j: e.matmul(
                    S[:, 2 * a + jj, 0:W], aqT[64 * a:64 * a + 64, j, n * 128:(n + 1) * 128],
                    akT[64 * a:64 * a + 64, k0:k0 + W], start=True, stop=True),
                    T["aq", j, n // 4], T["ak", 0, 0], T["ak", 0, n // 4], free, inc=(a == 1 and jj == 1))
        p, pfree = Pb.take()
        P = Pv[p].rearrange("p (g w) -> p g w", g=4)
        bias = alib[:, 1024 * jp:1024 * jp + 1024].rearrange("p (g w) -> p g w", g=4)[:, :, 256 - W:256]
        tP, tr = softmax(S[:, :, 0:W], tS, P[:, :, 0:W], W, 4, 0.125, bias, row("sinks", 4 * jp, 4 * jp + 4),
                         stat(), pfree, t_alib)
        banks2.give(b, tr)
        yield
        b, free = banks2.take()
        for g in range(4):
            for kt in range(nk):
                tt = transpose(pair(b)[:, (g * nk + kt) * 128:(g * nk + kt + 1) * 128],
                               P[:, g, kt * 128:(kt + 1) * 128], tP, free, t_cst,
                               inc=(g == 3 and kt == nk - 1))
        Pb.give(p, tt)
        q, qfree = PTb.take()
        PT = PTv[q]
        hw = 256 * nk
        if nk == 1:
            t1 = t2 = act(lambda e: e.activation(PT[:, 0:512], pair(b)[:, 0:512], ACT.Copy), tt, qfree)
        else:
            t1 = act(lambda e: e.activation(PT[:, 0:hw], pair(b)[:, 0:hw], ACT.Copy), tt, qfree)
            t2 = dve(lambda e: e.tensor_copy(PT[:, hw:2 * hw], pair(b)[:, hw:2 * hw]), tt, qfree)
        banks2.give(b, t1, t2)
        yield
        b, free = banks1.take()
        for a in range(2):
            for jj in range(2):
                for kt in range(nk):
                    g = 2 * a + jj
                    tile = k0 // 128 + kt
                    to = pe(lambda e, a=a, jj=jj, kt=kt, g=g, tile=tile: e.matmul(
                        bank(b)[64 * a:64 * a + 64, jj * 128:(jj + 1) * 128],
                        avt[:, tile, 64 * a:64 * a + 64],
                        PT[:, (g * nk + kt) * 128:(g * nk + kt + 1) * 128],
                        start=(kt == 0), stop=(kt == nk - 1)),
                        t1, t2, T["av", tile], free, inc=(g == 3 and kt == nk - 1))
        PTb.give(q, to)
        o = aqT[:, 2 * jp:2 * jp + 2, n * 128:(n + 1) * 128]
        t = act(lambda e: e.activation(o, bank(b)[:, 0:256].rearrange("p (j q) -> p j q", j=2), ACT.Copy), to)
        banks1.give(b, t)
        mix_tok["a", n, jp] = t

    attn = staggered([window(n, jp) for n in range(8) for jp in range(2)], DW)
    together(proj_m(1, HX, tH1), attn, NW)
    att_done = [mix_tok["a", n, jp] for jp in range(2) for n in range(8)] + [(pe.sem, pe.n)]

    R = [f32(X0 + 1024 * i, 1024)[0:4, :] for i in range(6)]
    rowfree = att_done
    iR, fR, bR, mR, c1, wi = R
    tg = []
    for q, dst in ((0, iR), (1, fR)):
        b, free = banks2.take()
        for tt in range(8):
            t = transpose(pair(b)[0:4, tt * 128:(tt + 1) * 128], gt[:, tt, 4 * q:4 * q + 4], T["gt", tt], free,
                          t_cst, inc=(tt == 7))
        t = dve(lambda e, dst=dst, b=b: e.tensor_copy(dst, pair(b)[0:4, :]), t, rowfree)
        banks2.give(b, t)
        tg.append(t)
    em = wi
    t = act(lambda e: e.activation(c1, fR, ACT.Abs), tg)
    t = act(lambda e: e.activation(c1, c1, ACT.Exp, scale=-1.0), t)
    t = act(lambda e: e.activation(c1, c1, ACT.Ln, bias=1.0), t)
    t = dve(lambda e: e.scalar_tensor_tensor(out=fR, in0=fR, scalar=0.0, in1=c1, op0=MIN, op1=SUB), t)
    t_rs = once(sp, wi, d["reset128"], rowfree)
    tb = dve(lambda e: e.tensor_tensor_scan(bR, wi, fR, 0.0, MUL, ADD), t, t_rs)
    tm = dve(lambda e: e.tensor_tensor_scan(mR, fR, iR, 0.0, ADD, MAX), tb)
    M9 = small[0:4, 256:265]
    c8 = lambda v: v.rearrange("p (c t) -> p c t", c=8)
    t0 = dve(lambda e: e.memset(M9[:, 0:1], 0.0))
    t1 = dve(lambda e: e.tensor_copy(M9[:, 1:9], c8(mR)[:, :, 127]), tm, t0)
    tc1 = dve(lambda e: e.tensor_tensor(c1, iR, bR, SUB), tb, tm)
    tR1 = dve(lambda e: e.tensor_tensor(bR, bR, mR, SUB), tc1)
    R1 = bR
    t_em = act(lambda e: e.activation(fR, mR, ACT.Exp, scale=-1.0), tm)
    twi = dve(lambda e: e.tensor_tensor(c8(wi), c8(R1), M9[:, 0:8].unsqueeze(2).to_broadcast([4, 8, 128]), ADD),
              tR1, t1)
    twi = act(lambda e: e.activation(wi, wi, ACT.Exp), twi)
    tws = dve(lambda e: e.tensor_tensor(c8(iR), c8(c1), c8(R1)[:, :, 127:128].to_broadcast([4, 8, 128]), ADD), tR1)
    tws = act(lambda e: e.activation(iR, iR, ACT.Exp), tws)
    mc = small[:, 288:384].rearrange("p (q t h) -> p q t h", q=3, t=8)
    b, free = banks1.take()
    for q, (src, tk) in enumerate(((c1, tc1), (iR, tws), (fR, t_em))):
        for tt in range(8):
            o = bank(b)[:, q * 32 + tt * 4:q * 32 + tt * 4 + 4]
            t = transpose(o, src[:, tt * 128:(tt + 1) * 128], tk, free, inc=(q == 2 and tt == 7))
    tmc = dve(lambda e: e.tensor_copy(small[:, 288:384], bank(b)[:, 0:96]), t)
    banks1.give(b, tmc)
    dec = small[:, 384:416]

    XA = [akT, work(13312, 1024)]
    XB, XC = Pv, PTv
    Cb = [v3(work(31784, 516), 4), v3(work(6144, 516), 4)]
    hbuf = [work(0, 1024), work(1024, 1024)]
    h_free = att_done
    hfree = [[], []]
    SC = 0.25 * 128.0 ** -0.5
    pe_att = (pe.sem, pe.n)
    xfree = [[pe_att], [pe_att]]

    def mlstm(h):
        u = h % 2
        E, kt, qt = XA[u], XB[u], XC[u]
        qT, kT = mqk[h], mqk[4 + h]
        hn = hbuf[u]
        wfree = [xfree[u], att_done]
        sel = cs("selh", 128 * h, 128 * h + 128)[0:4, :]
        b, free = banks2.take()
        for n in range(2):
            tk = pe(lambda e, n=n: e.matmul(pair(b)[:, 512 * n:512 * n + 512], sel, R1[:, 512 * n:512 * n + 512],
                                            start=True, stop=True), tR1, free, inc=(n == 1))
        for c in range(8):
            t = dve(lambda e, c=c: e.scalar_tensor_tensor(
                out=E[:, c * 128:(c + 1) * 128], in0=pair(b)[:, c * 128:(c + 1) * 128],
                scalar=mc[:, 0, c, h:h + 1], in1=cs("mst"), op0=ADD, op1=ADD), tk, tmc, wfree)
        banks2.give(b, t)
        tE = act(lambda e: e.activation(E, E, ACT.Exp), t)
        b, free = banks2.take()
        for n in range(2):
            tk = pe(lambda e, n=n, b=b: e.matmul(pair(b)[:, 512 * n:512 * n + 512], sel,
                                                 wi[:, 512 * n:512 * n + 512], start=True, stop=True),
                    twi, free, inc=(n == 1))
        tq = dve(lambda e, b=b: e.scalar_tensor_tensor(out=qt, in0=qT, scalar=SC, in1=pair(b), op0=MUL, op1=MUL),
                 tk, T["mqk", h, 0], T["mqk", h, 1], wfree)
        td = dve(lambda e, b=b: e.tensor_copy(dec[:, 8 * h:8 * h + 8], c8(pair(b))[:, :, 127]), tk)
        banks2.give(b, tq, td)
        yield
        b, free = banks2.take()
        for c in range(8):
            sl = slice(c * 128, (c + 1) * 128)
            tk = pe(lambda e, sl=sl, b=b: e.matmul(pair(b)[:, sl], kT[:, sl], qT[:, sl], start=True, stop=True),
                    T["mqk", h, 0], T["mqk", h, 1], T["mqk", 4 + h, 0], T["mqk", 4 + h, 1], free, inc=(c == 7))
        tsc = dve(lambda e, b=b: e.scalar_tensor_tensor(out=E, in0=pair(b), scalar=SC, in1=E, op0=MUL, op1=MUL),
                  tk, tE)
        banks2.give(b, tsc)
        b, free = banks2.take()
        for c in range(8):
            sl = slice(c * 128, (c + 1) * 128)
            tk = transpose(pair(b)[:, sl], kT[:, sl], free, inc=(c == 7))
        for c in range(8):
            sl = slice(c * 128, (c + 1) * 128)
            tkt = act(lambda e, sl=sl, c=c, b=b: e.activation(kt[:, sl], pair(b)[:, sl], ACT.Copy,
                                                              scale=mc[:, 1, c, h:h + 1]), tk, tmc, wfree)
        banks2.give(b, tkt)
        yield
        tC = None
        vt = [T["mv", tt] for tt in range(8)]
        th = []
        for c in range(8):
            sl = slice(c * 128, (c + 1) * 128)
            va = mva[:, c, h, :]
            Cold, Cnew = Cb[u][:, (c + 3) % 4, :], Cb[u][:, c % 4, :]
            b, free = banks1.take()
            num = bank(b)[:, 0:129]
            tn = pe(lambda e, num=num, sl=sl, va=va, c=c: e.matmul(num, E[:, sl], va, start=True, stop=(c == 0)),
                    tsc, vt, t_ones, free, inc=(c == 0))
            if c:
                tn = pe(lambda e, num=num, sl=sl, Cold=Cold: e.matmul(num, qt[:, sl], Cold, start=False,
                                                                      stop=True), tq, tC)
            if c < 7:
                b2, free = banks1.take()
                kv = bank(b2)[:, 0:129]
                tk = pe(lambda e, kv=kv, sl=sl, va=va: e.matmul(kv, kt[:, sl], va, start=True, stop=True),
                        tkt, free)
                if c == 0:
                    tC2 = dve(lambda e, kv=kv, Cnew=Cnew: e.tensor_copy(Cnew, kv), tk, h_free, xfree[u], t_alib)
                else:
                    tC2 = dve(lambda e, kv=kv, Cnew=Cnew, Cold=Cold, c=c: e.scalar_tensor_tensor(
                        out=Cnew, in0=Cold, scalar=dec[:, 8 * h + c:8 * h + c + 1], in1=kv, op0=MUL, op1=ADD),
                        tk, tC, td, tn)
                banks1.give(b2, tC2)
                tC = tC2
            dn = small[:, 416 + 8 * h + c:417 + 8 * h + c]
            t = act(lambda e: e.activation(dn, num[:, 128:129], ACT.Abs), tn)
            t = dve(lambda e: e.tensor_tensor(dn, dn, mc[:, 2, c, h:h + 1], MAX), t)
            t = dve(lambda e, dn=dn: e.reciprocal(dn, dn), t)
            t = dve(lambda e, num=num, dn=dn, sl=sl: e.tensor_scalar(hn[:, sl], num[:, 0:128], dn, 0.5, MUL, MUL),
                    t, h_free, hfree[u])
            banks1.give(b, t)
            th.append(t)
            if c % 2:
                yield
        b, free = banks2.take()
        for c in range(8):
            sl = slice(c * 128, (c + 1) * 128)
            tk = transpose(pair(b)[:, sl], hn[:, sl], th[c], free, inc=(c == 7))
        hfree[u] = [tk]
        xfree[u] = [tk, pe_att]
        t = dve(lambda e, b=b: e.scalar_tensor_tensor(out=mixM[h], in0=mo[:, h, :], scalar=1.0, in1=pair(b),
                                                      op0=ADD, op1=MUL), tk, T["mo", h, 0], T["mo", h, 1], h_free)
        banks2.give(b, t)
        mix_tok["m", h] = t

    together(staggered([mlstm(h) for h in range(4)], DM), ada(), NM)
    ml_done = [mix_tok["m", h] for h in range(4)] + [(pe.sem, pe.n), (dve.sem, dve.n), (act.sem, act.n)]
    tX = [once(sp, XT[:, k, :], d["xT"][k * 128:(k + 1) * 128, :], ml_done) for k in range(8)]

    def two_parts(tl, toks, half, dst, out, free):
        for k, v in enumerate(tl):
            out[k] = split(v[:, 512 * half:512 * half + 512], dst.hi[k], dst.lo[k], toks[k], free)

    mixs = tiles(aqT) + mixM
    MX = [Parts(W0 + 18432, W0 + 18432 + 4096), Parts(W0, W0 + 4096)]
    tM = [{}, {}]
    for h in range(2):
        two_parts(mixs, [ml_done] * 8, h, MX[h], tM[h], ml_done)
    parts_done = [(act.sem, act.n), (dve.sem, dve.n)]
    tX2 = [{}, {}]
    run(gemmT(d["w_out"], 0, 8, MX[0], tM[0], add_x(0, tX, tX2[0])))
    xs = [[XT[:, k, 512 * h:512 * h + 512] for k in range(8)] for h in range(2)]
    HB = Parts(W0 + 8192, W0 + 8192 + 4096)
    HA = Parts(W0, W0 + 4096)
    memT = [work(28672 + 256 * k, 256) for k in range(8)]
    t_mem = once(sp, v3(work(28672, 2048), 8), d["memT"].rearrange("(k p) n -> p k n", p=128), ml_done)
    HM = Parts(W0 + 30720, W0 + 28672, N=256)
    tq, tm = [{}, {}], {}
    together(gemmT(d["w_out"], 0, 8, MX[1], tM[1], add_x(1, tX, tX2[1])),
             chain(rms(memT, [t_mem] * 8, 256, lambda k: col("g_mem", k), HM, tm, HM.fhi, ml_done),
                   rms(xs[0], tX2[0], 512, lambda k: col("g_x", k), HB, tq[0], HB.fhi, [ml_done, parts_done])))
    qx = v3(work(16384, 8192), 8)
    kx = v3(work(24576, 2048), 8)
    vx = v3(work(26624, 2048), 2)
    Pv2 = [work(28672, 1024), work(29696, 1024)]
    PTv2 = [work(30720, 1024), work(31744, 1024)]
    wfree = [(pe.sem, pe.n)]

    def ev_vx(c):
        def f(tt, ps, tk):
            T["vx", tt, c] = act(lambda e: e.activation(vx[:, tt, 512 * c:512 * c + 512], ps, ACT.Copy), tk,
                                 wfree)
            return T["vx", tt, c]
        return f

    def ev_kx(m, ps, tk):
        T["kx", m] = act(lambda e: e.activation(kx[:, m, :], ps, ACT.Copy), tk, wfree)
        return T["kx", m]

    def kv():
        yield from gemmT(d["wkv"], 0, 8, HM, tm, ev_kx, N=256)
        for c in range(2):
            yield from gemmN(d["wkv"], 1024 + 512 * c, 512, HM, tm, ev_vx(c), T=2)
    together(kv(), rms(xs[1], tX2[1], 512, lambda k: col("g_x", k), HA, tq[1], HA.fhi, wfree))
    kvdone = [(pe.sem, pe.n)]
    run(gemmT(d["wq"], 0, 8, HB, tq[0], ev_to("qx", tiles(qx), 0, wait=wfree)))
    q0done = [(pe.sem, pe.n)]
    Pb, PTb = Places([]), Places([])
    Pb.free = [(0, kvdone), (1, kvdone)]
    PTb.free = [(0, kvdone), (1, kvdone)]
    tO = [{}, {}]
    OP = [HB, HA]
    ofree = [q0done, None]

    def cross(n):
        b, free = banks2.take()
        S = pair(b).rearrange("p (g w) -> p g w", g=4)
        for h in range(4):
            for dd in range(2):
                tS = pe(lambda e, h=h, dd=dd: e.matmul(
                    S[:, h, :], qx[:, 2 * h + dd, n * 128:(n + 1) * 128], kx[:, 2 * h + dd, :],
                    start=(dd == 0), stop=(dd == 1)), T["qx", 2 * h + dd, n // 4], T["kx", 2 * h + dd], free,
                    inc=(dd == 1))
        p, pfree = Pb.take()
        P = Pv2[p].rearrange("p (g w) -> p g w", g=4)
        tP, tr = softmax(S, tS, P, 256, 4, 1.0 / 16, None, None, stat(), pfree)
        banks2.give(b, tr)
        yield
        b, free = banks2.take()
        for g in range(4):
            for kt in range(2):
                tt = transpose(pair(b)[:, (2 * g + kt) * 128:(2 * g + kt + 1) * 128],
                               P[:, g, kt * 128:(kt + 1) * 128], tP, free, inc=(g == 3 and kt == 1))
        Pb.give(p, tt)
        q, qfree = PTb.take()
        PT = PTv2[q]
        t1 = act(lambda e: e.activation(PT[:, 0:512], pair(b)[:, 0:512], ACT.Copy), tt, qfree)
        t2 = dve(lambda e: e.tensor_copy(PT[:, 512:1024], pair(b)[:, 512:1024]), tt, qfree)
        banks2.give(b, t1, t2)
        yield
        b, free = banks2.take()
        for h in range(4):
            for dd in range(2):
                for kt in range(2):
                    m = 2 * h + dd
                    to = pe(lambda e, h=h, kt=kt, m=m, b=b: e.matmul(
                        pair(b)[:, m * 128:(m + 1) * 128], vx[:, kt, m * 128:(m + 1) * 128],
                        PT[:, (2 * h + kt) * 128:(2 * h + kt + 1) * 128], start=(kt == 0), stop=(kt == 1)),
                        t1, t2, T["vx", kt, m // 4], free, inc=(kt == 1))
        PTb.give(q, to)
        half, c0 = n // 4, 128 * (n % 4)
        ob = W0 + (8192 if half == 0 else 0)
        hi = f32r(ob, 4096).rearrange("p (k n) -> p k n", k=8)[:, :, c0:c0 + 128]
        lo = f32r(ob + 4096, 4096).rearrange("p (k n) -> p k n", k=8)[:, :, c0:c0 + 128]
        pv = pair(b).rearrange("p (m q) -> p m q", m=8)
        th = act(lambda e: e.activation(hi, pv, ACT.Copy), to, ofree[half])
        t = dve(lambda e: e.tensor_tensor(lo, pv, hi.bitcast(F32), SUB), th)
        banks2.give(b, t)
        tO[half][n] = [th, t]
    together(gemmT(d["wq"], 0, 8, HA, tq[1], ev_to("qx", tiles(qx), 1)),
             staggered([cross(n) for n in range(4)], 2), 2)
    ofree[1] = [(pe.sem, pe.n)]
    ot = [[list(tO[h].values())] * 8 for h in range(2)]
    tX3 = [{}, {}]
    together(gemmT(d["wo"], 0, 8, HB, ot[0], add_x(0, tX2[0], tX3[0])),
             staggered([cross(n) for n in range(4, 8)], 2), 2)
    o0done = [(pe.sem, pe.n)]
    ot = [[list(tO[h].values())] * 8 for h in range(2)]
    tF = [{}, {}]
    together(gemmT(d["wo"], 0, 8, HA, ot[1], add_x(1, tX2[1], tX3[1])),
             rms(xs[0], tX3[0], 512, lambda k: col("g_ffn", k), HB, tF[0], HB.fhi, o0done))
    place = lambda m: W0 + (16384 + 1024 * m if m < 16 else 1024 * (m - 16))
    pads = [work(6144, 514), work(6658, 514)]
    wfree = [(pe.sem, pe.n)]
    pf = [wfree, wfree]

    class AP:
        hi = [f32r(place(m) + 512, 512) for m in range(22)]
        lo = [f32r(place(m), 512) for m in range(22)]
    afree = [wfree, None]
    tX4 = [{}, {}]
    tY, tH2 = [{}, {}], [{}, {}]
    H2 = [HB, HA]

    def ffn(half, tA):
        def finish(m, o, t):
            tA[m] = act(lambda e: e.activation(o, o, ACT.Silu), t)

        def ev_u(m):
            def f(_, ps, tk):
                g = f32(place(m), 512)
                t = dve(lambda e: e.tensor_tensor(g, ps, g, MUL), tk, tA[m])
                tA[m] = split(g, AP.hi[m], AP.lo[m], t, afree[half])
                return t
            return f
        gate = conv_evac(half, "ffn", 3, lambda q, j: col("fw", q * 3 + j), lambda q: col("fb", q),
                         lambda i: f32(place(cur[0]), 512), small[:, 704:748], pf, lambda i, o, t:
                         finish(cur[0], o, t), wait=afree[half])
        cur = [0]

        def gate_at(m):
            def f(_, ps, tk):
                cur[0] = m
                return gate_q(m, ps, tk)
            return f

        def gate_q(m, ps, tk):
            return gate(m, ps, tk)
        for m in range(23):
            if m < 22:
                yield from gemmT(d["w_up"], m * 128, 1, HB, tF[half], gate_at(m))
            if m:
                yield from gemmT(d["w_up"], 2816 + (m - 1) * 128, 1, HB, tF[half], ev_u(m - 1))

    tA = {}
    run(ffn(0, tA))
    hb_free = [(pe.sem, pe.n)]
    together(gemmT(d["w_down"], 0, 8, AP, tA, add_x(0, tX3[0], tX4[0]), K=22),
             rms(xs[1], tX3[1], 512, lambda k: col("g_ffn", k), HB, tF[1], HB.fhi, hb_free))
    afree[1] = [(pe.sem, pe.n)]
    tA = {}
    run(ffn(1, tA))
    hb_free = [(pe.sem, pe.n)]

    def last_norms(h, free):
        yield from rms(xs[h], tX4[h], 512, lambda k: col("g_fin", k), None, tY[h], H2[h].fhi, free,
                       f32out=xs[h])
        yield from rms(xs[h], tY[h], 512, lambda k: gs2[:, k:k + 1], H2[h], tH2[h], H2[h].fhi,
                       [free, (dve.sem, dve.n)], extra=t_mod, bias=lambda k: mod[:, k:k + 1])
    together(gemmT(d["w_down"], 0, 8, AP, tA, add_x(1, tX3[1], tX4[1]), K=22), last_norms(0, hb_free))
    done3 = [(pe.sem, pe.n)]
    run(last_norms(1, done3))
    spilled = spill.rearrange("(k p) n -> p k n", p=128)
    t_spill = [once(sp, spilled, XT, tY[0], tY[1]), (act.sem, act.n), (dve.sem, dve.n)]
    W2 = d["w_in2"]
    yaT = v3(work(16384, 4096), 4)
    av = v3(work(23552, 4096), 8)
    atts = [[work(20480 + 1024 * i, 1024) for i in range(3)], [work(27648 + 1024 * i, 1024) for i in range(3)]]
    BTs = [f32(X0, 1280), f32(X0 + 1280, 1280)]
    bmask = f32(X0 + 6656, 640)
    t_bm = once(sp, bmask, d["bmask"], t_spill)
    bt_free = [[t_spill], [t_spill]]
    att_free = [[done3], [done3]]
    Pv3 = [f32(X0 + 2560 + 640 * i, 640) for i in range(2)]
    PTv3 = [f32(X0 + 3840 + 640 * i, 640) for i in range(2)]
    Pb, PTb = Places([]), Places([])
    Pb.free = [(0, [t_spill]), (1, [t_spill])]
    PTb.free = [(0, [t_spill]), (1, [t_spill])]
    tBT = {}
    T3 = {}

    def both(f):
        for h in range(2):
            yield from f(h, H2[h], tH2[h])

    def ev_av2(half):
        def f(tt, ps, tk):
            q = 4 * half + tt
            T3["av", q] = act(lambda e: e.activation(av[:, q, :], ps, ACT.Copy), tk, done3)
            return T3["av", q]
        return f

    def proj_b(j):
        q, k, g = atts[j % 2]
        fr = att_free[j % 2]
        bt = BTs[j % 2]
        t_bt = once(sp, v3(bt, 2), v3(d["band"][:, 1280 * j:1280 * j + 1280], 2), bt_free[j % 2])
        for a in range(2):
            tBT[j] = dve(lambda e: e.tensor_tensor(bt[:, 640 * a:640 * a + 640], bt[:, 640 * a:640 * a + 640],
                                                   bmask, ADD), t_bt, t_bm)
        yield from both(lambda h, s, t: gemmT(W2, 2176 + 128 * j, 1, s, t, ev_to(f"bq{j}", [q], h, wait=fr), cut=CUT))
        yield from both(lambda h, s, t: gemmT(W2, 2688 + 128 * j, 1, s, t, ev_to(f"bk{j}", [k], h, wait=fr), cut=CUT))

    def proj_g(j):
        g = atts[j % 2][2]
        fr = att_free[j % 2]
        yield from both(lambda h, s, t: gemmT(W2, 3712 + 128 * j, 1, s, t,
                                              ev_swish(f"bg{j}", [g], h, fr), cut=CUT))

    def head_scale(tl, toks, fin, sqs, sfree, rr, rrfree, scal, out):
        n = len(tl)
        b, free = banks1.take()
        sqf = [sfree] * len(sqs)
        for j in range(n):
            sq = sqs[j % len(sqs)]
            ts = act(lambda e: e.activation(sq, tl[j], ACT.Square), toks[j], sqf[j % len(sqs)])
            for tt in range(8):
                o = bank(b)[:, tt * 2 * n + 2 * j:tt * 2 * n + 2 * j + 2]
                tk = pe(lambda e: e.matmul(o, sq[:, tt * 128:(tt + 1) * 128], cs("bo"), start=True, stop=True),
                        ts, free)
            sqf[j % len(sqs)] = tk
            yield
        st = small[:, 448:448 + 16 * n]
        t, tst = fin(st, bank(b)[:, 0:16 * n], tk)
        banks1.give(b, t)
        yield
        for n0 in range(2):
            p, free = banks1.take()
            for tt in range(4):
                q = 4 * n0 + tt
                tk2 = transpose(bank(p)[0:2 * n, tt * 128:(tt + 1) * 128], st[:, q * 2 * n:(q + 1) * 2 * n],
                                tst, free, inc=(tt == 3))
            trr = dve(lambda e: e.tensor_copy(rr[0:2 * n, 512 * n0:512 * n0 + 512], bank(p)[0:2 * n, :]), tk2,
                      tk, rrfree)
            banks1.give(p, trr)
        yield
        for j in range(n):
            for n0 in range(2):
                p, free = banks1.take()
                sl = slice(512 * n0, 512 * n0 + 512)
                tk = pe(lambda e: e.matmul(bank(p), cs("selp", 128 * j, 128 * j + 128)[0:2 * n, :],
                                           rr[0:2 * n, sl], start=True, stop=True), trr, free)
                t = dve(lambda e: e.scalar_tensor_tensor(out=tl[j][:, sl], in0=tl[j][:, sl], scalar=scal(j),
                                                         in1=bank(p), op0=MUL, op1=MUL), tk, toks[j], t_col)
                banks1.give(p, t)
                out[j] = t
            yield

    def fin_rms(st, ps, tk):
        a = dve(lambda e: e.tensor_scalar(st, ps, 1.0 / 64, 1e-6, MUL, ADD), tk)
        t = act(lambda e: e.activation(st, st, ACT.Sqrt), a)
        return a, dve(lambda e: e.reciprocal(st, st), t)

    sqf_ = [[done3]]

    def qk_norm(j):
        nms, out = (f"bq{j}", f"bk{j}"), {}
        yield from head_scale(atts[j % 2][0:2], [[T[nm, 0, 0], T[nm, 0, 1]] for nm in nms], fin_rms,
                              [work(30720, 1024)], [sqf_[0], t_spill], work(31744, 1024), sqf_[0],
                              lambda q: col(("qng", "kng")[q]), out)
        sqf_[0] = [(pe.sem, pe.n)]
        for q, nm in enumerate(nms):
            T3[nm] = out[q]

    ob = {}
    tya = {}

    def band(j, n, a):
        nk = min(5, n + 1)
        W = 128 * nk
        k0 = (n + 1 - nk) * 128
        h = 2 * j + a
        q_, k_, g_ = atts[j % 2]
        b, free = banks2.take()
        for c0 in range(0, W, 512):
            cn = min(512, W - c0)
            tS = pe(lambda e, c0=c0, cn=cn, b=b: e.matmul(
                pair(b)[:, c0:c0 + cn], q_[64 * a:64 * a + 64, n * 128:(n + 1) * 128],
                k_[64 * a:64 * a + 64, k0 + c0:k0 + c0 + cn], start=True, stop=True),
                T3[f"bq{j}"], T3[f"bk{j}"], free)
        p, pfree = Pb.take()
        P = Pv3[p][:, 0:W].rearrange("p (g w) -> p g w", g=1)
        S = pair(b)[:, 0:W].rearrange("p (g w) -> p g w", g=1)
        bias = v3(BTs[j % 2], 2)[:, a:a + 1, 640 - W:640]
        tP, tr = softmax(S, tS, P, W, 1, 0.125, bias, None, stat(), pfree, tBT[j])
        banks2.give(b, tr)
        yield
        b, free = banks2.take()
        for kt in range(nk):
            tt = transpose(pair(b)[:, kt * 128:(kt + 1) * 128], P[:, 0, kt * 128:(kt + 1) * 128], tP, free,
                           inc=(kt == nk - 1))
        Pb.give(p, tt)
        q, qfree = PTb.take()
        PT = PTv3[q]
        t1 = act(lambda e, b=b: e.activation(PT[:, 0:W], pair(b)[:, 0:W], ACT.Copy), tt, qfree)
        banks2.give(b, t1)
        yield
        if a == 0:
            ob[j, n] = banks1.take()
        b, free = ob[j, n]
        for kt in range(nk):
            tile = k0 // 128 + kt
            to = pe(lambda e, kt=kt, tile=tile, b=b: e.matmul(
                bank(b)[64 * a:64 * a + 64, 0:128], av[:, tile, 64 * h:64 * h + 64],
                PT[:, kt * 128:(kt + 1) * 128], start=(kt == 0), stop=(kt == nk - 1)),
                t1, T3["av", tile], free, inc=(kt == nk - 1))
        PTb.give(q, to)
        if a == 1:
            sl = slice(n * 128, (n + 1) * 128)
            t = dve(lambda e: e.scalar_tensor_tensor(out=yaT[:, j, sl], in0=bank(b)[:, 0:128], scalar=0.5,
                                                     in1=g_[:, sl], op0=MUL, op1=MUL), to,
                    T[f"bg{j}", 0, 0], T[f"bg{j}", 0, 1], done3)
            banks1.give(b, t)
            tya[j, n] = t

    def attend(j):
        yield from staggered([band(j, n, a) for n in range(8) for a in range(2)], DB)
        att_free[j % 2] = bt_free[j % 2] = [(pe.sem, pe.n), (dve.sem, dve.n), (act.sem, act.n)]

    run(both(lambda h, s, t: gemmN(W2, 3200, 512, s, t, ev_av2(h))))
    def heads(j):
        return chain(proj_b(j), weave(proj_g(j), qk_norm(j), NQ))

    run(heads(0))
    for j in range(1, 4):
        together(heads(j), attend(j - 1), NB)
    wt = lambda a: work(a, 1024)
    xt_ = lambda a: f32(X0 + a, 1024)
    rr_ = [wt(20480), wt(21504), wt(22528), xt_(6656)]
    kk_ = [wt(27648), wt(28672), wt(29696), wt(23552)]
    vv_ = [wt(24576), wt(25600), wt(26624), xt_(0)]
    gg_ = [xt_(1024), xt_(2048), xt_(3072), xt_(4096)]
    lo = wt(30720)
    lw = work(31744, 512)
    pads = [f32(X0 + 5120, 513), f32(X0 + 5633, 513)]
    last3 = attend(3)
    lofree = [(pe.sem, pe.n), (dve.sem, dve.n), (act.sem, act.n)]
    t_lw = once(sp, lw, d["lora"], lofree)
    pf = [[t_spill], [t_spill]]
    T4 = {}
    mun = small[:, 512:529]
    tmu = dve(lambda e: e.tensor_scalar(mun, cols[:, COLS["mu"][0]:COLS["mu"][0] + 17], -1.0, 1.0, MUL, ADD),
              t_col)

    def ev_shift(half, base, name, dst, wait):
        def f(m, ps, tk):
            q = base + m
            i = cnt[0] % 2
            cnt[0] += 1
            pad, o, tq = pads[i], dst[m][:, 512 * half:512 * half + 512], small[:, 704 + q:705 + q]
            if half:
                tz = dve(lambda e: e.tensor_copy(pad[:, 0:1], tq), T["shtail", q], pf[i])
            else:
                tz = dve(lambda e: e.memset(pad[:, 0:1], 0.0), pf[i])
            te = act(lambda e: e.activation(pad[:, 1:513], ps, ACT.Copy), tk, pf[i])
            if not half:
                T["shtail", q] = dve(lambda e: e.tensor_copy(tq, pad[:, 512:513]), te)
            t = dve(lambda e: e.tensor_scalar(o, pad[:, 1:513], mun[:, q:q + 1], None, MUL), te, tmu, wait)
            t = dve(lambda e: e.scalar_tensor_tensor(out=o, in0=pad[:, 0:512], scalar=col("mu", q), in1=o,
                                                     op0=MUL, op1=ADD), t, tz)
            pf[i] = t if half else [t, T["shtail", q]]
            if name == "g":
                t = act(lambda e: e.activation(o, o, ACT.Silu), t)
            T4[name, m, half] = t
            return te
        return f
    rfree = att_free[0]
    together(chain(both(lambda h, s, t: gemmT(W2, 2048, 1, s, t, ev_shift(h, 16, "lo", [lo], lofree), cut=CUT)),
                   both(lambda h, s, t: gemmT(W2, 0, 4, s, t, ev_shift(h, 0, "r", rr_, [rfree, t_bm]), cut=CUT))),
             last3, NR)
    afree = [(pe.sem, pe.n), (dve.sem, dve.n), (act.sem, act.n)]
    for q, (nm, dst) in enumerate((("k", kk_), ("v", vv_), ("g", gg_))):
        run(both(lambda h, s, t: gemmT(W2, 512 * (q + 1), 4, s, t,
                                       ev_shift(h, 4 * (q + 1), nm, dst, afree))))
    hfree5 = [(pe.sem, pe.n)]
    for m in range(4):
        for nm in "rkvg":
            T4[nm, m] = [T4[nm, m, 0], T4[nm, m, 1]]
    tlo = [T4["lo", 0, 0], T4["lo", 0, 1]]
    ttanh = act(lambda e: e.activation(lo[0:64, :], lo[0:64, :], ACT.Tanh), tlo)
    sg, aa, kn = ([work(b0 + 1024 * j, 1024) for j in range(4)] for b0 in (0, 4096, 8192))
    for q, (dst, bias) in enumerate(((sg, "w0"), (aa, "a0"))):
        for j in range(4):
            b, free = banks2.take()
            for n in range(2):
                tk = pe(lambda e: e.matmul(
                    pair(b)[:, 512 * n:512 * n + 512], lw[64 * q:64 * q + 64, 128 * j:128 * j + 128],
                    lo[64 * q:64 * q + 64, 512 * n:512 * n + 512], start=True, stop=True),
                    t_lw, ttanh, tlo, free, inc=(n == 1))
            T4[bias, j] = act(lambda e: e.activation(dst[j], pair(b), ACT.Sigmoid, bias=col(bias, j)), tk,
                              hfree5)
            banks2.give(b, T4[bias, j])
    lora_done = [(pe.sem, pe.n)]
    sl_ids = lend_ring()
    sf = [x[1] for x in sl_ids]
    i0 = [x[0] for x in sl_ids]
    rs64 = slot(i0[0])[:, 0:1024]
    t_rs64 = once(sp, rs64, d["reset64"], sf[0])
    PLc = v3(small[:, 544:608], 4)
    tkk = {}
    for j in range(4):
        tkk[j] = act(lambda e: e.activation(kn[j], kk_[j], ACT.Copy, scale=col("kk", j)), T4["k", j], hfree5)

    def fin_l2(st, ps, tk):
        t = act(lambda e: e.activation(st, ps, ACT.Sqrt), tk)
        t2 = dve(lambda e: e.tensor_scalar(st, st, 1e-12, None, MAX), t)
        return t, dve(lambda e: e.reciprocal(st, st), t2)
    out = {}
    run(head_scale(kn, tkk, fin_l2, [slot(i0[1])[:, 0:1024], slot(i0[1])[:, 1024:2048]], sf[1],
                   slot(i0[0])[:, 1024:2048], sf[0], lambda j: 1.0, out))
    bon = v3(small[:, 608:672], 8)
    b, freeb = banks1.take()
    tr_ = {}
    for j in range(4):
        A, B, C, D = (work(12288 + 1024 * i, 1024) for i in range(4))
        pt = T4.get(("prep", j - 1))
        t1 = dve(lambda e, j=j: e.tensor_scalar(A, aa[j], 1.0, col("ka", j), SUB, MUL), T4["a0", j],
                 hfree5, pt)
        t1 = dve(lambda e, j=j: e.scalar_tensor_tensor(out=kk_[j], in0=A, scalar=1.0, in1=kk_[j],
                                                       op0=ADD, op1=MUL), t1, tkk[j])
        t2 = dve(lambda e, j=j: e.tensor_tensor(aa[j], aa[j], kn[j], MUL), out[j], t1)
        t3 = dve(lambda e, j=j: e.scalar_tensor_tensor(out=D, in0=rr_[j], scalar=col("rk", j),
                                                       in1=kk_[j], op0=MUL, op1=MUL), t1, T4["r", j],
                 pt, t_col)
        for tt in range(8):
            o = bank(b)[:, tt * 8 + 2 * j:tt * 8 + 2 * j + 2]
            tbo = pe(lambda e, tt=tt, o=o: e.matmul(o, D[:, tt * 128:(tt + 1) * 128], cs("bo"), start=True,
                                                    stop=True), t3, freeb)
        t4 = dve(lambda e, j=j: e.tensor_tensor_scan(B, rs64, sg[j], 0.0, MUL, ADD), T4["w0", j],
                 t_rs64, pt)
        t5 = dve(lambda e, j=j: e.tensor_tensor(A, B, sg[j], SUB), t4, t1)
        t6 = act(lambda e: e.activation(C, B, ACT.Exp, scale=EH), t4, pt)
        t7 = act(lambda e: e.activation(B, B, ACT.Exp, scale=-EH), t4, t5)
        t8 = act(lambda e: e.activation(A, A, ACT.Exp, scale=-EH), t5)
        t9 = dve(lambda e, j=j: e.scalar_tensor_tensor(out=sg[j], in0=kn[j], scalar=-1.0, in1=A,
                                                       op0=MUL, op1=MUL), t8, t5)
        ta = dve(lambda e, j=j: e.tensor_tensor(aa[j], aa[j], C, MUL), t6, t2)
        tb_ = dve(lambda e, j=j: e.tensor_tensor(kk_[j], kk_[j], C, MUL), t6, t3)
        tc = dve(lambda e, j=j: e.tensor_tensor(rr_[j], rr_[j], B, MUL), t7, t3)
        td = dve(lambda e, j=j: e.tensor_copy(PLc[:, j, :], B.rearrange("p (c t) -> p c t", c=16)[:, :, 63]),
                 t7)
        T4["prep", j] = [t9, ta, tb_, tc, td, tbo]
    prep = [T4["prep", j] for j in range(4)]
    tbon = dve(lambda e: e.tensor_copy(small[:, 608:672], bank(b)[:, 0:64]), tbo)
    banks1.give(b, tbon)
    At, Bh, Kh, Rt = sg, aa, kk_, rr_

    allf = [prep, tbon, lora_done]
    m2 = f32(X0 + 5120, 1280)
    t_m2 = once(sp, m2, d["m2"], allf)
    mAR = m2[:, 0:256].rearrange("p (q t) -> p q t", q=2)
    mL, m0, m0T = m2[:, 256:384], m2[:, 384:512], m2[:, 512:640]
    lv = [m2[:, 640 + 128 * l:768 + 128 * l] for l in range(5)]
    spare = [work(8192, 8192), f32(G0, 8192), work(30720, WN - 30720)]
    used = [0, 0, 0]

    def place(n):
        for i, r in enumerate(spare):
            if used[i] + n <= r.shape[1]:
                used[i] += n
                return r[:, used[i] - n:used[i]]
        assert False
    per = [dict(TT=place(1024), RB=place(1024), NV=place(512), RKV=place(512), vt=place(512), kt=place(512),
                bt=place(512)) for _ in range(2)]
    gMT, gM, gT, gX, gN = place(1024), place(1024), place(1024), place(1024), place(1024)
    gRK = gX
    Zb = v3(place(512), 4)
    Xs, Us = place(512), place(512)
    Zt = place(512)
    ych = [place(512), place(512)]
    t_z = dve(lambda e: e.memset(Zb, 0.0), allf)
    state = {"Z": t_z, "gfree": allf, "xs": allf, "us": allf}
    pfree_ = [allf, allf]
    yfree = [allf, allf]
    h8 = lambda v: v.rearrange("p (h t) -> p h t", h=8)
    yr = Rt
    tyr = {}

    def bc(m, n=8):
        return m.unsqueeze(1).to_broadcast([128, n, 128])

    banks = Places([])
    for _ in range(2):
        i, free = banks2.take()
        banks.give(2 * i, free)
        banks.give(2 * i + 1, free)
    for _ in range(4):
        i, free = banks1.take()
        banks.give(i, free)
    h4 = lambda v: v.rearrange("p (h t) -> p h t", h=4)

    def pre(cp):
        r = per[cp % 2]
        sl = slice(128 * cp, 128 * cp + 128)
        fr = [pfree_[cp % 2]]
        gf = state["gfree"]
        TT, RB = h8(r["TT"]), h8(r["RB"])
        MT, M, Tm, X, N = h8(gMT), h8(gM), h8(gT), h8(gX), h8(gN)
        RK = h8(gRK)
        tks = []
        for src, dst in ((vv_, "vt"), (Kh, "kt"), (Bh, "bt")):
            b, free = banks.take()
            for j in range(4):
                tk = transpose(bank(b)[:, 128 * j:128 * j + 128], src[j][:, sl], free, prep,
                               T4["v", j], inc=(j == 3))
            t = act(lambda e, b=b, dst=dst: e.activation(r[dst], bank(b), ACT.Copy), tk, fr)
            banks.give(b, t)
            tks.append(t)
        hv = lambda v, a: v[:, 4 * a:4 * a + 4, :]
        tMT, tRB, tN, tRK, tM = {}, {}, {}, {}, {}
        for lhs, outs in ((Bh, ((MT, At, mAR[:, 0, :], tMT), (RB, Rt, mAR[:, 1, :], tRB))),
                          (At, ((M, Bh, m0, tM),)),
                          (Kh, ((N, At, mAR[:, 0, :], tN), (RK, Rt, mAR[:, 1, :], tRK)))):
            for dst, rhs, mask, tok in outs:
                for a in range(2):
                    b, free = banks.take()
                    for j in range(4):
                        tk = pe(lambda e: e.matmul(
                            bank(b)[:, 128 * j:128 * j + 128], lhs[j][64 * a:64 * a + 64, sl],
                            rhs[j][64 * a:64 * a + 64, sl], start=True, stop=True), free, prep,
                            inc=(j == 3))
                    tok[a] = dve(lambda e: e.tensor_tensor(hv(dst, a), h4(bank(b)), bc(mask, 4), MUL),
                                 tk, t_m2, fr, gf)
                    banks.give(b, tok[a])
            yield
        tT, tTT, tX_ = {}, {}, {}
        for a in range(2):
            tT[a] = dve(lambda e: e.tensor_tensor(hv(Tm, a), hv(M, a), bc(I, 4), ADD), tM[a], gf)
            tTT[a] = dve(lambda e: e.tensor_tensor(hv(TT, a), hv(MT, a), bc(m0T, 4), MUL), tMT[a], fr)
            tTT[a] = dve(lambda e: e.tensor_tensor(hv(TT, a), hv(TT, a), bc(I, 4), ADD), tTT[a])
        for src, tsrc, dst in ((N, tN, "NV"), (RK, tRK, "RKV")):
            b, free = banks.take()
            for g in range(8):
                hh = 2 * (g % 4) + g // 4
                tk = pe(lambda e: e.matmul(
                    bank(b)[:, 64 * g:64 * g + 64], src[:, g, :], r["vt"][:, 64 * hh:64 * hh + 64],
                    start=True, stop=True), tsrc, tks[0], free, inc=(g == 7))
            t = act(lambda e: e.activation(r[dst], bank(b), ACT.Copy), tk, fr)
            banks.give(b, t)
            r["t" + dst] = t
        tX_ = {0: tk, 1: tk}
        for l in range(5):
            tXX = {}
            for a in range(2):
                b, free = banks.take()
                for g in range(4 * a, 4 * a + 4):
                    tk = pe(lambda e: e.matmul(bank(b)[:, 128 * (g % 4):128 * (g % 4) + 128], MT[:, g, :],
                                               Tm[:, g, :], start=True, stop=True), tMT[a], tT[a], free,
                            inc=(g % 4 == 3))
                tXX[a] = dve(lambda e: e.tensor_tensor(hv(X, a), h4(bank(b)), bc(lv[l], 4), MUL), tk,
                             tX_[a])
                banks.give(b, tXX[a])
            yield
            for a in range(2):
                outs = ((X, TT, TT, tTT), (TT, X, Tm, tT))[:2 if l < 4 else 1]
                done = []
                for lhs, rhs, dst, tok in outs:
                    b, free = banks.take()
                    for g in range(4 * a, 4 * a + 4):
                        tk = pe(lambda e: e.matmul(bank(b)[:, 128 * (g % 4):128 * (g % 4) + 128],
                                                   lhs[:, g, :], rhs[:, g, :], start=True, stop=True),
                                tXX[a], tTT[a], free, inc=(g % 4 == 3))
                    done.append((b, dst, tok))
                tX_[a] = tk
                for b, dst, tok in reversed(done):
                    tok[a] = dve(lambda e: e.tensor_tensor(hv(dst, a), h4(bank(b)), hv(dst, a), ADD), tk,
                                 tok[a])
                    banks.give(b, tok[a])
            yield
        r["tTT"], r["tRB"], r["tks"] = tTT, tRB, tks
        state["gfree"] = [tk, tTT]

    def seq(cp):
        r = per[cp % 2]
        sl = slice(128 * cp, 128 * cp + 128)
        TT, RB = h8(r["TT"]), h8(r["RB"])
        y = ych[cp % 2]
        yb, yfr = banks.take()
        for par in range(2):
            c = 2 * cp + par
            cols_ = slice(64 * c, 64 * c + 64)
            ps_ = slice(64 * par, 64 * par + 64)
            b, free = banks.take()
            for j in range(4):
                o = bank(b)[ps_, :].rearrange("p (a j i) -> p a j i", a=2, j=4)[:, :, j, :]
                tk = pe(lambda e, j=j, o=o, cols_=cols_: e.matmul(o, At[j][:, cols_], Zb[:, j, :], start=True,
                                                                  stop=True), state["Z"], free, prep,
                        inc=(j == 3))
            tx = dve(lambda e, b=b, ps_=ps_: e.tensor_tensor(Xs[ps_, :], bank(b)[ps_, :], r["NV"][ps_, :],
                                                             ADD), tk, r["tNV"], state["xs"])
            banks.give(b, tx)
            yield
            b, free = banks.take()
            for g in range(8):
                tk = pe(lambda e, g=g, b=b, ps_=ps_: e.matmul(
                    bank(b)[ps_, 64 * g:64 * g + 64], TT[ps_, g, ps_], Xs[ps_, 64 * g:64 * g + 64],
                    start=True, stop=True), tx, r["tTT"], free, inc=(g == 7))
            state["xs"] = tk
            tu = act(lambda e, b=b, ps_=ps_: e.activation(Us[ps_, :], bank(b)[ps_, :], ACT.Copy), tk,
                     state["us"])
            banks.give(b, tu)
            yield
            b, free = banks.take()
            for g in range(8):
                a, j = g // 4, g % 4
                hh = 2 * j + a
                o = bank(b)[64 * a:64 * a + 64, 64 * j:64 * j + 64]
                pe(lambda e, o=o, hh=hh, g=g, ps_=ps_: e.matmul(
                    o, r["bt"][ps_, 64 * hh:64 * hh + 64], Us[ps_, 64 * g:64 * g + 64], start=True,
                    stop=False), tu, r["tks"], free, inc=False)
                tk = pe(lambda e, o=o, hh=hh, ps_=ps_: e.matmul(
                    o, r["kt"][ps_, 64 * hh:64 * hh + 64], r["vt"][ps_, 64 * hh:64 * hh + 64],
                    start=False, stop=True), inc=(g == 7))
            ty = None
            for j in range(4):
                o = bank(yb)[ps_, :].rearrange("p (a j i) -> p a j i", a=2, j=4)[:, :, j, :]
                pe(lambda e, j=j, o=o, cols_=cols_: e.matmul(o, Rt[j][:, cols_], Zb[:, j, :], start=True,
                                                             stop=False, skip_group_check=True),
                   yfr, inc=False)
                for a in range(2):
                    g = 4 * a + j
                    ty = pe(lambda e, g=g, ps_=ps_: e.matmul(
                        bank(yb)[ps_, 64 * g:64 * g + 64], RB[ps_, g, ps_], Us[ps_, 64 * g:64 * g + 64],
                        start=False, stop=True, skip_group_check=True), r["tRB"], inc=(j == 3 and a == 1))
            state["us"] = ty
            tz_ = None
            for a in range(2):
                as_ = slice(64 * a, 64 * a + 64)
                zv = Zb[as_, :, 64 * a:64 * a + 64]
                pv = bank(b)[as_, 0:256].rearrange("p (j i) -> p j i", j=4)
                t1 = dve(lambda e, zv=zv, pv=pv: e.tensor_tensor(zv, pv, zv, ADD), tk, ty, state["Z"])
                tz_ = dve(lambda e, zv=zv, as_=as_, c=c: e.tensor_tensor(
                    zv, zv, PLc[as_, :, c:c + 1].to_broadcast([64, 4, 64]), MUL), t1)
            banks.give(b, tz_)
            state["Z"] = tz_
            yield
        yf = yfree[cp % 2]
        nat = lambda v: v.rearrange("p (j a i) -> p a j i", j=4, a=2)
        byp = lambda v: v.rearrange("p (a j i) -> p a j i", j=4, a=2)
        ty2 = dve(lambda e: e.tensor_tensor(nat(y), byp(bank(yb)), byp(r["RKV"]), ADD), ty, r["tRKV"], yf)
        banks.give(yb, ty2)
        yv = y.rearrange("p (g i) -> p g i", g=8)
        st = small[:, 672 + 16 * (cp % 2):688 + 16 * (cp % 2)]
        q2 = Zt
        b8 = lambda v: v.unsqueeze(2).to_broadcast([128, 8, 64])
        t = dve(lambda e: e.tensor_reduce(st[:, 0:8], yv, AX.X, ADD), ty2)
        t = dve(lambda e: e.tensor_scalar(st[:, 0:8], st[:, 0:8], 1.0 / 64, None, MUL), t)
        t = dve(lambda e: e.tensor_tensor(yv, yv, b8(st[:, 0:8]), SUB), t)
        ta = act(lambda e: e.activation(q2, y, ACT.Square), t, state.get("q2"))
        t = dve(lambda e: e.tensor_reduce(st[:, 8:16], q2.rearrange("p (g i) -> p g i", g=8), AX.X, ADD), ta)
        state["q2"] = t
        t = dve(lambda e: e.tensor_scalar(st[:, 8:16], st[:, 8:16], 1.0 / 64, 64e-5, MUL, ADD), t)
        t = act(lambda e: e.activation(st[:, 8:16], st[:, 8:16], ACT.Sqrt), t)
        t = dve(lambda e: e.reciprocal(st[:, 8:16], st[:, 8:16]), t)
        t = dve(lambda e: e.tensor_tensor(yv, yv, b8(st[:, 8:16]), MUL), t)
        t = dve(lambda e: e.tensor_tensor(y, y, row("lng"), MUL), t)
        t = dve(lambda e: e.tensor_tensor(y, y, row("lnb"), ADD), t)
        t = dve(lambda e: e.tensor_tensor(q2.rearrange("p (g i) -> p g i", g=8),
                                          r["vt"].rearrange("p (g i) -> p g i", g=8), b8(bon[:, cp, :]), MUL),
                t, tbon)
        t = dve(lambda e: e.tensor_tensor(y, y, q2, ADD), t)
        state["q2"] = t
        yield
        b, free = banks.take()
        for j in range(4):
            tk = transpose(bank(b)[:, 128 * j:128 * j + 128], y[:, 128 * j:128 * j + 128], t, free,
                           inc=(j == 3))
        yfree[cp % 2] = tk
        for j in range(4):
            t = dve(lambda e: e.tensor_tensor(yr[j][:, sl], bank(b)[:, 128 * j:128 * j + 128],
                                              gg_[j][:, sl], MUL), tk, T4["g", j], ty)
        banks.give(b, t)
        tyr[cp] = t
        pfree_[cp % 2] = [t, tk, ty]
        yield

    run(pre(0))
    for cp in range(8):
        if cp < 7:
            together(pre(cp + 1), seq(cp), 1)
        else:
            run(seq(cp))
    for _ in range(8):
        i, free = banks.take()
        if i >= 4:
            banks1.give(i, free)
    fin = [(pe.sem, pe.n), (act.sem, act.n), (dve.sem, dve.n)]
    for i in i0:
        slots.give(i, fin)
    src = yr + tiles(yaT)
    OP = [Parts(W0 + 8192, W0 + 8192 + 4096), Parts(W0, W0 + 4096)]
    tO = [{}, {}]
    for h in range(2):
        two_parts(src, [fin] * 8, h, OP[h], tO[h], fin)
    tXr = [once(sp, XT[:, k, :], spilled[:, k, :], tO[0], tO[1], t_spill) for k in range(8)]

    def ev_out(half):
        def f(m, ps, tk):
            o = XT[:, m, 512 * half:512 * half + 512]
            t = dve(lambda e: e.scalar_tensor_tensor(out=o, in0=ps, scalar=mod[:, 16 + m:17 + m], in1=o,
                                                     op0=MUL, op1=ADD), tk, tXr[m], t_mod)
            finals.append(once(act, d["out"][m * 128:(m + 1) * 128, 512 * half:512 * half + 512], o, t))
            return t
        return f
    for h in range(2):
        run(gemmT(d["w_out2"], 0, 8, OP[h], tO[h], ev_out(h)))
    sp(lambda e: e.nop(), finals, inc=False)


def host_layout(inputs):
    import numpy as np
    f = {k: np.asarray(v) for k, v in inputs.items()}

    def colv(v, k):
        return v.reshape(k, 128).T
    s = np.zeros((128, NCOLS), np.float32)

    def put(name, m):
        o, w = COLS[name]
        s[:, o:o + w] = m
    for name, key in (("g_mix", "norm_mix_g"), ("g_x", "norm_xattn_g"), ("g_mem", "norm_mem_g"),
                      ("g_ffn", "norm_ffn_g"), ("g_fin", "norm_final_g"), ("g_n2", "norm_g_2"), ("c", "c_2")):
        put(name, colv(f[key], 8))
    put("b_ada", colv(f["b_ada_2"], 24))
    put("convw", f["conv_qk_w"][0].reshape(4, 8, 128).transpose(2, 1, 0).reshape(128, 32))
    put("convb", colv(f["conv_qk_b"], 8))
    put("fw", f["conv_ffn_w"][0].reshape(3, 22, 128).transpose(2, 1, 0).reshape(128, 66))
    put("fb", colv(f["conv_ffn_b"], 22))
    put("mu", colv(f["mu_shift_2"], 17))
    for name, key in (("w0", "w0_2"), ("a0", "a0_2"), ("kk", "k_k_2"), ("ka", "k_a_2"), ("rk", "r_k_2")):
        put(name, colv(f[key], 4))
    for name, key in (("qng", "q_norm_g_2"), ("kng", "k_norm_g_2")):
        put(name, np.concatenate([f[key][0], f[key][0]])[:, None])
    order = [4 * a + j for j in range(4) for a in range(2)]
    sk = f["attn_sinks"][0]
    sinks = np.concatenate([sk[[2 * jp, 2 * jp + 1, 4 + 2 * jp, 5 + 2 * jp]] for jp in range(2)])
    lng = f["lnx_g_2"][0]
    lnb = f["lnx_b_2"][0]
    rows = np.concatenate([f["b_gate_if"][0], sinks, lng, lnb])
    rows = np.ascontiguousarray(np.broadcast_to(rows, (128, NROWS)))
    cst = np.zeros((128, NCST), np.float32)

    def putc(name, m):
        o, w = CST[name]
        cst[:m.shape[0], o:o + w] = m
    p = np.arange(128)
    putc("I", np.eye(128))
    putc("ones", np.ones((128, 128)))
    putc("bo", (p[:, None] // 64 == np.arange(2)[None]) * 1.0)
    putc("mst", np.where(p[:, None] <= p[None], 0.0, -1e30))
    putc("selh", (np.arange(4)[:, None] == (np.arange(512) // 128)[None]) * 1.0)
    q = np.arange(512)
    putc("selp", (np.arange(8)[:, None] == (2 * (q // 128) + (q % 128) // 64)[None]) * 1.0)
    slopes = 2.0 ** (-np.arange(1, 9, dtype=np.float32))
    dist = p[:, None] + 128 - np.arange(256)[None]
    ok = (dist >= 0) & (dist < 128)
    alibi = np.concatenate([np.where(ok, -slopes[h] * dist, -1e30) for jp in range(2)
                            for h in (2 * jp, 2 * jp + 1, 4 + 2 * jp, 5 + 2 * jp)], axis=1).astype(np.float32)
    r128 = np.ones((4, 1024), np.float32)
    r128[:, ::128] = 0
    r64 = np.ones((128, 1024), np.float32)
    r64[:, ::64] = 0
    same = p[:, None] // 64 == p[None] // 64
    strict = same & (p[:, None] < p[None])
    incl = same & (p[:, None] <= p[None])
    low = same & (p[:, None] > p[None])
    ms = [strict, incl, low]

    def level(l):
        n = 1 << l
        t, u = p[:, None], p[None]
        return (t // (2 * n) == u // (2 * n)) & (t // n % 2 == 1) & (u // n % 2 == 0)
    ms += [level(0), level(0).T] + [level(l) for l in range(1, 6)]
    m2 = np.concatenate([m.astype(np.float32) for m in ms], axis=1)
    rb = f["rel_bias_2"][0]
    kq = np.arange(640)
    dd = p[:, None] + 512 - kq[None]
    idx = np.clip(np.clip(dd, -63, 128) + 63, 0, 191)
    band = np.ascontiguousarray(rb[:, idx].transpose(1, 0, 2).reshape(128, 8 * 640))
    hi = (p[:, None] >= 64)
    bad = (hi & (kq[None] < 64)) | (~hi & (kq[None] >= 576))
    bmask = np.where(bad, -1e30, 0.0).astype(np.float32)
    perm = np.concatenate([np.arange(64) + 64 * h for h in [4 * a + j for j in range(4) for a in range(2)]])
    w_in = f["w_in"][0].copy()
    w_in[:, :512] = f["w_in"][0][:, perm]
    w_out = f["w_out"][0].copy()
    w_out[:512] = f["w_out"][0][perm]
    return {
        "xT": f["x"][0].T, "memT": f["mem"][0].T, "cols": s, "rows": rows, "cst": cst, "alibi": alibi,
        "reset128": r128, "reset64": r64, "m2": m2, "band": band, "bmask": bmask,
        "w_in": w_in, "w_out": w_out, "wq": f["wq_x"][0], "wkv": f["wkv_x"][0], "wo": f["wo_x"][0],
        "w_up": f["w_up"][0], "w_down": f["w_down"][0], "w_ada": f["w_ada_2"][0], "w_in2": f["w_in_2"][0],
        "w_out2": f["w_out_2"][0], "lora": np.concatenate([f["w2_2"][0], f["a2_2"][0]], axis=0),
    }


def kernel(**inputs):
    import numpy as _np
    import concourse.bacc as _bacc
    from concourse import mybir as _mybir
    from concourse.bass_utils import run_bass_kernel_spmd as _run

    nc = _bacc.Bacc("TRN2", target_bir_lowering=False, num_devices=1)
    arrays, d = {}, {}
    for name, a in host_layout(inputs).items():
        a = _np.ascontiguousarray(a)
        arrays[f"in_{name}"] = a
        d[name] = nc.dram_tensor(f"in_{name}", a.shape, _mybir.dt.from_np(a.dtype), kind="ExternalInput").ap()
    d["out"] = nc.dram_tensor("out", (1024, 1024), F32, kind="ExternalOutput").ap()
    build(nc, d)
    r = _run(nc, [arrays], core_ids=[0])
    return _np.ascontiguousarray(r.results[0]["out"].T)[None]
```

```python
import concourse.bass as bass
from concourse import mybir
from contextlib import ExitStack

F32 = mybir.dt.float32
F32R = mybir.dt.float32r
TOTAL = 52736
ALU = mybir.AluOpType
ACT = mybir.ActivationFunctionType
AX = mybir.AxisListType
MUL, ADD, SUB, MAX, MIN = ALU.mult, ALU.add, ALU.subtract, ALU.max, ALU.min
EH = 0.6065306597126334
NSLOT = 4
NSEM = 110
CUT = 2
DW = 3
NW = 0.3
DM = 2
NG = 1
NM = 0.1
N7 = 0.34
NA = 0.5
NS = 0.62
NP = 1
RX1 = 1
RX2 = 1.5
RX3 = 1.5
NB = 0.6
NQ = 1
NR = 0.6
DB = 3

COLS = {}
ROWS = {}
CST = {}


def _lay(table, names):
    at = 0
    for n, w in names:
        table[n] = (at, w)
        at += w
    return at


NCOLS = _lay(COLS, [("g_mix", 8), ("g_x", 8), ("g_mem", 8), ("g_ffn", 8), ("g_fin", 8), ("g_n2", 8), ("c", 8),
                    ("b_ada", 24), ("convw", 32), ("convb", 8), ("fw", 66), ("fb", 22), ("mu", 17), ("w0", 4),
                    ("a0", 4), ("kk", 4), ("ka", 4), ("rk", 4), ("qng", 1), ("kng", 1), ("bg", 1)])
NROWS = _lay(ROWS, [("sinks", 8), ("lng", 512), ("lnb", 512)])
NCST = _lay(CST, [("I", 128), ("ones", 128), ("bo", 2), ("mst", 128), ("selh", 512), ("selp", 512)])
NSMALL = 800 + -(NCOLS + NROWS + NCST) % 16
X0 = NCOLS + NROWS + NCST + 32 + NSMALL
PIECES = [X0, 8192, 2048 * NSLOT, 16384, (TOTAL - X0 - 32768) // 16 * 16]


class Queue:

    def __init__(self, sem, eng):
        self.sem, self.n, self.eng, self.seen = sem, 0, eng, {}

    def issue(self, fn, sem, by, waits):
        if self.eng is None:
            return
        for s, v in flat(waits):
            if self.seen.get(id(s), 0) < v:
                self.seen[id(s)] = v
                self.eng.wait_ge(s, v)
        ins = fn(self.eng)
        if sem is not None:
            ins.then_inc(sem, by)

    def __call__(self, fn, *waits, inc=True):
        self.issue(fn, self.sem if inc else None, 1, waits)
        if inc:
            self.n += 1
        return (self.sem, self.n)

    def dma(self, fn, sem, value, *waits):
        self.issue(fn, sem, 16, waits)
        return (sem, value)


def flat(x):
    if x is None:
        return []
    if isinstance(x, dict):
        x = list(x.values())
    if isinstance(x, tuple) and len(x) == 2 and isinstance(x[1], int):
        return [x]
    return [t for y in x for t in flat(y)]


class Places:

    def __init__(self, items):
        self.free = [(i, []) for i in items]

    def take(self):
        return self.free.pop(0)

    def give(self, item, *toks):
        self.free.append((item, flat(toks)))


def staggered(units, depth):
    units, live = list(units), []
    while units or live:
        if units and len(live) < depth:
            live.append(units.pop(0))
        for u in list(live):
            try:
                next(u)
            except StopIteration:
                live.remove(u)
        yield


def run(gen):
    for _ in gen:
        pass


def build(nc, d):
    with ExitStack() as ctx:
        SB, SR = [], []
        for i, n in enumerate(PIECES):
            with nc.sbuf_tensor(f"SB{i}", [128, n], F32) as t:
                SB.append(t)
            SR.append(ctx.enter_context(nc.sbuf_tensor(f"SR{i}", [128, n], F32R)))
        PS = ctx.enter_context(nc.psum_tensor("PS", [128, 4096], F32))
        sems = [ctx.enter_context(nc.semaphore(f"s{i}")) for i in range(NSEM)]
        spill = nc.dram_tensor("spill", (1024, 1024), F32, kind="Internal").ap()
        block = ctx.enter_context(nc.Block())

        plan = []
        walk(SB, SR, PS, sems, spill, d, None, None, plan, True)

        @block.tensor
        def _(eng):
            walk(SB, SR, PS, sems, spill, d, 0, eng, plan, False)

        @block.vector
        def _(eng):
            walk(SB, SR, PS, sems, spill, d, 1, eng, plan, False)

        @block.scalar
        def _(eng):
            walk(SB, SR, PS, sems, spill, d, 2, eng, plan, False)

        @block.gpsimd
        def _(eng):
            walk(SB, SR, PS, sems, spill, d, 3, eng, plan, False)

        @block.sync
        def _(eng):
            walk(SB, SR, PS, sems, spill, d, 4, eng, plan, False)


def walk(SB, SR, PS, sems, spill, d, me, engine, plan, recording):
    nsem = [0]

    def sem():
        nsem[0] += 1
        return sems[nsem[0] - 1]

    pe, dve, act, pool, sp = (Queue(sem(), engine if i == me else None) for i in range(5))
    at = [0]

    def region(n):
        a = at[0]
        at[0] += n
        return SB[0][:, a:a + n]

    def v3(ap, k):
        return ap.rearrange("p (k n) -> p k n", k=k)

    def once(q, out, in_, *waits):
        return q.dma(lambda e: e.dma_start(out, in_), sem(), 16, *waits)

    cols, rows, cst = region(NCOLS), region(NROWS), region(NCST)
    t_cst = once(act, cst, d["cst"])
    t_col = once(act, cols, d["cols"])
    t_row = once(act, rows, d["rows"])

    def col(name, i=0):
        return cols[:, COLS[name][0] + i:COLS[name][0] + i + 1]

    def row(name, a=0, b=None):
        o, w = ROWS[name]
        return rows[:, o + a:o + (w if b is None else b)]

    def cs(name, a=0, b=None):
        o, w = CST[name]
        return cst[:, o + a:o + (w if b is None else b)]

    I = cs("I")
    mod = region(24)
    gs2 = region(8)
    small = region(NSMALL)
    assert at[0] == X0
    G0 = X0 + 8192
    W0 = G0 + NSLOT * 2048
    WN = sum(PIECES[3:])
    XTr = SB[1][:, :]
    XT = v3(XTr, 8)

    def seen(views, a, n):
        i, o = 0, a
        while o >= PIECES[i]:
            o -= PIECES[i]
            i += 1
        assert o + n <= PIECES[i]
        return views[i][:, o:o + n]

    def f32(a, n):
        return seen(SB, a, n)

    def f32r(a, n):
        return seen(SR, a, n)

    def work(a, n):
        return f32(W0 + a, n)

    class Parts:

        def __init__(self, a, b, K=8, N=512, step=None):
            step = step or N
            self.hi = [f32r(a + k * step, N) for k in range(K)]
            self.lo = [f32r(b + k * step, N) for k in range(K)]
            self.fhi = [f32(a + k * step, N) for k in range(K)]
            self.flo = [f32(b + k * step, N) for k in range(K)]

    banks2 = Places([0, 1])
    banks1 = Places([4, 5, 6, 7])

    def pair(b):
        return PS[:, 1024 * b:1024 * b + 1024]

    def bank(b):
        return PS[:, 512 * b:512 * b + 512]

    slots = Places(list(range(NSLOT)))
    slot_sem = [sem() for _ in range(NSLOT)]
    slot_n = [0] * NSLOT

    def slot(i):
        return f32(G0 + 2048 * i, 2048)

    def split(src, hi, lo, tok, *free, late=None):
        th = act(lambda e: e.activation(hi, src, ACT.Copy), tok, free)
        if late is not None:
            late.append(lambda: [th, dve(lambda e: e.tensor_tensor(lo, src, hi.bitcast(F32), SUB), th, tok, free)])
            return None
        tl = dve(lambda e: e.tensor_tensor(lo, src, hi.bitcast(F32), SUB), th, tok, free)
        return [th, tl]

    asked = [0]
    fetched, divided = [], []

    def fetch(w, k0, kn, c0, cn, parts):
        i, free = slots.take()
        slot_n[i] += 16
        view = f32(G0 + 2048 * i, kn * cn).rearrange("p (k n) -> p k n", k=kn)
        src = w[k0 * 128:(k0 + kn) * 128, c0:c0 + cn].rearrange("(k p) n -> p k n", p=128)
        return i, view, sp.dma(lambda e: e.dma_start(view, src), slot_sem[i], slot_n[i], free)

    def divide(i, view, t, kn, cn, parts):
        if not parts:
            return i, view, None, t
        a, n = G0 + 2048 * i, kn * cn
        t = split(f32(a, n), f32r(a + 1024, n), f32r(a, n), t)
        shape = lambda v: v.rearrange("p (k n) -> p k n", k=kn)
        return i, shape(f32r(a + 1024, n)), shape(f32r(a, n)), t

    def lend_ring():
        if recording:
            plan.append(None)
        fetched.append(None)
        divided.append(None)
        asked[0] += 1
        return [slots.take() for _ in range(NSLOT)]

    def slab(w, k0, kn, c0, cn, parts=True):
        if recording:
            plan.append((w, k0, kn, c0, cn, parts))
        at_ = asked[0]
        asked[0] += 1

        def ahead(done, by, f):
            while len(done) < min(at_ + by + 1, len(plan)) and plan[len(done)] is not None:
                done.append(f(len(done)))
        ahead(fetched, 3, lambda q: fetch(*plan[q]))
        ahead(divided, 2, lambda q: divide(*fetched[q], plan[q][2], plan[q][4], plan[q][5]))
        return divided[at_]

    def gemmT(w, c0, ntile, src, stok, evac, N=512, K=8, cut=8):
        for m in range(ntile):
            b, free = banks1.take()
            out = bank(b)[:, 0:N]
            for k0 in range(0, K, 8):
                kn = min(8, K - k0)
                i, whi, wlo, t = slab(w, k0, kn, c0 + m * 128, 128)
                for k in range(k0, k0 + kn):
                    hi, lo = src.hi[k], src.lo[k]
                    pe(lambda e: e.matmul(out, whi[:, k - k0, :], hi, start=(k == 0), stop=False),
                       t, stok[k], free, inc=False)
                    pe(lambda e: e.matmul(out, whi[:, k - k0, :], lo, start=False, stop=False), inc=False)
                    tk = pe(lambda e: e.matmul(out, wlo[:, k - k0, :], hi, start=False, stop=(k == K - 1)),
                            inc=(k == k0 + kn - 1))
                    if (k + 1) % cut == 0 and k < K - 1 and k < k0 + kn - 1:
                        yield
                slots.give(i, tk)
            banks1.give(b, evac(m, out, tk))
            yield

    def gemmN(w, c0, cn, src, stok, evac, T=4):
        kn = min(8, 1024 // cn)
        bs = [banks1.take() for _ in range(T)]
        for k0 in range(0, 8, kn):
            i, whi, wlo, t = slab(w, k0, kn, c0, cn)
            for tt in range(T):
                b, free = bs[tt]
                out = bank(b)[:, 0:cn]
                sl = slice(tt * 128, (tt + 1) * 128)
                for k in range(k0, k0 + kn):
                    hi, lo = src.hi[k][:, sl], src.lo[k][:, sl]
                    pe(lambda e: e.matmul(out, hi, whi[:, k - k0, :], start=(k == 0), stop=False),
                       t, stok[k], free, inc=False)
                    pe(lambda e: e.matmul(out, hi, wlo[:, k - k0, :], start=False, stop=False), inc=False)
                    tk = pe(lambda e: e.matmul(out, lo, whi[:, k - k0, :], start=False, stop=(k == 7)),
                            inc=(k == k0 + kn - 1))
                bs[tt] = (b, free) if k0 + kn < 8 else (b, tk)
            slots.give(i, tk)
        for tt in range(T):
            b, tk = bs[tt]
            banks1.give(b, evac(tt, bank(b)[:, 0:cn], tk))
        yield

    def transpose(out, in_, *waits, inc=True):
        p = in_.shape[0]
        idn = I[0:p, 0:p]
        return pe(lambda e: e.transpose(out, in_, idn), *waits, inc=inc)

    def rms(src, stok, T, gcol, out, toks, sq, free, extra=None, bias=None, f32out=None):
        nt = T // 128
        ts = [act(lambda e: e.activation(sq[k], src[k], ACT.Square), stok[k], free) for k in range(8)]
        yield
        b, bfree = banks1.take()
        for k in range(8):
            tk = pe(lambda e: e.matmul(bank(b)[:, 0:T], cs("ones"), sq[k], start=(k == 0), stop=(k == 7)),
                    ts[k], bfree, t_cst, inc=(k == 7))
        inv = sq[0]
        t = dve(lambda e: e.tensor_scalar(inv, bank(b)[:, 0:T], 1.0 / 1024, 1e-6, MUL, ADD), tk)
        banks1.give(b, t)
        t = act(lambda e: e.activation(inv, inv, ACT.Sqrt), t)
        yield
        b, bfree = banks2.take()
        tb = dve(lambda e: e.reciprocal(pair(b)[:, 0:T], inv), t, bfree)
        late = []
        for k in range(8):
            o = f32out[k] if f32out else out.flo[k]
            t = dve(lambda e: e.scalar_tensor_tensor(out=o, in0=src[k], scalar=gcol(k), in1=pair(b)[:, 0:T],
                                                     op0=MUL, op1=MUL), tb, t_col, extra, free)
            if late:
                toks[k - 1] = late.pop()()
            last = t
            if bias is not None:
                t = act(lambda e: e.activation(o, o, ACT.Identity, bias=bias(k)), t)
            toks[k] = t if f32out else split(o, out.hi[k], out.lo[k], t, tb, late=late)
            if k % 2 and k < 7:
                yield
        if late:
            toks[7] = late.pop()()
        banks2.give(b, last)

    def together(main, side, n=1):
        run(weave(main, side, n))

    def partly(main, side, n):
        due = 0
        for _ in main:
            due += n
            while due >= 1:
                due -= 1
                next(side, None)
            yield

    def weave(main, side, n=1):
        live, due = True, 0
        for _ in main:
            due += n
            while due >= 1:
                due -= 1
                if live:
                    live = next(side, "end") != "end"
            yield
        if live:
            yield from side

    def chain(*gens):
        for g in gens:
            yield from g

    def tiles(v):
        return [v[:, k, :] for k in range(v.shape[1])]

    def add_x(half, src_toks, new):
        def evac(m, ps, tk):
            o = XT[:, m, 512 * half:512 * half + 512]
            new[m] = dve(lambda e: e.tensor_tensor(o, ps, o, ADD), tk, src_toks[m])
            return new[m]
        return evac

    finals = []
    prior = []

    t_mod = []

    def ada():
        cact = small[:, 16:24]
        tc = act(lambda e: e.activation(cact, cols[:, COLS["c"][0]:COLS["c"][0] + 8], ACT.Silu), t_col)
        b, free = banks1.take()
        for m in range(24):
            i, view, _, t = slab(d["w_ada"], 0, 8, m * 128, 128, parts=False)
            for k in range(8):
                tk = pe(lambda e: e.matmul(bank(b)[:, m:m + 1], view[:, k, :], cact[:, k:k + 1], start=(k == 0),
                                           stop=(k == 7)), t, tc, free, inc=(k == 7))
            slots.give(i, tk)
            if m % 2:
                yield
        ba = cols[:, COLS["b_ada"][0]:COLS["b_ada"][0] + 24]
        t = dve(lambda e: e.tensor_tensor(mod, bank(b)[:, 0:24], ba, ADD), tk, t_col)
        banks1.give(b, t)
        g2 = cols[:, COLS["g_n2"][0]:COLS["g_n2"][0] + 8]
        t2 = dve(lambda e: e.tensor_scalar(gs2, mod[:, 8:16], 1.0, None, ADD), t)
        t2 = dve(lambda e: e.tensor_tensor(gs2, gs2, g2, MUL), t2)
        t_mod.extend([t, t2])

    def softmax(S, tS, P, W, G, scale, bias, sinks, st, pfree, extra=None):
        mx, nm, sm, es = (st[:, k * G:(k + 1) * G] for k in range(4))
        if bias is not None:
            t = dve(lambda e: e.scalar_tensor_tensor(out=P, in0=S, scalar=scale, in1=bias, op0=MUL, op1=ADD),
                    tS, pfree, extra)
            tr = t
            src, sc, neg = P, 1.0, -1.0
        else:
            src, sc, neg, t, tr = S, scale, -scale, tS, None
        t = dve(lambda e: e.tensor_reduce(mx, src, AX.X, MAX), t, pfree)
        if sinks is not None:
            t = dve(lambda e: e.tensor_tensor(mx, mx, sinks, MAX), t, t_row)
        t = dve(lambda e: e.tensor_scalar(nm, mx, neg, None, MUL), t)
        if sinks is not None:
            te = dve(lambda e: e.tensor_tensor(es, nm, sinks, ADD), t)
            te = act(lambda e: e.activation(es, es, ACT.Exp), te)
        for g in range(G):
            tx = act(lambda e, g=g: e.activation(P[:, g, :], src[:, g, :], ACT.Exp, bias=nm[:, g:g + 1], scale=sc,
                                                 accum_out=sm[:, g:g + 1]), t)
        ts = tx
        if sinks is not None:
            tx = dve(lambda e: e.tensor_tensor(sm, sm, es, ADD), tx, te)
        tx = dve(lambda e: e.reciprocal(sm, sm), tx)
        for g in range(G):
            tp = dve(lambda e, g=g: e.tensor_scalar(P[:, g, :], P[:, g, :], sm[:, g:g + 1], None, MUL), tx)
        return tp, (tr if bias is not None else ts)

    xh = [[f32(X0 + 4096 * h + 512 * k, 512) for k in range(8)] for h in range(2)]
    tXh = [once(sp, v3(f32(X0 + 4096 * h, 4096), 8),
                d["xT"][:, 512 * h:512 * h + 512].rearrange("(k p) n -> p k n", p=128)) for h in range(2)]
    HA = Parts(W0 + 4096, W0)
    HX = Parts(X0, X0 + 4096)
    tH0, tH1 = {}, {}
    g_mix = lambda k: col("g_mix", k)
    run(rms(xh[0], [tXh[0]] * 8, 512, g_mix, HA, tH0, HA.fhi, None))
    free0 = [(dve.sem, dve.n)]

    aqT, akT = v3(work(8192, 4096), 4), work(12288, 1024)
    avt = v3(work(13312, 1024), 8)
    mqk = [work(14336 + 1024 * m, 1024) for m in range(8)]
    mva = work(22528, 4128).rearrange("p (t h e) -> p t h e", t=8, h=4)
    mo = v3(work(26656, 4096), 4)
    pads = [work(30752, 516), work(31268, 516)]
    tail = small[:, 704:776]
    pad_free = [[], []]
    T = {}

    t_ones = pool(lambda e: e.memset(mva[:, :, :, 128:129], 1.0))

    gate8 = [work(32296, 512)[0:8, :], work(6660, 512)[0:8, :]]

    def proj_gate(half, src, tok, wait=None):
        b, free = banks1.take()
        out = bank(b)[0:8, :]
        i, whi, wlo, t = slab(w_in, 0, 8, 2816, 8)
        for k in range(8):
            hi, lo = src.hi[k], src.lo[k]
            pe(lambda e: e.matmul(out, whi[:, k, :], hi, start=(k == 0), stop=False), t, tok[k], free, inc=False)
            pe(lambda e: e.matmul(out, whi[:, k, :], lo, start=False, stop=False), inc=False)
            tk = pe(lambda e: e.matmul(out, wlo[:, k, :], hi, start=False, stop=(k == 7)), inc=(k == 7))
        slots.give(i, tk)
        T["gate", half] = dve(lambda e: e.tensor_scalar(gate8[half], out, col("bg")[0:8, :], None, ADD),
                                tk, t_col, wait)
        banks1.give(b, T["gate", half])
        yield

    def ev_av(half):
        def f(tt, ps, tk):
            q = 4 * half + tt
            T["av", q] = act(lambda e: e.activation(avt[:, q, :], ps, ACT.Copy), tk)
            return T["av", q]
        return f

    def ev_mv(half):
        def f(tt, ps, tk):
            q = 4 * half + tt
            T["mv", q] = act(lambda e: e.activation(mva[:, q, :, 0:128], ps.rearrange("p (h e) -> p h e", h=4),
                                                    ACT.Copy), tk)
            return T["mv", q]
        return f

    def ev_to(name, dst, half, func=ACT.Copy, wait=None, scale=1.0):
        def f(m, ps, tk):
            T[name, m, half] = act(lambda e: e.activation(dst[m][:, 512 * half:512 * half + 512], ps, func,
                                                          scale=scale), tk, wait)
            return T[name, m, half]
        return f

    def ev_swish(name, dst, half, wait):
        def f(m, ps, tk):
            o = dst[m][:, 512 * half:512 * half + 512]
            t = act(lambda e: e.activation(o, ps, ACT.Tanh, scale=0.5), tk, wait)
            T[name, m, half] = dve(lambda e: e.scalar_tensor_tensor(out=o, in0=o, scalar=1.0, in1=ps, op0=ADD,
                                                                    op1=MUL), t)
            return T[name, m, half]
        return f

    cnt = [0]

    def conv_evac(half, name, K, w, b, dst, tl, pf, finish, wait=None, base=0):
        K1 = K - 1

        def f(m, ps, tk):
            q = base + m
            i = cnt[0] % 2
            cnt[0] += 1
            pad, o, tq = pads[i], dst(m), tl[:, K1 * q:K1 * q + K1]
            if half:
                tz = dve(lambda e: e.tensor_copy(pad[:, 0:K1], tq), T[name + "tail", q], pf[i])
            else:
                tz = dve(lambda e: e.memset(pad[:, 0:K1], 0.0), pf[i])
            te = act(lambda e: e.activation(pad[:, K1:K1 + 512], ps, ACT.Copy), tk, pf[i])
            t = te
            if not half:
                T[name + "tail", q] = t2 = dve(lambda e: e.tensor_copy(tq, pad[:, 512:512 + K1]), te)
            t = dve(lambda e: e.tensor_scalar(o, pad[:, 0:512], w(q, 0), b(q), MUL, ADD), te, tz, t_col, wait)
            for j in range(1, K):
                t = dve(lambda e: e.scalar_tensor_tensor(out=o, in0=pad[:, j:j + 512], scalar=w(q, j), in1=o,
                                                         op0=MUL, op1=ADD), t)
            pf[i] = [t] if half else [t, t2]
            finish(m, o, t)
            return te
        return f

    def ev_mqk(half):
        def finish(m, o, t):
            tmp = work(31784, 512)
            t = act(lambda e: e.activation(tmp, o, ACT.Tanh, scale=0.5), t, T.get("tmp"))
            T["mqk", m, half] = dve(lambda e: e.scalar_tensor_tensor(out=o, in0=tmp, scalar=1.0, in1=o, op0=ADD,
                                                                     op1=MUL), t)
            T["tmp"] = T["mqk", m, half]
        return conv_evac(half, "mqk", 4, lambda q, j: col("convw", q * 4 + j), lambda q: col("convb", q),
                         lambda m: mqk[m][:, 512 * half:512 * half + 512], tail, pad_free, finish)

    w_in = d["w_in"]

    def proj_a(half, src, tok):
        yield from gemmT(w_in, 0, 4, src, tok, ev_to("aq", tiles(aqT), half))
        yield from gemmT(w_in, 512, 1, src, tok, ev_to("ak", [akT], half))
        yield from gemmN(w_in, 640, 128, src, tok, ev_av(half))

    def proj_m(half, src, tok):
        yield from proj_gate(half, src, tok, ha_free if half else None)
        yield from gemmT(w_in, 768, 8, src, tok, ev_mqk(half), cut=CUT)
        yield from gemmN(w_in, 1792, 512, src, tok, ev_mv(half))
        yield from gemmT(w_in, 2304, 4, src, tok, ev_to("mo", tiles(mo), half, ACT.Tanh, scale=0.5),
                         cut=CUT)

    together(chain(proj_a(0, HA, tH0), proj_m(0, HA, tH0)),
             rms(xh[1], [tXh[1]] * 8, 512, g_mix, HX, tH1, HX.fhi, free0), RX1)
    ha_free = [(pe.sem, pe.n)]
    run(proj_a(1, HX, tH1))

    alib = work(0, 2048)
    t_alib = once(sp, alib, d["alibi"], ha_free)
    Pb, PTb = Places([]), Places([])
    Pb.free = [(0, ha_free), (1, ha_free)]
    PTb.free = [(0, ha_free), (1, ha_free)]
    Pv = [work(2048, 1024), work(3072, 1024)]
    PTv = [work(4096, 1024), work(5120, 1024)]
    mixM = mqk[0:4]
    mix_tok = {}
    stn = [0]

    def stat():
        stn[0] = (stn[0] + 1) % 4
        return small[:, 128 + 32 * stn[0]:160 + 32 * stn[0]]

    def window(n, jp):
        W = 128 if n == 0 else 256
        k0 = 0 if n == 0 else (n - 1) * 128
        nk = W // 128
        b, free = banks2.take()
        S = pair(b).rearrange("p (g w) -> p g w", g=4)
        for a in range(2):
            for jj in range(2):
                j = 2 * jp + jj
                tS = pe(lambda e, a=a, jj=jj, j=j: e.matmul(
                    S[:, 2 * a + jj, 0:W], aqT[64 * a:64 * a + 64, j, n * 128:(n + 1) * 128],
                    akT[64 * a:64 * a + 64, k0:k0 + W], start=True, stop=True),
                    T["aq", j, n // 4], T["ak", 0, 0], T["ak", 0, n // 4], free, inc=(a == 1 and jj == 1))
        p, pfree = Pb.take()
        P = Pv[p].rearrange("p (g w) -> p g w", g=4)
        bias = alib[:, 1024 * jp:1024 * jp + 1024].rearrange("p (g w) -> p g w", g=4)[:, :, 256 - W:256]
        tP, tr = softmax(S[:, :, 0:W], tS, P[:, :, 0:W], W, 4, 0.125, bias, row("sinks", 4 * jp, 4 * jp + 4),
                         stat(), pfree, t_alib)
        banks2.give(b, tr)
        yield
        b, free = banks2.take()
        for g in range(4):
            for kt in range(nk):
                tt = transpose(pair(b)[:, (g * nk + kt) * 128:(g * nk + kt + 1) * 128],
                               P[:, g, kt * 128:(kt + 1) * 128], tP, free, t_cst,
                               inc=(g == 3 and kt == nk - 1))
        Pb.give(p, tt)
        q, qfree = PTb.take()
        PT = PTv[q]
        hw = 256 * nk
        if nk == 1:
            t1 = t2 = act(lambda e: e.activation(PT[:, 0:512], pair(b)[:, 0:512], ACT.Copy), tt, qfree)
        else:
            t1 = act(lambda e: e.activation(PT[:, 0:hw], pair(b)[:, 0:hw], ACT.Copy), tt, qfree)
            t2 = dve(lambda e: e.tensor_copy(PT[:, hw:2 * hw], pair(b)[:, hw:2 * hw]), tt, qfree)
        banks2.give(b, t1, t2)
        yield
        b, free = banks1.take()
        for a in range(2):
            for jj in range(2):
                for kt in range(nk):
                    g = 2 * a + jj
                    tile = k0 // 128 + kt
                    to = pe(lambda e, a=a, jj=jj, kt=kt, g=g, tile=tile: e.matmul(
                        bank(b)[64 * a:64 * a + 64, jj * 128:(jj + 1) * 128],
                        avt[:, tile, 64 * a:64 * a + 64],
                        PT[:, (g * nk + kt) * 128:(g * nk + kt + 1) * 128],
                        start=(kt == 0), stop=(kt == nk - 1)),
                        t1, t2, T["av", tile], free, inc=(g == 3 and kt == nk - 1))
        PTb.give(q, to)
        o = aqT[:, 2 * jp:2 * jp + 2, n * 128:(n + 1) * 128]
        t = act(lambda e: e.activation(o, bank(b)[:, 0:256].rearrange("p (j q) -> p j q", j=2), ACT.Copy), to)
        banks1.give(b, t)
        mix_tok["a", n, jp] = t

    attn = staggered([window(n, jp) for n in range(8) for jp in range(2)], DW)
    run(partly(proj_m(1, HX, tH1), attn, NW))
    gfree = [(pe.sem, pe.n)]

    R = [f32(X0 + 1024 * i, 1024)[0:4, :] for i in range(6)]
    iR, fR, bR, mR, c1, wi = R
    G = {}
    c8 = lambda v: v.rearrange("p (c t) -> p c t", c=8)

    def gates():
        tg = []
        both_ = [T["gate", 0], T["gate", 1]]
        for n in range(2):
            tg.append(act(lambda e: e.activation(iR[:, 512 * n:512 * n + 512], gate8[n][0:4, :], ACT.Copy),
                          both_, gfree))
        b, free = banks2.take()
        for n in range(2):
            t = pe(lambda e: e.matmul(pair(b)[0:4, 512 * n:512 * n + 512], I[0:8, 4:8],
                                      gate8[n], start=True, stop=True), both_, free,
                   t_cst, inc=(n == 1))
        t = dve(lambda e: e.tensor_copy(fR, pair(b)[0:4, :]), t, gfree)
        banks2.give(b, t)
        tg.append(t)
        yield
        t = act(lambda e: e.activation(c1, fR, ACT.Abs), tg)
        t = act(lambda e: e.activation(c1, c1, ACT.Exp, scale=-1.0), t)
        t = act(lambda e: e.activation(c1, c1, ACT.Ln, bias=1.0), t)
        t = dve(lambda e: e.scalar_tensor_tensor(out=fR, in0=fR, scalar=0.0, in1=c1, op0=MIN, op1=SUB), t)
        t_rs = once(sp, wi, d["reset128"], gfree)
        yield
        tb = dve(lambda e: e.tensor_tensor_scan(bR, wi, fR, 0.0, MUL, ADD), t, t_rs)
        tm = dve(lambda e: e.tensor_tensor_scan(mR, fR, iR, 0.0, ADD, MAX), tb)
        M9 = small[0:4, 256:265]
        yield
        t0 = dve(lambda e: e.memset(M9[:, 0:1], 0.0))
        t1 = dve(lambda e: e.tensor_copy(M9[:, 1:9], c8(mR)[:, :, 127]), tm, t0)
        tc1 = dve(lambda e: e.tensor_tensor(c1, iR, bR, SUB), tb, tm)
        tR1 = dve(lambda e: e.tensor_tensor(bR, bR, mR, SUB), tc1)
        yield
        t_em = act(lambda e: e.activation(fR, mR, ACT.Exp, scale=-1.0), tm)
        twi = dve(lambda e: e.tensor_tensor(c8(wi), c8(R1), M9[:, 0:8].unsqueeze(2).to_broadcast([4, 8, 128]), ADD),
                  tR1, t1)
        twi = act(lambda e: e.activation(wi, wi, ACT.Exp), twi)
        tws = dve(lambda e: e.tensor_tensor(c8(iR), c8(c1), c8(R1)[:, :, 127:128].to_broadcast([4, 8, 128]), ADD), tR1)
        tws = act(lambda e: e.activation(iR, iR, ACT.Exp), tws)
        yield
        mc_ = small[:, 288:384].rearrange("p (q t h) -> p q t h", q=3, t=8)
        b, free = banks1.take()
        for q, (src, tk) in enumerate(((c1, tc1), (iR, tws), (fR, t_em))):
            for tt in range(8):
                o = bank(b)[:, q * 32 + tt * 4:q * 32 + tt * 4 + 4]
                t = transpose(o, src[:, tt * 128:(tt + 1) * 128], tk, free, inc=(q == 2 and tt == 7))
        tmc = dve(lambda e: e.tensor_copy(small[:, 288:384], bank(b)[:, 0:96]), t)
        banks1.give(b, tmc)
        G.update(tR1=tR1, twi=twi, tmc=tmc)

    R1 = bR
    mc = small[:, 288:384].rearrange("p (q t h) -> p q t h", q=3, t=8)
    together(gates(), attn, NG)
    tR1, twi, tmc = G["tR1"], G["twi"], G["tmc"]
    att_done = [mix_tok["a", n, jp] for jp in range(2) for n in range(8)] + [(pe.sem, pe.n)]

    dec = small[:, 384:416]

    XA = [akT, work(13312, 1024)]
    XB, XC = Pv, PTv
    Cb = [v3(work(31784, 516), 4), v3(work(6144, 516), 4)]
    hbuf = [work(0, 1024), work(1024, 1024)]
    h_free = att_done
    hfree = [[], []]
    SC = 0.25 * 128.0 ** -0.5
    pe_att = (pe.sem, pe.n)
    xfree = [[pe_att], [pe_att]]

    def mlstm(h):
        u = h % 2
        E, kt, qt = XA[u], XB[u], XC[u]
        qT, kT = mqk[h], mqk[4 + h]
        hn = hbuf[u]
        wfree = [xfree[u], att_done]
        sel = cs("selh", 128 * h, 128 * h + 128)[0:4, :]
        b, free = banks2.take()
        for n in range(2):
            tk = pe(lambda e, n=n: e.matmul(pair(b)[:, 512 * n:512 * n + 512], sel, R1[:, 512 * n:512 * n + 512],
                                            start=True, stop=True), tR1, free, inc=(n == 1))
        for c in range(8):
            t = dve(lambda e, c=c: e.scalar_tensor_tensor(
                out=E[:, c * 128:(c + 1) * 128], in0=pair(b)[:, c * 128:(c + 1) * 128],
                scalar=mc[:, 0, c, h:h + 1], in1=cs("mst"), op0=ADD, op1=ADD), tk, tmc, wfree)
        banks2.give(b, t)
        tE = act(lambda e: e.activation(E, E, ACT.Exp), t)
        b, free = banks2.take()
        for n in range(2):
            tk = pe(lambda e, n=n, b=b: e.matmul(pair(b)[:, 512 * n:512 * n + 512], sel,
                                                 wi[:, 512 * n:512 * n + 512], start=True, stop=True),
                    twi, free, inc=(n == 1))
        tq = dve(lambda e, b=b: e.scalar_tensor_tensor(out=qt, in0=qT, scalar=SC, in1=pair(b), op0=MUL, op1=MUL),
                 tk, T["mqk", h, 0], T["mqk", h, 1], wfree)
        td = dve(lambda e, b=b: e.tensor_copy(dec[:, 8 * h:8 * h + 8], c8(pair(b))[:, :, 127]), tk)
        banks2.give(b, tq, td)
        yield
        b, free = banks2.take()
        for c in range(8):
            sl = slice(c * 128, (c + 1) * 128)
            tk = pe(lambda e, sl=sl, b=b: e.matmul(pair(b)[:, sl], kT[:, sl], qT[:, sl], start=True, stop=True),
                    T["mqk", h, 0], T["mqk", h, 1], T["mqk", 4 + h, 0], T["mqk", 4 + h, 1], free, inc=(c == 7))
        tsc = dve(lambda e, b=b: e.scalar_tensor_tensor(out=E, in0=pair(b), scalar=SC, in1=E, op0=MUL, op1=MUL),
                  tk, tE)
        banks2.give(b, tsc)
        b, free = banks2.take()
        for c in range(8):
            sl = slice(c * 128, (c + 1) * 128)
            tk = transpose(pair(b)[:, sl], kT[:, sl], free, inc=(c == 7))
        for c in range(8):
            sl = slice(c * 128, (c + 1) * 128)
            tkt = act(lambda e, sl=sl, c=c, b=b: e.activation(kt[:, sl], pair(b)[:, sl], ACT.Copy,
                                                              scale=mc[:, 1, c, h:h + 1]), tk, tmc, wfree)
        banks2.give(b, tkt)
        yield
        tC = None
        vt = [T["mv", tt] for tt in range(8)]
        th = []
        for c in range(8):
            sl = slice(c * 128, (c + 1) * 128)
            va = mva[:, c, h, :]
            Cold, Cnew = Cb[u][:, (c + 3) % 4, :], Cb[u][:, c % 4, :]
            b, free = banks1.take()
            num = bank(b)[:, 0:129]
            tn = pe(lambda e, num=num, sl=sl, va=va, c=c: e.matmul(num, E[:, sl], va, start=True, stop=(c == 0)),
                    tsc, vt, t_ones, free, inc=(c == 0))
            if c:
                tn = pe(lambda e, num=num, sl=sl, Cold=Cold: e.matmul(num, qt[:, sl], Cold, start=False,
                                                                      stop=True), tq, tC)
            if c < 7:
                b2, free = banks1.take()
                kv = bank(b2)[:, 0:129]
                tk = pe(lambda e, kv=kv, sl=sl, va=va: e.matmul(kv, kt[:, sl], va, start=True, stop=True),
                        tkt, free)
                if c == 0:
                    tC2 = dve(lambda e, kv=kv, Cnew=Cnew: e.tensor_copy(Cnew, kv), tk, h_free, xfree[u], t_alib)
                else:
                    tC2 = dve(lambda e, kv=kv, Cnew=Cnew, Cold=Cold, c=c: e.scalar_tensor_tensor(
                        out=Cnew, in0=Cold, scalar=dec[:, 8 * h + c:8 * h + c + 1], in1=kv, op0=MUL, op1=ADD),
                        tk, tC, td, tn)
                banks1.give(b2, tC2)
                tC = tC2
            dn = small[:, 416 + 8 * h + c:417 + 8 * h + c]
            t = act(lambda e: e.activation(dn, num[:, 128:129], ACT.Abs), tn)
            t = dve(lambda e: e.tensor_tensor(dn, dn, mc[:, 2, c, h:h + 1], MAX), t)
            t = dve(lambda e, dn=dn: e.reciprocal(dn, dn), t)
            t = dve(lambda e, num=num, dn=dn, sl=sl: e.tensor_scalar(hn[:, sl], num[:, 0:128], dn, 0.5, MUL, MUL),
                    t, h_free, hfree[u])
            banks1.give(b, t)
            th.append(t)
            yield
        b, free = banks2.take()
        for c in range(8):
            sl = slice(c * 128, (c + 1) * 128)
            tk = transpose(pair(b)[:, sl], hn[:, sl], th[c], free, inc=(c == 7))
        hfree[u] = [tk]
        xfree[u] = [tk, pe_att]
        t = dve(lambda e, b=b: e.scalar_tensor_tensor(out=mixM[h], in0=mo[:, h, :], scalar=1.0, in1=pair(b),
                                                      op0=ADD, op1=MUL), tk, T["mo", h, 0], T["mo", h, 1], h_free)
        banks2.give(b, t)
        mix_tok["m", h] = t

    modulation = ada()
    run(partly(staggered([mlstm(h) for h in range(4)], DM), modulation, NM))
    ml_done = [mix_tok["m", h] for h in range(4)] + [(pe.sem, pe.n), (dve.sem, dve.n), (act.sem, act.n)]
    tX = [once(sp, XT[:, k, :], d["xT"][k * 128:(k + 1) * 128, :], ml_done) for k in range(8)]

    def two_parts(tl, toks, half, dst, out, free):
        for k, v in enumerate(tl):
            out[k] = split(v[:, 512 * half:512 * half + 512], dst.hi[k], dst.lo[k], toks[k], free)

    mixs = tiles(aqT) + mixM
    MX = [Parts(W0 + 18432, W0 + 18432 + 4096), Parts(W0, W0 + 4096)]
    tM = [{}, {}]
    for h in range(2):
        two_parts(mixs, [ml_done] * 8, h, MX[h], tM[h], ml_done)
    parts_done = [(act.sem, act.n), (dve.sem, dve.n)]
    tX2 = [{}, {}]
    run(partly(gemmT(d["w_out"], 0, 8, MX[0], tM[0], add_x(0, tX, tX2[0])), modulation, NA))
    xs = [[XT[:, k, 512 * h:512 * h + 512] for k in range(8)] for h in range(2)]
    HB = Parts(W0 + 8192, W0 + 8192 + 4096)
    HA = Parts(W0, W0 + 4096)
    memT = [work(28672 + 256 * k, 256) for k in range(8)]
    t_mem = once(sp, v3(work(28672, 2048), 8), d["memT"].rearrange("(k p) n -> p k n", p=128), ml_done)
    HM = Parts(W0 + 30720, W0 + 28672, N=256)
    tq, tm = [{}, {}], {}
    together(partly(gemmT(d["w_out"], 0, 8, MX[1], tM[1], add_x(1, tX, tX2[1]), cut=4), modulation, NA / 2),
             chain(rms(memT, [t_mem] * 8, 256, lambda k: col("g_mem", k), HM, tm, HM.fhi, ml_done),
                   rms(xs[0], tX2[0], 512, lambda k: col("g_x", k), HB, tq[0], HB.fhi, [ml_done, parts_done])))
    qx = v3(work(16384, 8192), 8)
    kx = v3(work(24576, 2048), 8)
    vx = v3(work(26624, 2048), 2)
    Pv2 = [work(28672, 1024), work(29696, 1024)]
    PTv2 = [work(30720, 1024), work(31744, 1024)]
    wfree = [(pe.sem, pe.n)]

    def ev_vx(c):
        def f(tt, ps, tk):
            T["vx", tt, c] = act(lambda e: e.activation(vx[:, tt, 512 * c:512 * c + 512], ps, ACT.Copy), tk,
                                 wfree)
            return T["vx", tt, c]
        return f

    def ev_kx(m, ps, tk):
        T["kx", m] = act(lambda e: e.activation(kx[:, m, :], ps, ACT.Copy), tk, wfree)
        return T["kx", m]

    def kv():
        yield from gemmT(d["wkv"], 0, 8, HM, tm, ev_kx, N=256)
        for c in range(2):
            yield from gemmN(d["wkv"], 1024 + 512 * c, 512, HM, tm, ev_vx(c), T=2)
    together(kv(), rms(xs[1], tX2[1], 512, lambda k: col("g_x", k), HA, tq[1], HA.fhi, wfree))
    run(modulation)
    kvdone = [(pe.sem, pe.n)]
    run(gemmT(d["wq"], 0, 8, HB, tq[0], ev_to("qx", tiles(qx), 0, wait=wfree)))
    q0done = [(pe.sem, pe.n)]
    Pb, PTb = Places([]), Places([])
    Pb.free = [(0, kvdone), (1, kvdone)]
    PTb.free = [(0, kvdone), (1, kvdone)]
    tO = [{}, {}]
    OP = [HB, HA]
    ofree = [q0done, None]

    def cross(n):
        b, free = banks2.take()
        S = pair(b).rearrange("p (g w) -> p g w", g=4)
        for h in range(4):
            for dd in range(2):
                tS = pe(lambda e, h=h, dd=dd: e.matmul(
                    S[:, h, :], qx[:, 2 * h + dd, n * 128:(n + 1) * 128], kx[:, 2 * h + dd, :],
                    start=(dd == 0), stop=(dd == 1)), T["qx", 2 * h + dd, n // 4], T["kx", 2 * h + dd], free,
                    inc=(dd == 1))
        p, pfree = Pb.take()
        P = Pv2[p].rearrange("p (g w) -> p g w", g=4)
        tP, tr = softmax(S, tS, P, 256, 4, 1.0 / 16, None, None, stat(), pfree)
        banks2.give(b, tr)
        yield
        b, free = banks2.take()
        for g in range(4):
            for kt in range(2):
                tt = transpose(pair(b)[:, (2 * g + kt) * 128:(2 * g + kt + 1) * 128],
                               P[:, g, kt * 128:(kt + 1) * 128], tP, free, inc=(g == 3 and kt == 1))
        Pb.give(p, tt)
        q, qfree = PTb.take()
        PT = PTv2[q]
        t1 = act(lambda e: e.activation(PT[:, 0:512], pair(b)[:, 0:512], ACT.Copy), tt, qfree)
        t2 = dve(lambda e: e.tensor_copy(PT[:, 512:1024], pair(b)[:, 512:1024]), tt, qfree)
        banks2.give(b, t1, t2)
        yield
        b, free = banks2.take()
        for h in range(4):
            for dd in range(2):
                for kt in range(2):
                    m = 2 * h + dd
                    to = pe(lambda e, h=h, kt=kt, m=m, b=b: e.matmul(
                        pair(b)[:, m * 128:(m + 1) * 128], vx[:, kt, m * 128:(m + 1) * 128],
                        PT[:, (2 * h + kt) * 128:(2 * h + kt + 1) * 128], start=(kt == 0), stop=(kt == 1)),
                        t1, t2, T["vx", kt, m // 4], free, inc=(kt == 1))
        PTb.give(q, to)
        half, c0 = n // 4, 128 * (n % 4)
        ob = W0 + (8192 if half == 0 else 0)
        hi = f32r(ob, 4096).rearrange("p (k n) -> p k n", k=8)[:, :, c0:c0 + 128]
        lo = f32r(ob + 4096, 4096).rearrange("p (k n) -> p k n", k=8)[:, :, c0:c0 + 128]
        pv = pair(b).rearrange("p (m q) -> p m q", m=8)
        th = act(lambda e: e.activation(hi, pv, ACT.Copy), to, ofree[half])
        t = dve(lambda e: e.tensor_tensor(lo, pv, hi.bitcast(F32), SUB), th)
        banks2.give(b, t)
        tO[half][n] = [th, t]
    together(gemmT(d["wq"], 0, 8, HA, tq[1], ev_to("qx", tiles(qx), 1)),
             staggered([cross(n) for n in range(4)], 2), 2)
    ofree[1] = [(pe.sem, pe.n)]
    ot = [[list(tO[h].values())] * 8 for h in range(2)]
    tX3 = [{}, {}]
    together(gemmT(d["wo"], 0, 8, HB, ot[0], add_x(0, tX2[0], tX3[0])),
             staggered([cross(n) for n in range(4, 8)], 2), 2)
    o0done = [(pe.sem, pe.n)]
    ot = [[list(tO[h].values())] * 8 for h in range(2)]
    tF = [{}, {}]
    together(gemmT(d["wo"], 0, 8, HA, ot[1], add_x(1, tX2[1], tX3[1])),
             rms(xs[0], tX3[0], 512, lambda k: col("g_ffn", k), HB, tF[0], HB.fhi, o0done))
    place = lambda m: W0 + (16384 + 1024 * m if m < 16 else 1024 * (m - 16))
    pads = [work(6144, 514), work(6658, 514)]
    wfree = [(pe.sem, pe.n)]
    pf = [wfree, wfree]

    class AP:
        hi = [f32r(place(m) + 512, 512) for m in range(22)]
        lo = [f32r(place(m), 512) for m in range(22)]
    afree = [wfree, None]
    tX4 = [{}, {}]
    tY, tH2 = [{}, {}], [{}, {}]
    H2 = [HB, HA]

    def ffn(half, tA):
        def finish(m, o, t):
            tA[m] = act(lambda e: e.activation(o, o, ACT.Silu), t)

        def ev_u(m):
            def f(_, ps, tk):
                g = f32(place(m), 512)
                t = dve(lambda e: e.tensor_tensor(g, ps, g, MUL), tk, tA[m])
                tA[m] = split(g, AP.hi[m], AP.lo[m], t, afree[half])
                return t
            return f
        gate = conv_evac(half, "ffn", 3, lambda q, j: col("fw", q * 3 + j), lambda q: col("fb", q),
                         lambda i: f32(place(cur[0]), 512), small[:, 704:748], pf, lambda i, o, t:
                         finish(cur[0], o, t), wait=afree[half])
        cur = [0]

        def gate_at(m):
            def f(_, ps, tk):
                cur[0] = m
                return gate_q(m, ps, tk)
            return f

        def gate_q(m, ps, tk):
            return gate(m, ps, tk)
        for m in range(23):
            if m < 22:
                yield from gemmT(d["w_up"], m * 128, 1, HB, tF[half], gate_at(m))
            if m:
                yield from gemmT(d["w_up"], 2816 + (m - 1) * 128, 1, HB, tF[half], ev_u(m - 1))

    tA = {}
    run(ffn(0, tA))
    hb_free = [(pe.sem, pe.n)]
    together(gemmT(d["w_down"], 0, 8, AP, tA, add_x(0, tX3[0], tX4[0]), K=22),
             rms(xs[1], tX3[1], 512, lambda k: col("g_ffn", k), HB, tF[1], HB.fhi, hb_free))
    afree[1] = [(pe.sem, pe.n)]
    tA = {}
    run(ffn(1, tA))
    hb_free = [(pe.sem, pe.n)]

    def last_norms(h, free):
        yield from rms(xs[h], tX4[h], 512, lambda k: col("g_fin", k), None, tY[h], H2[h].fhi, free,
                       f32out=xs[h])
        yield from rms(xs[h], tY[h], 512, lambda k: gs2[:, k:k + 1], H2[h], tH2[h], H2[h].fhi,
                       [free, (dve.sem, dve.n)], extra=t_mod, bias=lambda k: mod[:, k:k + 1])
    together(gemmT(d["w_down"], 0, 8, AP, tA, add_x(1, tX3[1], tX4[1]), K=22, cut=8), last_norms(0, hb_free), RX2)
    done3 = [(pe.sem, pe.n)]
    W2 = d["w_in2"]
    yaT = v3(work(16384, 4096), 4)
    av = v3(work(23552, 4096), 8)
    atts = [[work(20480 + 1024 * i, 1024) for i in range(3)], [work(27648 + 1024 * i, 1024) for i in range(3)]]
    att_free = [[done3], [done3]]
    T3 = {}

    def ev_av2(half):
        def f(tt, ps, tk):
            q = 4 * half + tt
            T3["av", q] = act(lambda e: e.activation(av[:, q, :], ps, ACT.Copy), tk, done3)
            return T3["av", q]
        return f

    def proj(j, i, h):
        fr, dst, c0 = att_free[j % 2], [atts[j % 2][i]], (2176, 2688, 3712)[i] + 128 * j
        ev = ev_to(("bq", "bk")[i] + str(j), dst, h, wait=fr) if i < 2 else ev_swish(f"bg{j}", dst, h, fr)
        return gemmT(W2, c0, 1, H2[h], tH2[h], ev, cut=CUT)

    together(chain(gemmN(W2, 3200, 512, H2[0], tH2[0], ev_av2(0)), *(proj(0, i, 0) for i in range(3))),
             last_norms(1, done3), RX3)
    spilled = spill.rearrange("(k p) n -> p k n", p=128)
    t_spill = [once(sp, spilled, XT, tY[0], tY[1]), (act.sem, act.n), (dve.sem, dve.n)]
    BTs = [f32(X0, 1280), f32(X0 + 1280, 1280)]
    bmask = f32(X0 + 6656, 640)
    t_bm = once(sp, bmask, d["bmask"], t_spill)
    bt_free = [[t_spill], [t_spill]]
    Pv3 = [f32(X0 + 2560 + 640 * i, 640) for i in range(2)]
    PTv3 = [f32(X0 + 3840 + 640 * i, 640) for i in range(2)]
    Pb, PTb = Places([]), Places([])
    Pb.free = [(0, [t_spill]), (1, [t_spill])]
    PTb.free = [(0, [t_spill]), (1, [t_spill])]
    tBT = {}

    def both(f):
        for h in range(2):
            yield from f(h, H2[h], tH2[h])

    def proj_b(j):
        bt = BTs[j % 2]
        t_bt = once(sp, v3(bt, 2), v3(d["band"][:, 1280 * j:1280 * j + 1280], 2), bt_free[j % 2])
        for a in range(2):
            tBT[j] = dve(lambda e: e.tensor_tensor(bt[:, 640 * a:640 * a + 640], bt[:, 640 * a:640 * a + 640],
                                                   bmask, ADD), t_bt, t_bm)
        for i in range(2):
            for h in range(j == 0, 2):
                yield from proj(j, i, h)

    def proj_g(j):
        for h in range(j == 0, 2):
            yield from proj(j, 2, h)

    def head_scale(tl, toks, fin, sqs, sfree, rr, rrfree, scal, out, dst=None, gain=None, dfree=None):
        n = len(tl)
        b, free = banks1.take()
        sqf = [sfree] * len(sqs)
        for j in range(n):
            sq = sqs[j % len(sqs)]
            ts = act(lambda e: e.activation(sq, tl[j], ACT.Square, scale=gain(j) if gain else 1.0),
                     toks[j], t_col, sqf[j % len(sqs)])
            yield
            for tt in range(8):
                o = bank(b)[:, tt * 2 * n + 2 * j:tt * 2 * n + 2 * j + 2]
                tk = pe(lambda e: e.matmul(o, sq[:, tt * 128:(tt + 1) * 128], cs("bo"), start=True, stop=True),
                        ts, free)
            sqf[j % len(sqs)] = tk
            yield
        st = small[:, 448:448 + 16 * n]
        t, tst = fin(st, bank(b)[:, 0:16 * n], tk)
        banks1.give(b, t)
        yield
        for n0 in range(2):
            p, free = banks1.take()
            for tt in range(4):
                q = 4 * n0 + tt
                tk2 = transpose(bank(p)[0:2 * n, tt * 128:(tt + 1) * 128], st[:, q * 2 * n:(q + 1) * 2 * n],
                                tst, free, inc=(tt == 3))
            trr = dve(lambda e: e.tensor_copy(rr[n0][0:2 * n, :], bank(p)[0:2 * n, :]), tk2,
                      tk, rrfree)
            banks1.give(p, trr)
        yield
        for j in range(n):
            for n0 in range(2):
                p, free = banks1.take()
                sl = slice(512 * n0, 512 * n0 + 512)
                tk = pe(lambda e: e.matmul(bank(p), cs("selp", 128 * j, 128 * j + 128)[0:2 * n, :],
                                           rr[n0][0:2 * n, :], start=True, stop=True), trr, free)
                t = dve(lambda e: e.scalar_tensor_tensor(out=(dst or tl)[j][:, sl], in0=tl[j][:, sl],
                                                         scalar=scal(j), in1=bank(p), op0=MUL, op1=MUL),
                        tk, toks[j], t_col, dfree)
                banks1.give(p, t)
                out[j] = t
            yield

    def fin_rms(st, ps, tk):
        a = dve(lambda e: e.tensor_scalar(st, ps, 1.0 / 64, 1e-6, MUL, ADD), tk)
        t = act(lambda e: e.activation(st, st, ACT.Sqrt), a)
        return a, dve(lambda e: e.reciprocal(st, st), t)

    sqf_ = [[done3]]

    def qk_norm(j):
        nms, out = (f"bq{j}", f"bk{j}"), {}
        yield from head_scale(atts[j % 2][0:2], [[T[nm, 0, 0], T[nm, 0, 1]] for nm in nms], fin_rms,
                              [work(30720, 1024)], [sqf_[0], t_spill], [work(31744, 512), work(32256, 512)], sqf_[0],
                              lambda q: col(("qng", "kng")[q]), out)
        sqf_[0] = [(pe.sem, pe.n)]
        for q, nm in enumerate(nms):
            T3[nm] = out[q]

    ob = {}
    tya = {}

    def band(j, n, a):
        nk = min(5, n + 1)
        W = 128 * nk
        k0 = (n + 1 - nk) * 128
        h = 2 * j + a
        q_, k_, g_ = atts[j % 2]
        b, free = banks2.take()
        for c0 in range(0, W, 512):
            cn = min(512, W - c0)
            tS = pe(lambda e, c0=c0, cn=cn, b=b: e.matmul(
                pair(b)[:, c0:c0 + cn], q_[64 * a:64 * a + 64, n * 128:(n + 1) * 128],
                k_[64 * a:64 * a + 64, k0 + c0:k0 + c0 + cn], start=True, stop=True),
                T3[f"bq{j}"], T3[f"bk{j}"], free)
        p, pfree = Pb.take()
        P = Pv3[p][:, 0:W].rearrange("p (g w) -> p g w", g=1)
        S = pair(b)[:, 0:W].rearrange("p (g w) -> p g w", g=1)
        bias = v3(BTs[j % 2], 2)[:, a:a + 1, 640 - W:640]
        tP, tr = softmax(S, tS, P, W, 1, 0.125, bias, None, stat(), pfree, tBT[j])
        banks2.give(b, tr)
        yield
        b, free = banks2.take()
        for kt in range(nk):
            tt = transpose(pair(b)[:, kt * 128:(kt + 1) * 128], P[:, 0, kt * 128:(kt + 1) * 128], tP, free,
                           inc=(kt == nk - 1))
        Pb.give(p, tt)
        q, qfree = PTb.take()
        PT = PTv3[q]
        t1 = act(lambda e, b=b: e.activation(PT[:, 0:W], pair(b)[:, 0:W], ACT.Copy), tt, qfree)
        banks2.give(b, t1)
        yield
        if a == 0:
            ob[j, n] = banks1.take()
        b, free = ob[j, n]
        for kt in range(nk):
            tile = k0 // 128 + kt
            to = pe(lambda e, kt=kt, tile=tile, b=b: e.matmul(
                bank(b)[64 * a:64 * a + 64, 0:128], av[:, tile, 64 * h:64 * h + 64],
                PT[:, kt * 128:(kt + 1) * 128], start=(kt == 0), stop=(kt == nk - 1)),
                t1, T3["av", tile], free, inc=(kt == nk - 1))
        PTb.give(q, to)
        if a == 1:
            sl = slice(n * 128, (n + 1) * 128)
            t = dve(lambda e: e.scalar_tensor_tensor(out=yaT[:, j, sl], in0=bank(b)[:, 0:128], scalar=0.5,
                                                     in1=g_[:, sl], op0=MUL, op1=MUL), to,
                    T[f"bg{j}", 0, 0], T[f"bg{j}", 0, 1], done3)
            banks1.give(b, t)
            tya[j, n] = t

    def attend(j):
        yield from staggered([band(j, n, a) for n in range(8) for a in range(2)], DB)
        att_free[j % 2] = bt_free[j % 2] = [(pe.sem, pe.n), (dve.sem, dve.n), (act.sem, act.n)]

    run(gemmN(W2, 3200, 512, H2[1], tH2[1], ev_av2(1)))
    def heads(j):
        return chain(proj_b(j), weave(proj_g(j), qk_norm(j), NQ))

    run(heads(0))
    for j in range(1, 4):
        together(heads(j), attend(j - 1), NB)
    wt = lambda a: work(a, 1024)
    xt_ = lambda a: f32(X0 + a, 1024)
    rr_ = [wt(20480), wt(21504), wt(22528), xt_(6656)]
    kk_ = [wt(27648), wt(28672), wt(29696), wt(23552)]
    vv_ = [wt(24576), wt(25600), wt(26624), xt_(0)]
    gg_ = [xt_(1024), xt_(2048), xt_(3072), xt_(4096)]
    lo = wt(30720)
    lw = work(31744, 512)
    pads = [f32(X0 + 5120, 513), f32(X0 + 5633, 513)]
    last3 = attend(3)
    lofree = [(pe.sem, pe.n), (dve.sem, dve.n), (act.sem, act.n)]
    t_lw = once(sp, lw, d["lora"], lofree)
    pf = [[t_spill], [t_spill]]
    T4 = {}
    mun = small[:, 512:529]
    tmu = dve(lambda e: e.tensor_scalar(mun, cols[:, COLS["mu"][0]:COLS["mu"][0] + 17], -1.0, 1.0, MUL, ADD),
              t_col)

    def ev_shift(half, base, name, dst, wait):
        def f(m, ps, tk):
            q = base + m
            i = cnt[0] % 2
            cnt[0] += 1
            pad, o, tq = pads[i], dst[m][:, 512 * half:512 * half + 512], small[:, 704 + q:705 + q]
            if half:
                tz = dve(lambda e: e.tensor_copy(pad[:, 0:1], tq), T["shtail", q], pf[i])
            else:
                tz = dve(lambda e: e.memset(pad[:, 0:1], 0.0), pf[i])
            te = act(lambda e: e.activation(pad[:, 1:513], ps, ACT.Copy), tk, pf[i])
            if not half:
                T["shtail", q] = dve(lambda e: e.tensor_copy(tq, pad[:, 512:513]), te)
            t = dve(lambda e: e.tensor_scalar(o, pad[:, 1:513], mun[:, q:q + 1], None, MUL), te, tmu, wait)
            t = dve(lambda e: e.scalar_tensor_tensor(out=o, in0=pad[:, 0:512], scalar=col("mu", q), in1=o,
                                                     op0=MUL, op1=ADD), t, tz)
            pf[i] = t if half else [t, T["shtail", q]]
            if name == "g":
                t = act(lambda e: e.activation(o, o, ACT.Silu), t)
            T4[name, m, half] = t
            return te
        return f
    rfree = att_free[0]
    together(chain(both(lambda h, s, t: gemmT(W2, 2048, 1, s, t, ev_shift(h, 16, "lo", [lo], lofree), cut=CUT)),
                   both(lambda h, s, t: gemmT(W2, 0, 4, s, t, ev_shift(h, 0, "r", rr_, [rfree, t_bm]), cut=CUT))),
             last3, NR)
    afree = [(pe.sem, pe.n), (dve.sem, dve.n), (act.sem, act.n)]
    PK = lambda q, nm, dst, h, fr: gemmT(W2, 512 * q, 4, H2[h], tH2[h], ev_shift(h, 4 * q, nm, dst, fr),
                                         cut=4)
    run(both(lambda h, s, t: PK(1, "k", kk_, h, afree)))

    def fin_l2(st, ps, tk):
        t = act(lambda e: e.activation(st, ps, ACT.Sqrt), tk)
        t2 = dve(lambda e: e.tensor_scalar(st, st, 1e-12, None, MAX), t)
        return t, dve(lambda e: e.reciprocal(st, st), t2)

    kn, out, dfree = [work(1024 * j, 1024) for j in range(4)], {}, []
    norms = head_scale(kk_, [[T4["k", j, 0], T4["k", j, 1]] for j in range(4)], fin_l2, gg_[0:2], afree,
                       [f32(X0 + 7680, 512), work(32256, 512)], afree, lambda j: col("kk", j), out, kn,
                       lambda j: col("kk", j), dfree)
    first = (next(norms) for _ in range(10))
    together(both(lambda h, s, t: PK(2, "v", vv_, h, afree)), first)
    gfree_ = [afree, (pe.sem, pe.n)]
    run(PK(3, "g", gg_, 0, gfree_))
    hb5 = [(pe.sem, pe.n)]
    sg, aa = ([work(b0 + 1024 * j, 1024) for j in range(4)] for b0 in (8192, 12288))
    tlo = [T4["lo", 0, 0], T4["lo", 0, 1]]

    def lora():
        ttanh = act(lambda e: e.activation(lo[0:64, :], lo[0:64, :], ACT.Tanh), tlo)
        for q, (dst, bias) in enumerate(((sg, "w0"), (aa, "a0"))):
            for j in range(4):
                b, free = banks2.take()
                for n in range(2):
                    tk = pe(lambda e: e.matmul(
                        pair(b)[:, 512 * n:512 * n + 512], lw[64 * q:64 * q + 64, 128 * j:128 * j + 128],
                        lo[64 * q:64 * q + 64, 512 * n:512 * n + 512], start=True, stop=True),
                        t_lw, ttanh, tlo, free, inc=(n == 1))
                T4[bias, j] = act(lambda e: e.activation(dst[j], pair(b), ACT.Sigmoid, bias=col(bias, j)),
                                  tk, hb5)
                banks2.give(b, T4[bias, j])
                yield
    together(PK(3, "g", gg_, 1, gfree_), lora(), 1)
    hfree5 = [(pe.sem, pe.n)]
    dfree.extend(hfree5)
    for m in range(4):
        for nm in "rkvg":
            T4[nm, m] = [T4[nm, m, 0], T4[nm, m, 1]]
    sl_ids = lend_ring()
    sf = [x[1] for x in sl_ids]
    i0 = [x[0] for x in sl_ids]
    rs64 = f32(G0, 1024)
    t_rs64 = once(sp, rs64, d["reset64"], sf)
    PLc = v3(small[:, 544:608], 4)
    run(norms)
    bon = v3(small[:, 608:672], 8)
    prepd, tbon = {}, {}
    m2 = f32(X0 + 5120, 1280)
    shifted = [(dve.sem, dve.n), (act.sem, act.n), (pe.sem, pe.n)]
    t_m2 = once(sp, m2, d["m2"], shifted)

    def prepare(half, free_banks):
        b, freeb = free_banks.take()
        hs = slice(512 * half, 512 * half + 512)
        done = {}

        def front(j):
            A, B, C, D = (work(4096 + 1024 * i + 512 * (j % 2), 512) for i in range(4))
            pt = done.get(j - 2)
            t1 = dve(lambda e: e.tensor_scalar(A, aa[j][:, hs], 1.0, col("ka", j), SUB, MUL), T4["a0", j],
                     hfree5, pt)
            t1 = dve(lambda e: e.scalar_tensor_tensor(out=kk_[j][:, hs], in0=A, scalar=1.0,
                                                      in1=kk_[j][:, hs], op0=ADD, op1=MUL), t1, out[j])
            t4 = dve(lambda e: e.tensor_tensor_scan(B, rs64[:, hs], sg[j][:, hs], 0.0, MUL, ADD),
                     T4["w0", j], t_rs64, pt)
            t6 = act(lambda e: e.activation(C, B, ACT.Exp, scale=EH), t4, pt)
            t5 = dve(lambda e: e.tensor_tensor(A, B, sg[j][:, hs], SUB), t4, t1)
            t7 = act(lambda e: e.activation(B, B, ACT.Exp, scale=-EH), t4, t5)
            t8 = act(lambda e: e.activation(A, A, ACT.Exp, scale=-EH), t5)
            t2 = pool(lambda e: e.tensor_tensor(aa[j][:, hs], aa[j][:, hs], kn[j][:, hs], MUL), out[j], t1)
            t3 = dve(lambda e: e.scalar_tensor_tensor(out=D, in0=rr_[j][:, hs], scalar=col("rk", j),
                                                      in1=kk_[j][:, hs], op0=MUL, op1=MUL), t1, T4["r", j],
                     pt, t_col)
            for tt in range(4):
                o = bank(b)[:, tt * 8 + 2 * j:tt * 8 + 2 * j + 2]
                tbo = pe(lambda e: e.matmul(o, D[:, tt * 128:(tt + 1) * 128], cs("bo"), start=True,
                                            stop=True), t3, freeb)
            return A, B, C, t2, t3, t5, t6, t7, t8, tbo

        def back(j, A, B, C, t2, t3, t5, t6, t7, t8, tbo):
            ta = pool(lambda e: e.tensor_tensor(aa[j][:, hs], aa[j][:, hs], C, MUL), t6, t2)
            tb_ = dve(lambda e: e.tensor_tensor(kk_[j][:, hs], kk_[j][:, hs], C, MUL), t6, t3)
            tc = pool(lambda e: e.tensor_tensor(rr_[j][:, hs], rr_[j][:, hs], B, MUL), t7, t3)
            td = dve(lambda e: e.tensor_copy(PLc[:, j, 8 * half:8 * half + 8],
                                             B.rearrange("p (c t) -> p c t", c=8)[:, :, 63]), t7)
            t9 = dve(lambda e: e.scalar_tensor_tensor(out=sg[j][:, hs], in0=kn[j][:, hs], scalar=-1.0, in1=A,
                                                      op0=MUL, op1=MUL), t8, t5)
            done[j] = [t9, ta, tb_, tc, td, tbo]

        before = None
        for j in range(4):
            f = front(j)
            if before:
                back(j - 1, *before)
            before = f
            yield
        back(3, *before)
        tbo = before[-1]
        prepd[half] = [done[j] for j in range(4)]
        tbon[half] = dve(lambda e: e.tensor_copy(small[:, 608 + 32 * half:640 + 32 * half],
                                                 bank(b)[:, 0:32]), tbo)
        free_banks.give(b, tbon[half])
    run(prepare(0, banks1))
    At, Bh, Kh, Rt = sg, aa, kk_, rr_

    mAR = m2[:, 0:256].rearrange("p (q t) -> p q t", q=2)
    mL, m0, m0T = m2[:, 256:384], m2[:, 384:512], m2[:, 512:640]
    lv = [m2[:, 640 + 128 * l:768 + 128 * l] for l in range(5)]
    spare = [f32(G0 + 1024, 7168), work(30720, WN - 30720), work(0, 8192)]
    used = [0, 0, 0]

    def place(n, late=False):
        for i in ((2,) if late else (0, 1)):
            if used[i] + n <= spare[i].shape[1]:
                used[i] += n
                return spare[i][:, used[i] - n:used[i]]
        assert False
    sizes = dict(TT=1024, RB=1024, NV=512, RKV=512, vt=512, kt=512, bt=512)
    gMT, gM, gT, gX = place(1024), place(1024), place(1024), place(1024)
    gN, gRK = gT, gX
    per = [{n: place(w, late) for n, w in sizes.items()} for late in (False, True)]
    Zb = v3(place(512, True), 4)
    Xs, Us, Zt = place(512, True), place(512, True), place(512, True)
    ych = [place(512, True), place(512, True)]
    allf0 = [prepd[0], sf, shifted]
    allf = [allf0]
    state = {"gfree": allf0, "xs": allf, "us": allf, "Z": []}
    pfree_ = [allf0, allf]
    yfree = [allf, allf]
    h8 = lambda v: v.rearrange("p (h t) -> p h t", h=8)
    yr = Rt
    tyr = {}

    def bc(m, n=8):
        return m.unsqueeze(1).to_broadcast([128, n, 128])

    banks = Places([])
    for _ in range(2):
        i, free = banks2.take()
        banks.give(2 * i, free)
        banks.give(2 * i + 1, free)
    for _ in range(4):
        i, free = banks1.take()
        banks.give(i, free)
    h4 = lambda v: v.rearrange("p (h t) -> p h t", h=4)

    def pre(cp):
        r = per[cp % 2]
        sl = slice(128 * cp, 128 * cp + 128)
        fr = [pfree_[cp % 2]]
        gf = state["gfree"]
        TT, RB = h8(r["TT"]), h8(r["RB"])
        MT, M, Tm, X, N = h8(gMT), h8(gM), h8(gT), h8(gX), h8(gN)
        RK = h8(gRK)
        tks = []
        for src, dst in ((vv_, "vt"), (Kh, "kt"), (Bh, "bt")):
            b, free = banks.take()
            for j in range(4):
                tk = transpose(bank(b)[:, 128 * j:128 * j + 128], src[j][:, sl], free, prepd[cp // 4],
                               T4["v", j], inc=(j == 3))
            t = act(lambda e, b=b, dst=dst: e.activation(r[dst], bank(b), ACT.Copy), tk, fr)
            banks.give(b, t)
            tks.append(t)
        hv = lambda v, a: v[:, 4 * a:4 * a + 4, :]
        tMT, tRB, tN, tRK, tM = {}, {}, {}, {}, {}
        for lhs, outs in ((Bh, ((MT, At, mAR[:, 0, :], tMT), (RB, Rt, mAR[:, 1, :], tRB))),
                          (At, ((M, Bh, m0, tM),)),
                          (Kh, ((N, At, mAR[:, 0, :], tN), (RK, Rt, mAR[:, 1, :], tRK)))):
            for dst, rhs, mask, tok in outs:
                for a in range(2):
                    b, free = banks.take()
                    for j in range(4):
                        tk = pe(lambda e: e.matmul(
                            bank(b)[:, 128 * j:128 * j + 128], lhs[j][64 * a:64 * a + 64, sl],
                            rhs[j][64 * a:64 * a + 64, sl], start=True, stop=True), free, prepd[cp // 4],
                            inc=(j == 3))
                    tok[a] = dve(lambda e: e.tensor_tensor(hv(dst, a), h4(bank(b)), bc(mask, 4), MUL),
                                 tk, t_m2, fr, gf)
                    banks.give(b, tok[a])
            yield
        tT, tTT, tX_ = {}, {}, {}
        for a in range(2):
            tTT[a] = dve(lambda e: e.tensor_tensor(hv(TT, a), hv(MT, a), bc(m0T, 4), MUL), tMT[a], fr)
            tTT[a] = dve(lambda e: e.tensor_tensor(hv(TT, a), hv(TT, a), bc(I, 4), ADD), tTT[a])
        for src, tsrc, dst in ((N, tN, "NV"), (RK, tRK, "RKV")):
            b, free = banks.take()
            for g in range(8):
                hh = 2 * (g % 4) + g // 4
                tk = pe(lambda e: e.matmul(
                    bank(b)[:, 64 * g:64 * g + 64], src[:, g, :], r["vt"][:, 64 * hh:64 * hh + 64],
                    start=True, stop=True), tsrc, tks[0], free, inc=(g == 7))
            t = act(lambda e: e.activation(r[dst], bank(b), ACT.Copy), tk, fr)
            banks.give(b, t)
            r["t" + dst] = t
        tX_ = {0: tk, 1: tk}
        for a in range(2):
            tT[a] = dve(lambda e: e.tensor_tensor(hv(Tm, a), hv(M, a), bc(I, 4), ADD), tM[a], tk)
        for l in range(5):
            tXX = {}
            for a in range(2):
                b, free = banks.take()
                for g in range(4 * a, 4 * a + 4):
                    tk = pe(lambda e: e.matmul(bank(b)[:, 128 * (g % 4):128 * (g % 4) + 128], MT[:, g, :],
                                               Tm[:, g, :], start=True, stop=True), tMT[a], tT[a], free,
                            inc=(g % 4 == 3))
                tXX[a] = dve(lambda e: e.tensor_tensor(hv(X, a), h4(bank(b)), bc(lv[l], 4), MUL), tk,
                             tX_[a])
                banks.give(b, tXX[a])
            yield
            for a in range(2):
                b, free = banks.take()
                for g in range(4 * a, 4 * a + 4):
                    tk = pe(lambda e: e.matmul(bank(b)[:, 128 * (g % 4):128 * (g % 4) + 128], X[:, g, :],
                                               TT[:, g, :], start=True, stop=True), tXX[a], tTT[a], free,
                            inc=(g % 4 == 3))
                tX_[a] = tk
                tTT[a] = dve(lambda e: e.tensor_tensor(hv(TT, a), h4(bank(b)), hv(TT, a), ADD), tk, tTT[a])
                banks.give(b, tTT[a])
            if l < 4:
                yield
                for a in range(2):
                    b, free = banks.take()
                    for g in range(4 * a, 4 * a + 4):
                        tk = transpose(bank(b)[:, 128 * (g % 4):128 * (g % 4) + 128], TT[:, g, :], tTT[a],
                                       free, inc=(g % 4 == 3))
                    tT[a] = act(lambda e: e.activation(hv(Tm, a), h4(bank(b)), ACT.Copy), tk, tT[a])
                    banks.give(b, tT[a])
            yield
        r["tTT"], r["tRB"], r["tks"] = tTT, tRB, tks
        state["gfree"] = [tk, tTT]

    def seq(cp):
        r = per[cp % 2]
        sl = slice(128 * cp, 128 * cp + 128)
        TT, RB = h8(r["TT"]), h8(r["RB"])
        y = ych[cp % 2]
        yb, yfr = banks.take()
        for par in range(2):
            c = 2 * cp + par
            cols_ = slice(64 * c, 64 * c + 64)
            ps_ = slice(64 * par, 64 * par + 64)
            b, free = banks.take()
            for j in range(4):
                o = bank(b)[ps_, :].rearrange("p (a j i) -> p a j i", a=2, j=4)[:, :, j, :]
                tk = pe(lambda e, j=j, o=o, cols_=cols_: e.matmul(o, At[j][:, cols_], Zb[:, j, :], start=True,
                                                                  stop=True), state["Z"], free, prepd[cp // 4],
                        inc=(j == 3))
            tx = dve(lambda e, b=b, ps_=ps_: e.tensor_tensor(Xs[ps_, :], bank(b)[ps_, :], r["NV"][ps_, :],
                                                             ADD), tk, r["tNV"], state["xs"])
            banks.give(b, tx)
            yield
            b, free = banks.take()
            for g in range(8):
                tk = pe(lambda e, g=g, b=b, ps_=ps_: e.matmul(
                    bank(b)[ps_, 64 * g:64 * g + 64], TT[ps_, g, ps_], Xs[ps_, 64 * g:64 * g + 64],
                    start=True, stop=True), tx, r["tTT"], free, inc=(g == 7))
            state["xs"] = tk
            tu = act(lambda e, b=b, ps_=ps_: e.activation(Us[ps_, :], bank(b)[ps_, :], ACT.Copy), tk,
                     state["us"])
            banks.give(b, tu)
            yield
            b, free = banks.take()
            for g in range(8):
                a, j = g // 4, g % 4
                hh = 2 * j + a
                o = bank(b)[64 * a:64 * a + 64, 64 * j:64 * j + 64]
                pe(lambda e, o=o, hh=hh, g=g, ps_=ps_: e.matmul(
                    o, r["bt"][ps_, 64 * hh:64 * hh + 64], Us[ps_, 64 * g:64 * g + 64], start=True,
                    stop=False), tu, r["tks"], free, inc=False)
                tk = pe(lambda e, o=o, hh=hh, ps_=ps_: e.matmul(
                    o, r["kt"][ps_, 64 * hh:64 * hh + 64], r["vt"][ps_, 64 * hh:64 * hh + 64],
                    start=False, stop=True), inc=(g == 7))
            ty = None
            for j in range(4):
                o = bank(yb)[ps_, :].rearrange("p (a j i) -> p a j i", a=2, j=4)[:, :, j, :]
                pe(lambda e, j=j, o=o, cols_=cols_: e.matmul(o, Rt[j][:, cols_], Zb[:, j, :], start=True,
                                                             stop=False, skip_group_check=True),
                   yfr, inc=False)
                for a in range(2):
                    g = 4 * a + j
                    ty = pe(lambda e, g=g, ps_=ps_: e.matmul(
                        bank(yb)[ps_, 64 * g:64 * g + 64], RB[ps_, g, ps_], Us[ps_, 64 * g:64 * g + 64],
                        start=False, stop=True, skip_group_check=True), r["tRB"], inc=(j == 3 and a == 1))
            state["us"] = ty
            tz_ = None
            for a in range(2):
                as_ = slice(64 * a, 64 * a + 64)
                zv = Zb[as_, :, 64 * a:64 * a + 64]
                pv = bank(b)[as_, 0:256].rearrange("p (j i) -> p j i", j=4)
                t1 = dve(lambda e, zv=zv, pv=pv: e.tensor_tensor(zv, pv, zv, ADD), tk, ty, state["Z"])
                tz_ = dve(lambda e, zv=zv, as_=as_, c=c: e.tensor_tensor(
                    zv, zv, PLc[as_, :, c:c + 1].to_broadcast([64, 4, 64]), MUL), t1)
            banks.give(b, tz_)
            state["Z"] = tz_
            yield
        yf = yfree[cp % 2]
        nat = lambda v: v.rearrange("p (j a i) -> p a j i", j=4, a=2)
        byp = lambda v: v.rearrange("p (a j i) -> p a j i", j=4, a=2)
        ty2 = dve(lambda e: e.tensor_tensor(nat(y), byp(bank(yb)), byp(r["RKV"]), ADD), ty, r["tRKV"], yf)
        banks.give(yb, ty2)
        yv = y.rearrange("p (g i) -> p g i", g=8)
        st = small[:, 672 + 16 * (cp % 2):688 + 16 * (cp % 2)]
        q2 = Zt
        b8 = lambda v: v.unsqueeze(2).to_broadcast([128, 8, 64])
        t = dve(lambda e: e.tensor_reduce(st[:, 0:8], yv, AX.X, ADD), ty2)
        t = dve(lambda e: e.tensor_scalar(st[:, 0:8], st[:, 0:8], 1.0 / 64, None, MUL), t)
        t = dve(lambda e: e.tensor_tensor(yv, yv, b8(st[:, 0:8]), SUB), t)
        yield
        ta = act(lambda e: e.activation(q2, y, ACT.Square), t, state.get("q2"))
        t = dve(lambda e: e.tensor_reduce(st[:, 8:16], q2.rearrange("p (g i) -> p g i", g=8), AX.X, ADD), ta)
        state["q2"] = t
        t = dve(lambda e: e.tensor_scalar(st[:, 8:16], st[:, 8:16], 1.0 / 64, 64e-5, MUL, ADD), t)
        t = act(lambda e: e.activation(st[:, 8:16], st[:, 8:16], ACT.Sqrt), t)
        t = dve(lambda e: e.reciprocal(st[:, 8:16], st[:, 8:16]), t)
        t = dve(lambda e: e.tensor_tensor(yv, yv, b8(st[:, 8:16]), MUL), t)
        yield
        t = pool(lambda e: e.tensor_tensor(y, y, row("lng"), MUL), t)
        t = pool(lambda e: e.tensor_tensor(y, y, row("lnb"), ADD), t)
        t = pool(lambda e: e.tensor_tensor(q2.rearrange("p (g i) -> p g i", g=8),
                                          r["vt"].rearrange("p (g i) -> p g i", g=8), b8(bon[:, cp, :]), MUL),
                t, tbon[cp // 4])
        t = pool(lambda e: e.tensor_tensor(y, y, q2, ADD), t)
        state["q2"] = t
        yield
        b, free = banks.take()
        for j in range(4):
            tk = transpose(bank(b)[:, 128 * j:128 * j + 128], y[:, 128 * j:128 * j + 128], t, free,
                           inc=(j == 3))
        yfree[cp % 2] = tk
        for j in range(4):
            t = dve(lambda e: e.tensor_tensor(yr[j][:, sl], bank(b)[:, 128 * j:128 * j + 128],
                                              gg_[j][:, sl], MUL), tk, T4["g", j], ty)
        banks.give(b, t)
        tyr[cp] = t
        pfree_[cp % 2] = [t, tk, ty]
        yield

    together(pre(0), prepare(1, banks), NP)
    allf.append([prepd[1], (pe.sem, pe.n)])
    state["Z"] = dve(lambda e: e.memset(Zb, 0.0), allf)
    now = lambda: [(pe.sem, pe.n), (act.sem, act.n), (dve.sem, dve.n)]
    src = yr + tiles(yaT)
    class Half:
        hi = [f32r(W0 + 8192 + 1024 * k, 512) for k in range(8)]
        lo = [f32r(a_, 512) for a_ in (W0 + 27648, W0 + 28672, W0 + 29696, W0 + 23552,
                                       W0 + 24576, W0 + 25600, W0 + 26624, W0 + 30720)]
    OP = [Half, Parts(W0, W0 + 4096)]
    tO, tXr = [{}, {}], [{}, {}]
    back = [[XT[:, k, 512 * (h ^ (k == 7)):512 * (h ^ (k == 7)) + 512] for k in range(8)] for h in range(2)]

    def reload(h, toks):
        for k in range(8):
            tXr[h][k] = once(sp, back[h][k], spilled[:, k, 512 * h:512 * h + 512], toks, t_spill)

    def ev_out(half):
        def f(m, ps, tk):
            o = back[half][m]
            t = dve(lambda e: e.scalar_tensor_tensor(out=o, in0=ps, scalar=mod[:, 16 + m:17 + m], in1=o,
                                                     op0=MUL, op1=ADD), tk, tXr[half][m], t_mod)
            finals.append(once(act, d["out"][m * 128:(m + 1) * 128, 512 * half:512 * half + 512], o, t))
            return t
        return f

    def part(h, k, toks):
        return split(src[k][:, 512 * h:512 * h + 512], OP[h].hi[k], OP[h].lo[k], toks)
    for cp in range(7):
        together(pre(cp + 1), seq(cp), NS)
        if cp == 3:
            mid = now()
        if cp >= 4:
            for k in range(3 * cp - 12, min(3 * cp - 9, 7)):
                tO[0][k] = part(0, k, mid)
    mid7 = now()
    tO[0][7] = part(0, 7, mid7)
    for i in i0:
        slots.give(i, mid7)
    reload(0, [mid7, tO[0]])
    for _ in range(2):
        i, free = banks.take()
        banks1.give(i, free)
    last = seq(7)
    for _ in range(3):
        next(last)
    together(gemmT(d["w_out2"], 0, 8, OP[0], tO[0], ev_out(0), cut=2), last, N7)
    fin = now()
    two_parts(src, [fin] * 8, 1, OP[1], tO[1], fin)
    reload(1, [fin, tO[1]])
    run(gemmT(d["w_out2"], 0, 8, OP[1], tO[1], ev_out(1)))
    sp(lambda e: e.nop(), finals, inc=False)


def host_layout(inputs):
    import numpy as np
    f = {k: np.asarray(v) for k, v in inputs.items()}

    def colv(v, k):
        return v.reshape(k, 128).T
    s = np.zeros((128, NCOLS), np.float32)

    def put(name, m):
        o, w = COLS[name]
        s[:, o:o + w] = m
    for name, key in (("g_mix", "norm_mix_g"), ("g_x", "norm_xattn_g"), ("g_mem", "norm_mem_g"),
                      ("g_ffn", "norm_ffn_g"), ("g_fin", "norm_final_g"), ("g_n2", "norm_g_2"), ("c", "c_2")):
        put(name, colv(f[key], 8))
    put("b_ada", colv(f["b_ada_2"], 24))
    put("convw", f["conv_qk_w"][0].reshape(4, 8, 128).transpose(2, 1, 0).reshape(128, 32))
    put("convb", colv(f["conv_qk_b"], 8))
    put("fw", f["conv_ffn_w"][0].reshape(3, 22, 128).transpose(2, 1, 0).reshape(128, 66))
    put("fb", colv(f["conv_ffn_b"], 22))
    put("mu", colv(f["mu_shift_2"], 17))
    for name, key in (("w0", "w0_2"), ("a0", "a0_2"), ("kk", "k_k_2"), ("ka", "k_a_2"), ("rk", "r_k_2")):
        put(name, colv(f[key], 4))
    for name, key in (("qng", "q_norm_g_2"), ("kng", "k_norm_g_2")):
        put(name, np.concatenate([f[key][0], f[key][0]])[:, None])
    put("bg", np.concatenate([f["b_gate_if"][0], np.zeros(120, np.float32)])[:, None])
    order = [4 * a + j for j in range(4) for a in range(2)]
    sk = f["attn_sinks"][0]
    sinks = np.concatenate([sk[[2 * jp, 2 * jp + 1, 4 + 2 * jp, 5 + 2 * jp]] for jp in range(2)])
    lng = f["lnx_g_2"][0]
    lnb = f["lnx_b_2"][0]
    rows = np.concatenate([sinks, lng, lnb])
    rows = np.ascontiguousarray(np.broadcast_to(rows, (128, NROWS)))
    cst = np.zeros((128, NCST), np.float32)

    def putc(name, m):
        o, w = CST[name]
        cst[:m.shape[0], o:o + w] = m
    p = np.arange(128)
    putc("I", np.eye(128))
    putc("ones", np.ones((128, 128)))
    putc("bo", (p[:, None] // 64 == np.arange(2)[None]) * 1.0)
    putc("mst", np.where(p[:, None] <= p[None], 0.0, -1e30))
    putc("selh", (np.arange(4)[:, None] == (np.arange(512) // 128)[None]) * 1.0)
    q = np.arange(512)
    putc("selp", (np.arange(8)[:, None] == (2 * (q // 128) + (q % 128) // 64)[None]) * 1.0)
    slopes = 2.0 ** (-np.arange(1, 9, dtype=np.float32))
    dist = p[:, None] + 128 - np.arange(256)[None]
    ok = (dist >= 0) & (dist < 128)
    alibi = np.concatenate([np.where(ok, -slopes[h] * dist, -1e30) for jp in range(2)
                            for h in (2 * jp, 2 * jp + 1, 4 + 2 * jp, 5 + 2 * jp)], axis=1).astype(np.float32)
    r128 = np.ones((4, 1024), np.float32)
    r128[:, ::128] = 0
    r64 = np.ones((128, 1024), np.float32)
    r64[:, ::64] = 0
    same = p[:, None] // 64 == p[None] // 64
    strict = same & (p[:, None] < p[None])
    incl = same & (p[:, None] <= p[None])
    low = same & (p[:, None] > p[None])
    ms = [strict, incl, low]

    def level(l):
        n = 1 << l
        t, u = p[:, None], p[None]
        return (t // (2 * n) == u // (2 * n)) & (t // n % 2 == 1) & (u // n % 2 == 0)
    ms += [level(0), level(0).T] + [level(l) for l in range(1, 6)]
    m2 = np.concatenate([m.astype(np.float32) for m in ms], axis=1)
    rb = f["rel_bias_2"][0]
    kq = np.arange(640)
    dd = p[:, None] + 512 - kq[None]
    idx = np.clip(np.clip(dd, -63, 128) + 63, 0, 191)
    band = np.ascontiguousarray(rb[:, idx].transpose(1, 0, 2).reshape(128, 8 * 640))
    hi = (p[:, None] >= 64)
    bad = (hi & (kq[None] < 64)) | (~hi & (kq[None] >= 576))
    bmask = np.where(bad, -1e30, 0.0).astype(np.float32)
    perm = np.concatenate([np.arange(64) + 64 * h for h in [4 * a + j for j in range(4) for a in range(2)]])
    w_in = f["w_in"][0].copy()
    w_in[:, :512] = f["w_in"][0][:, perm]
    w_out = f["w_out"][0].copy()
    w_out[:512] = f["w_out"][0][perm]
    return {
        "xT": f["x"][0].T, "memT": f["mem"][0].T, "cols": s, "rows": rows, "cst": cst, "alibi": alibi,
        "reset128": r128, "reset64": r64, "m2": m2, "band": band, "bmask": bmask,
        "w_in": w_in, "w_out": w_out, "wq": f["wq_x"][0], "wkv": f["wkv_x"][0], "wo": f["wo_x"][0],
        "w_up": f["w_up"][0], "w_down": f["w_down"][0], "w_ada": f["w_ada_2"][0], "w_in2": f["w_in_2"][0],
        "w_out2": f["w_out_2"][0], "lora": np.concatenate([f["w2_2"][0], f["a2_2"][0]], axis=0),
    }


def kernel(**inputs):
    import numpy as _np
    import concourse.bacc as _bacc
    from concourse import mybir as _mybir
    from concourse.bass_utils import run_bass_kernel_spmd as _run

    nc = _bacc.Bacc("TRN2", target_bir_lowering=False, num_devices=1)
    arrays, d = {}, {}
    for name, a in host_layout(inputs).items():
        a = _np.ascontiguousarray(a)
        arrays[f"in_{name}"] = a
        d[name] = nc.dram_tensor(f"in_{name}", a.shape, _mybir.dt.from_np(a.dtype), kind="ExternalInput").ap()
    d["out"] = nc.dram_tensor("out", (1024, 1024), F32, kind="ExternalOutput").ap()
    build(nc, d)
    r = _run(nc, [arrays], core_ids=[0])
    return _np.ascontiguousarray(r.results[0]["out"].T)[None]
```
